# Optimizing a Trainium2 kernel written in Bass

```python
import jax, jax.numpy as jnp
from jax import lax
import numpy as np

D_MODEL = 1024
BATCH = 1
SEQ = 256
DEPTH = 1

HEAD_DIM = 64
SB_HEADS = 4
DSA_HEADS = 4
NSA_HEADS = 4
BRANCH_WIDTH = 4 * HEAD_DIM
IDX_HEADS = 4
IDX_DIM = 64
DSA_TOPK = 256
CMP_LEN = 32
CMP_STRIDE = 16
CMP_HIDDEN = 128
SEL_LEN = 64
SEL_TOPN = 16
WINDOW = 512
N_MEM = 256
MEM_HEADS = 4
MEM_HEAD_DIM = 64
D_FF = ((8 * D_MODEL + 3 * 256 - 1) // (3 * 256)) * 256
Q_BLOCK = 128
ROPE_THETA = 10000.0
RMS_EPS = 1e-6
FORCED_SCORE = 1e4

IN_SPLITS = (
    ('q_a', SB_HEADS * HEAD_DIM), ('k_a', SB_HEADS * HEAD_DIM), ('v_a', SB_HEADS * HEAD_DIM),
    ('q_b', DSA_HEADS * HEAD_DIM), ('k_b', HEAD_DIM), ('v_b', HEAD_DIM),
    ('q_idx', IDX_HEADS * IDX_DIM), ('k_idx', IDX_DIM), ('w_idx', IDX_HEADS),
    ('q_c', NSA_HEADS * HEAD_DIM), ('k_cmp', HEAD_DIM), ('v_cmp', HEAD_DIM),
    ('k_sel', HEAD_DIM), ('v_sel', HEAD_DIM), ('k_win', HEAD_DIM), ('v_win', HEAD_DIM),
    ('g_c', NSA_HEADS * 3),
    ('g_merge', 3 * D_MODEL),
)
D_IN = sum(w for _, w in IN_SPLITS)


def _rmsnorm(x, g):
    xf = x.astype(jnp.float32)
    y = xf * lax.rsqrt(jnp.mean(xf * xf, axis=-1, keepdims=True) + RMS_EPS)
    return (y * g.astype(jnp.float32)).astype(x.dtype)

def _rope(x):
    S, hd = x.shape[1], x.shape[-1]
    inv = ROPE_THETA ** (-jnp.arange(0, hd, 2, dtype=jnp.float32) / hd)
    ang = jnp.arange(S, dtype=jnp.float32)[:, None] * inv[None, :]
    cos = jnp.cos(ang)[None, :, None, :]
    sin = jnp.sin(ang)[None, :, None, :]
    xf = x.astype(jnp.float32)
    x1, x2 = xf[..., : hd // 2], xf[..., hd // 2:]
    return jnp.concatenate([x1 * cos - x2 * sin, x2 * cos + x1 * sin], axis=-1).astype(x.dtype)

def _masked_softmax(s, mask):
    s = jnp.where(mask, s.astype(jnp.float32), -jnp.inf)
    m = jnp.max(s, axis=-1, keepdims=True)
    m = jnp.where(jnp.isfinite(m), m, 0.0)
    e = jnp.where(mask, jnp.exp(s - m), 0.0)
    den = jnp.sum(e, axis=-1, keepdims=True)
    return e / jnp.maximum(den, 1e-30)

def _sweep(block_fn, S):
    out = lax.map(block_fn, jnp.arange(S // Q_BLOCK))
    out = jnp.moveaxis(out, 0, 1)
    return out.reshape((out.shape[0], S) + out.shape[3:])

def _split_columns(p):
    parts, off = {}, 0
    for name, w in IN_SPLITS:
        parts[name] = p[..., off:off + w]
        off += w
    return parts

def _stick_breaking(q, k, v):
    B, S, H, hd = q.shape
    scale = hd ** -0.5
    kpos = jnp.arange(S)

    def block(i):
        q0 = i * Q_BLOCK
        qpos = q0 + jnp.arange(Q_BLOCK)
        qb = lax.dynamic_slice_in_dim(q, q0, Q_BLOCK, axis=1)
        z = jnp.einsum('bqhd,bkhd->bhqk', qb, k).astype(jnp.float32) * scale
        strict = kpos[None, :] < qpos[:, None]
        log_1m = jnp.where(strict, jax.nn.log_sigmoid(-z), 0.0)
        suffix = lax.cumsum(log_1m, axis=3, reverse=True) - log_1m
        w = jnp.where(strict, jnp.exp(jax.nn.log_sigmoid(z) + suffix), 0.0)
        return jnp.einsum('bhqk,bkhd->bqhd', w.astype(v.dtype), v)

    return _sweep(block, S)

def _dsa_attention(q, k, v, q_idx, k_idx, w_idx):
    B, S, H, hd = q.shape
    topk = min(DSA_TOPK, S // 4)
    kpos = jnp.arange(S)
    bidx = jnp.arange(B)[:, None, None]
    w_scale = (IDX_HEADS * IDX_DIM) ** -0.5
    scale = hd ** -0.5

    def block(i):
        q0 = i * Q_BLOCK
        qpos = q0 + jnp.arange(Q_BLOCK)
        qi = lax.dynamic_slice_in_dim(q_idx, q0, Q_BLOCK, axis=1)
        wi = lax.dynamic_slice_in_dim(w_idx, q0, Q_BLOCK, axis=1).astype(jnp.float32) * w_scale
        rel = jax.nn.relu(jnp.einsum('bqhd,bkd->bqhk', qi, k_idx).astype(jnp.float32))
        score = jnp.einsum('bqh,bqhk->bqk', wi, rel)
        score = jnp.where(kpos[None, None, :] <= qpos[None, :, None], score, -jnp.inf)
        _, sel = lax.top_k(score, topk)
        kg = k[bidx, sel]
        vg = v[bidx, sel]
        qb = lax.dynamic_slice_in_dim(q, q0, Q_BLOCK, axis=1)
        s = jnp.einsum('bqhd,bqkd->bhqk', qb, kg).astype(jnp.float32) * scale
        valid = (sel <= qpos[None, :, None])[:, None]
        p = _masked_softmax(s, valid)
        return jnp.einsum('bhqk,bqkd->bqhd', p.astype(v.dtype), vg)

    return _sweep(block, S)

def _compress(tok, pos_emb, w1, w2):
    B, S, hd = tok.shape
    n_cmp = (S - CMP_LEN) // CMP_STRIDE + 1
    idx = np.arange(n_cmp)[:, None] * CMP_STRIDE + np.arange(CMP_LEN)[None, :]
    blocks = tok[:, idx] + pos_emb
    hid = jax.nn.gelu(blocks.reshape(B, n_cmp, CMP_LEN * hd) @ w1)
    return hid @ w2

def _nsa_attention(q, k_cmp, v_cmp, k_sel, v_sel, k_win, v_win, gates,
                   cmp_pos_k, cmp_w1_k, cmp_w2_k, cmp_pos_v, cmp_w1_v, cmp_w2_v):
    B, S, H, hd = q.shape
    scale = hd ** -0.5
    kc = _compress(k_cmp, cmp_pos_k, cmp_w1_k, cmp_w2_k)
    vc = _compress(v_cmp, cmp_pos_v, cmp_w1_v, cmp_w2_v)
    n_cmp = kc.shape[1]
    cmp_end = jnp.arange(n_cmp) * CMP_STRIDE + CMP_LEN - 1
    n_sel = S // SEL_LEN
    topn = min(SEL_TOPN, n_sel)
    cs = np.arange(n_cmp) * CMP_STRIDE
    ss = np.arange(n_sel) * SEL_LEN
    overlap = jnp.asarray(((cs[:, None] < ss[None, :] + SEL_LEN) &
                           (cs[:, None] + CMP_LEN > ss[None, :])).astype(np.float32))
    k_blocks = k_sel.reshape(B, n_sel, SEL_LEN, hd)
    v_blocks = v_sel.reshape(B, n_sel, SEL_LEN, hd)
    k_pad = jnp.pad(k_win, ((0, 0), (WINDOW, 0), (0, 0)))
    v_pad = jnp.pad(v_win, ((0, 0), (WINDOW, 0), (0, 0)))
    sel_ids = jnp.arange(n_sel)
    offs = jnp.arange(SEL_LEN)
    band_offs = jnp.arange(WINDOW + Q_BLOCK)
    bidx = jnp.arange(B)[:, None, None]

    def block(i):
        q0 = i * Q_BLOCK
        qpos = q0 + jnp.arange(Q_BLOCK)
        qb = lax.dynamic_slice_in_dim(q, q0, Q_BLOCK, axis=1)
        gb = lax.dynamic_slice_in_dim(gates, q0, Q_BLOCK, axis=1)
        s_c = jnp.einsum('bqhd,bnd->bhqn', qb, kc).astype(jnp.float32) * scale
        p_c = _masked_softmax(s_c, (cmp_end[None, :] <= qpos[:, None])[None, None])
        o_cmp = jnp.einsum('bhqn,bnd->bqhd', p_c.astype(vc.dtype), vc)
        imp = jnp.einsum('bhqn,nj->bqj', p_c, overlap)
        cur = qpos // SEL_LEN
        forced = ((sel_ids[None, :] == 0) | (sel_ids[None, :] == cur[:, None]) |
                  (sel_ids[None, :] == cur[:, None] - 1))
        admissible = sel_ids[None, :] * SEL_LEN <= qpos[:, None]
        imp = jnp.where(forced[None], FORCED_SCORE, imp)
        imp = jnp.where(admissible[None], imp, -jnp.inf)
        _, sel = lax.top_k(imp, topn)
        kg = k_blocks[bidx, sel].reshape(B, Q_BLOCK, topn * SEL_LEN, hd)
        vg = v_blocks[bidx, sel].reshape(B, Q_BLOCK, topn * SEL_LEN, hd)
        tok = (sel[..., None] * SEL_LEN + offs).reshape(B, Q_BLOCK, topn * SEL_LEN)
        s_s = jnp.einsum('bqhd,bqkd->bhqk', qb, kg).astype(jnp.float32) * scale
        p_s = _masked_softmax(s_s, (tok <= qpos[None, :, None])[:, None])
        o_sel = jnp.einsum('bhqk,bqkd->bqhd', p_s.astype(vg.dtype), vg)
        kw = lax.dynamic_slice_in_dim(k_pad, q0, WINDOW + Q_BLOCK, axis=1)
        vw = lax.dynamic_slice_in_dim(v_pad, q0, WINDOW + Q_BLOCK, axis=1)
        wpos = q0 - WINDOW + band_offs
        diff = qpos[:, None] - wpos[None, :]
        wmask = (diff >= 0) & (diff < WINDOW) & (wpos[None, :] >= 0)
        s_w = jnp.einsum('bqhd,bkd->bhqk', qb, kw).astype(jnp.float32) * scale
        p_w = _masked_softmax(s_w, wmask[None, None])
        o_win = jnp.einsum('bhqk,bkd->bqhd', p_w.astype(vw.dtype), vw)
        return gb[..., 0:1] * o_cmp + gb[..., 1:2] * o_sel + gb[..., 2:3] * o_win

    return _sweep(block, S)

def _hybrid_mixer(u, w_in, cmp_pos_k, cmp_w1_k, cmp_w2_k, cmp_pos_v, cmp_w1_v, cmp_w2_v, w_up, w_out):
    B, S, _ = u.shape
    p = _split_columns(u @ w_in)

    def heads(t, h, d=HEAD_DIM):
        return t.reshape(B, S, h, d)

    def rope1(t):
        return _rope(t[:, :, None, :])[:, :, 0]

    o_a = _stick_breaking(heads(p['q_a'], SB_HEADS), heads(p['k_a'], SB_HEADS), heads(p['v_a'], SB_HEADS))
    o_b = _dsa_attention(_rope(heads(p['q_b'], DSA_HEADS)), rope1(p['k_b']), p['v_b'],
                         _rope(heads(p['q_idx'], IDX_HEADS, IDX_DIM)), rope1(p['k_idx']), p['w_idx'])
    gates_c = jax.nn.sigmoid(p['g_c'].reshape(B, S, NSA_HEADS, 3))
    o_c = _nsa_attention(_rope(heads(p['q_c'], NSA_HEADS)), rope1(p['k_cmp']), p['v_cmp'],
                         rope1(p['k_sel']), p['v_sel'], rope1(p['k_win']), p['v_win'], gates_c,
                         cmp_pos_k, cmp_w1_k, cmp_w2_k, cmp_pos_v, cmp_w1_v, cmp_w2_v)
    g = jax.nn.sigmoid(p['g_merge'].reshape(B, S, 3, D_MODEL))
    merged = (g[:, :, 0] * (o_a.reshape(B, S, BRANCH_WIDTH) @ w_up[0]) +
              g[:, :, 1] * (o_b.reshape(B, S, BRANCH_WIDTH) @ w_up[1]) +
              g[:, :, 2] * (o_c.reshape(B, S, BRANCH_WIDTH) @ w_up[2]))
    return merged @ w_out

def _memory_attention(h, mem, g_q, g_kv, w_q, w_kv, w_o):
    B, S, _ = h.shape
    M = mem.shape[1]
    q = (_rmsnorm(h, g_q) @ w_q).reshape(B, S, MEM_HEADS, MEM_HEAD_DIM)
    kv = (_rmsnorm(mem, g_kv) @ w_kv).reshape(B, M, 2, MEM_HEADS, MEM_HEAD_DIM)
    s = jnp.einsum('bshd,bmhd->bhsm', q, kv[:, :, 0]).astype(jnp.float32) * MEM_HEAD_DIM ** -0.5
    pr = jax.nn.softmax(s, axis=-1)
    o = jnp.einsum('bhsm,bmhd->bshd', pr.astype(h.dtype), kv[:, :, 1])
    return o.reshape(B, S, MEM_HEADS * MEM_HEAD_DIM) @ w_o

def _swiglu(u, w_in, w_out):
    a = u @ w_in
    return (jax.nn.silu(a[..., :D_FF]) * a[..., D_FF:]) @ w_out

def first_inputs(seed: int = 0) -> dict:
    key = jax.random.key(seed)
    ks = jax.random.split(key, 21)

    def nrm(k, shape, fan_in):
        return jax.random.normal(k, shape, jnp.float32) * fan_in ** -0.5

    def gain(k, shape):
        return 1.0 + 0.05 * jax.random.normal(k, shape, jnp.float32)

    L = DEPTH
    mem_w = MEM_HEADS * MEM_HEAD_DIM
    return {
        'x': jax.random.normal(ks[0], (BATCH, SEQ, D_MODEL), jnp.float32),
        'mem': jax.random.normal(ks[1], (BATCH, N_MEM, D_MODEL), jnp.float32),
        'norm_mix': gain(ks[2], (L, D_MODEL)),
        'w_in': nrm(ks[3], (L, D_MODEL, D_IN), D_MODEL),
        'cmp_pos_k': 0.1 * jax.random.normal(ks[4], (L, CMP_LEN, HEAD_DIM), jnp.float32),
        'cmp_w1_k': nrm(ks[5], (L, CMP_LEN * HEAD_DIM, CMP_HIDDEN), CMP_LEN * HEAD_DIM),
        'cmp_w2_k': nrm(ks[6], (L, CMP_HIDDEN, HEAD_DIM), CMP_HIDDEN),
        'cmp_pos_v': 0.1 * jax.random.normal(ks[7], (L, CMP_LEN, HEAD_DIM), jnp.float32),
        'cmp_w1_v': nrm(ks[8], (L, CMP_LEN * HEAD_DIM, CMP_HIDDEN), CMP_LEN * HEAD_DIM),
        'cmp_w2_v': nrm(ks[9], (L, CMP_HIDDEN, HEAD_DIM), CMP_HIDDEN),
        'w_up': nrm(ks[10], (L, 3, BRANCH_WIDTH, D_MODEL), BRANCH_WIDTH),
        'w_out': nrm(ks[11], (L, D_MODEL, D_MODEL), D_MODEL),
        'norm_mem_q': gain(ks[12], (L, D_MODEL)),
        'norm_mem_kv': gain(ks[13], (L, D_MODEL)),
        'w_mem_q': nrm(ks[14], (L, D_MODEL, mem_w), D_MODEL),
        'w_mem_kv': nrm(ks[15], (L, D_MODEL, 2 * mem_w), D_MODEL),
        'w_mem_o': nrm(ks[16], (L, mem_w, D_MODEL), mem_w),
        'norm_ffn': gain(ks[17], (L, D_MODEL)),
        'w_ffn_in': nrm(ks[18], (L, D_MODEL, 2 * D_FF), D_MODEL),
        'w_ffn_out': nrm(ks[19], (L, D_FF, D_MODEL), D_FF),
        'norm_final': gain(ks[20], (D_MODEL,)),
    }

def first_block(x, mem, norm_mix, w_in, cmp_pos_k, cmp_w1_k, cmp_w2_k, cmp_pos_v, cmp_w1_v, cmp_w2_v,
              w_up, w_out, norm_mem_q, norm_mem_kv, w_mem_q, w_mem_kv, w_mem_o,
              norm_ffn, w_ffn_in, w_ffn_out, norm_final):
    h = x
    for l in range(DEPTH):
        h = h + _hybrid_mixer(_rmsnorm(h, norm_mix[l]), w_in[l],
                              cmp_pos_k[l], cmp_w1_k[l], cmp_w2_k[l],
                              cmp_pos_v[l], cmp_w1_v[l], cmp_w2_v[l], w_up[l], w_out[l])
        h = h + _memory_attention(h, mem, norm_mem_q[l], norm_mem_kv[l], w_mem_q[l], w_mem_kv[l], w_mem_o[l])
        h = h + _swiglu(_rmsnorm(h, norm_ffn[l]), w_ffn_in[l], w_ffn_out[l])
    return _rmsnorm(h, norm_final)


FOX_HEADS = 8
FOX_HEAD_DIM = 64
FOX_WIDTH = FOX_HEADS * FOX_HEAD_DIM
RET_HEADS = 4
RET_HEAD_DIM = 128
RET_WIDTH = RET_HEADS * RET_HEAD_DIM
MIX_WIDTH = FOX_WIDTH + RET_WIDTH
D_FF_2 = 4 * D_MODEL
RET_CHUNK = 128
ROPE_BASE = 10000.0
EPS = 1e-6
N_MOD = 6
IN_COLS = 4 * FOX_WIDTH + FOX_HEADS + 4 * RET_WIDTH


def _rms(x):
    x32 = x.astype(jnp.float32)
    return x32 * lax.rsqrt(jnp.mean(x32 * x32, axis=-1, keepdims=True) + EPS)

def _rope_2(x):
    s, d = x.shape[1], x.shape[-1]
    pos = jnp.arange(s, dtype=jnp.float32)
    inv_freq = ROPE_BASE ** (-jnp.arange(0, d, 2, dtype=jnp.float32) / d)
    ang = pos[:, None] * inv_freq[None, :]
    cos = jnp.cos(ang)[None, :, None, :]
    sin = jnp.sin(ang)[None, :, None, :]
    x32 = x.astype(jnp.float32)
    x1, x2 = x32[..., : d // 2], x32[..., d // 2:]
    return jnp.concatenate([x1 * cos - x2 * sin, x1 * sin + x2 * cos], axis=-1).astype(x.dtype)

def _forgetting_attention(q, k, v, log_f):
    b, s, h, d = q.shape
    scale = 1.0 / np.sqrt(d)
    cum = jnp.cumsum(log_f, axis=1).transpose(0, 2, 1)
    qh = q.transpose(0, 2, 1, 3)
    kh = k.transpose(0, 2, 1, 3)
    vh = v.transpose(0, 2, 1, 3)
    outs = []
    for blk in range(s // Q_BLOCK):
        s0, s1 = blk * Q_BLOCK, (blk + 1) * Q_BLOCK
        logits = jnp.einsum('bhqd,bhkd->bhqk', qh[:, :, s0:s1], kh[:, :, :s1]).astype(jnp.float32) * scale
        logits = logits + cum[:, :, s0:s1, None] - cum[:, :, None, :s1]
        q_pos = jnp.arange(s0, s1)[:, None]
        k_pos = jnp.arange(s1)[None, :]
        logits = jnp.where(q_pos >= k_pos, logits, -jnp.inf)
        p = jax.nn.softmax(logits, axis=-1).astype(v.dtype)
        outs.append(jnp.einsum('bhqk,bhkd->bhqd', p, vh[:, :, :s1]))
    out = jnp.concatenate(outs, axis=2)
    return out.transpose(0, 2, 1, 3)

def _retention(q, k, v):
    b, s, h, dk = q.shape
    dv = v.shape[-1]
    n_chunks = s // RET_CHUNK
    log_g = jnp.log(1.0 - 2.0 ** (-5.0 - jnp.arange(h, dtype=jnp.float32)))
    n = jnp.arange(RET_CHUNK, dtype=jnp.float32)
    diff = n[:, None] - n[None, :]
    decay_mask = jnp.where(diff[None] >= 0,
                           jnp.exp(jnp.maximum(diff, 0.0)[None] * log_g[:, None, None]), 0.0)
    xi = jnp.exp((n[None, :] + 1.0) * log_g[:, None])
    zeta = jnp.exp((RET_CHUNK - 1.0 - n[None, :]) * log_g[:, None])
    g_chunk = jnp.exp(RET_CHUNK * log_g)

    def to_chunks(t):
        return t.astype(jnp.float32).reshape(b, n_chunks, RET_CHUNK, h, t.shape[-1]).transpose(1, 0, 3, 2, 4)

    qc, kc, vc = to_chunks(q), to_chunks(k * (dk ** -0.5)), to_chunks(v)

    def step(state, inp):
        qi, ki, vi = inp
        inner = jnp.einsum('bhnd,bhmd->bhnm', qi, ki) * decay_mask[None]
        inner_out = jnp.einsum('bhnm,bhmv->bhnv', inner, vi)
        cross_out = jnp.einsum('bhnd,bhdv->bhnv', qi, state) * xi[None, :, :, None]
        new_state = state * g_chunk[None, :, None, None] + \
            jnp.einsum('bhmd,bhmv->bhdv', ki * zeta[None, :, :, None], vi)
        return new_state, inner_out + cross_out

    state0 = jnp.zeros((b, h, dk, dv), jnp.float32)
    _, out = lax.scan(step, state0, (qc, kc, vc))
    return out.transpose(1, 0, 3, 2, 4).reshape(b, s, h, dv)

def second_inputs(seed: int = 0) -> dict:
    key = jax.random.key(seed)
    ks = jax.random.split(key, 16)
    nrm = jax.random.normal
    f32 = jnp.float32
    return {
        "x": nrm(ks[0], (BATCH, SEQ, D_MODEL), f32),
        "c": nrm(ks[1], (BATCH, D_MODEL), f32),
        "w_ada": nrm(ks[2], (DEPTH, D_MODEL, N_MOD * D_MODEL), f32) * (0.5 * D_MODEL ** -0.5),
        "b_ada": nrm(ks[3], (DEPTH, N_MOD * D_MODEL), f32) * 0.02,
        "w_in": nrm(ks[4], (DEPTH, D_MODEL, IN_COLS), f32) * D_MODEL ** -0.5,
        "b_forget": 2.0 + 0.5 * nrm(ks[5], (DEPTH, FOX_HEADS), f32),
        "q_norm_gain": 1.0 + 0.05 * nrm(ks[6], (DEPTH, FOX_HEAD_DIM), f32),
        "k_norm_gain": 1.0 + 0.05 * nrm(ks[7], (DEPTH, FOX_HEAD_DIM), f32),
        "fox_out_gain": 1.0 + 0.05 * nrm(ks[8], (DEPTH, FOX_HEADS, FOX_HEAD_DIM), f32),
        "ret_out_gain": 1.0 + 0.05 * nrm(ks[9], (DEPTH, RET_HEADS, RET_HEAD_DIM), f32),
        "w_out": nrm(ks[10], (DEPTH, MIX_WIDTH, D_MODEL), f32) * MIX_WIDTH ** -0.5,
        "w_mlp_in": nrm(ks[11], (DEPTH, D_MODEL, D_FF_2), f32) * D_MODEL ** -0.5,
        "w_mlp_out": nrm(ks[12], (DEPTH, D_FF_2, D_MODEL), f32) * D_FF_2 ** -0.5,
    }

def second_block(x, c, w_ada, b_ada, w_in, b_forget, q_norm_gain, k_norm_gain,
              fox_out_gain, ret_out_gain, w_out, w_mlp_in, w_mlp_out):
    b, s, _ = x.shape
    dt = x.dtype
    c_act = jax.nn.silu(c)
    o_fq, o_fk, o_fv, o_fog = 0, FOX_WIDTH, 2 * FOX_WIDTH, 3 * FOX_WIDTH
    o_ff = 4 * FOX_WIDTH
    o_rq = o_ff + FOX_HEADS
    o_rk, o_rv, o_rg = o_rq + RET_WIDTH, o_rq + 2 * RET_WIDTH, o_rq + 3 * RET_WIDTH
    for l in range(DEPTH):
        mod = jnp.einsum('bd,de->be', c_act, w_ada[l]) + b_ada[l]
        shift_m, scale_m, gate_m, shift_f, scale_f, gate_f = [m[:, None, :] for m in jnp.split(mod, N_MOD, axis=-1)]

        h = (_rms(x) * (1.0 + scale_m) + shift_m).astype(dt)
        proj = jnp.einsum('bsd,de->bse', h, w_in[l])

        fq = proj[..., o_fq:o_fk].reshape(b, s, FOX_HEADS, FOX_HEAD_DIM)
        fk = proj[..., o_fk:o_fv].reshape(b, s, FOX_HEADS, FOX_HEAD_DIM)
        fv = proj[..., o_fv:o_fog].reshape(b, s, FOX_HEADS, FOX_HEAD_DIM)
        f_og = proj[..., o_fog:o_ff]
        f_logit = proj[..., o_ff:o_rq]
        fq = (_rms(fq) * q_norm_gain[l]).astype(dt)
        fk = (_rms(fk) * k_norm_gain[l]).astype(dt)
        log_f = jax.nn.log_sigmoid(f_logit.astype(jnp.float32) + b_forget[l])
        fox = _forgetting_attention(fq, fk, fv, log_f)
        fox = (_rms(fox) * fox_out_gain[l]).reshape(b, s, FOX_WIDTH) * jax.nn.sigmoid(f_og.astype(jnp.float32))

        rq = _rope_2(proj[..., o_rq:o_rk].reshape(b, s, RET_HEADS, RET_HEAD_DIM))
        rk = _rope_2(proj[..., o_rk:o_rv].reshape(b, s, RET_HEADS, RET_HEAD_DIM))
        rv = proj[..., o_rv:o_rg].reshape(b, s, RET_HEADS, RET_HEAD_DIM)
        r_gate = proj[..., o_rg:]
        ret = _retention(rq, rk, rv)
        ret = (_rms(ret) * ret_out_gain[l]).reshape(b, s, RET_WIDTH) * jax.nn.silu(r_gate.astype(jnp.float32))

        mixed = jnp.concatenate([fox, ret], axis=-1).astype(dt)
        x = x + gate_m * jnp.einsum('bse,ed->bsd', mixed, w_out[l])

        h = (_rms(x) * (1.0 + scale_f) + shift_f).astype(dt)
        u = jnp.square(jax.nn.relu(jnp.einsum('bsd,df->bsf', h, w_mlp_in[l])))
        x = x + gate_f * jnp.einsum('bsf,fd->bsd', u, w_mlp_out[l])
    return x


def setup_inputs(seed=0):
    out = dict(first_inputs(seed))
    for name, value in second_inputs(seed + 1).items():
        if name != "x":
            out[name + "_2"] = value
    return out


def reference(
    x, mem, norm_mix, w_in, cmp_pos_k, cmp_w1_k, cmp_w2_k, cmp_pos_v, cmp_w1_v, cmp_w2_v, w_up,
    w_out, norm_mem_q, norm_mem_kv, w_mem_q, w_mem_kv, w_mem_o, norm_ffn, w_ffn_in, w_ffn_out,
    norm_final, c_2, w_ada_2, b_ada_2, w_in_2, b_forget_2, q_norm_gain_2, k_norm_gain_2,
    fox_out_gain_2, ret_out_gain_2, w_out_2, w_mlp_in_2, w_mlp_out_2,
):
    x = first_block(
        x, mem, norm_mix, w_in, cmp_pos_k, cmp_w1_k, cmp_w2_k, cmp_pos_v, cmp_w1_v, cmp_w2_v,
        w_up, w_out, norm_mem_q, norm_mem_kv, w_mem_q, w_mem_kv, w_mem_o, norm_ffn, w_ffn_in,
        w_ffn_out, norm_final,
    )
    return second_block(
        x, c_2, w_ada_2, b_ada_2, w_in_2, b_forget_2, q_norm_gain_2, k_norm_gain_2,
        fox_out_gain_2, ret_out_gain_2, w_out_2, w_mlp_in_2, w_mlp_out_2,
    )


_drawn_inputs = setup_inputs


def setup_inputs(seed=0):
    import zlib

    import numpy as np

    out = dict(_drawn_inputs(seed))
    spreads = {}
    factors = {'cmp_pos_k': 8.0,
     'cmp_pos_v': 3.814,
     'norm_mem_q': 8.0,
     'norm_mem_kv': 6.516,
     'q_norm_gain_2': 8.0,
     'k_norm_gain_2': 8.0,
     'fox_out_gain_2': 8.0,
     'ret_out_gain_2': 8.0}
    for name, (base, spread) in spreads.items():
        noise = np.random.default_rng([zlib.crc32(name.encode()), seed]).standard_normal(out[name].shape)
        drawn = base * np.exp(spread * noise) if base else spread * noise
        out[name] = __import__('jax').numpy.asarray(drawn.astype(out[name].dtype))
    for name, factor in factors.items():
        out[name] = (out[name] * factor).astype(out[name].dtype)
    return out
```

```python
from contextlib import ExitStack

import numpy as np

import concourse.bass as bass
from concourse import mybir

F32 = mybir.dt.float32
F32R = mybir.dt.float32r
ALU = mybir.AluOpType
ACT = mybir.ActivationFunctionType
X = mybir.AxisListType.X

P = 128
T = 256
NT = T // P
D = 1024
KD = D // P
HD = 64
SCALE = HD ** -0.5
EPS = 1e-6
NEG = -1e30
TAKEN = -3e30
TOPK = min(256, T // 4)
CMP_LEN, CMP_STRIDE, CMP_HIDDEN = 32, 16, 128
NC = (T - CMP_LEN) // CMP_STRIDE + 1
W_COLS = 256
ROWS = 256
BLOCK = KD * W_COLS
RAW, SPLIT = 4, 3
D_FF = 2816
D_FF2 = 4096
FH, RH, RD = 8, 4, 128
AUG = HD + 2

QA, KA, VA, QB, KB, VB, QI, KI, WI, QC, KCMP, VCMP, KSEL, VSEL, KWIN, VWIN, GC, GM = np.cumsum(
    [0, 256, 256, 256, 256, 64, 64, 256, 64, 4, 256, 64, 64, 64, 64, 64, 64, 12]).tolist()
PROJ = GM
FQ, FK, FV, FOG, FF, RQ, RK, RV, RG = np.cumsum([0, 512, 512, 512, 512, 8, 512, 512, 512]).tolist()
PROJ2 = RG + 512

CONST_WIDTHS = dict(ident=P, suffix=P, prefix=P, ones=P, causal=2 * P, strict=3 * P, cos1=64, sin1=64, nsin1=64,
                    cos2=128, sin2=128, nsin2=128, cmpneg=2 * NC, cmp01=2 * NC, decay=RH * 2 * P)
CONST_AT = dict(zip(CONST_WIDTHS, np.cumsum([0] + list(CONST_WIDTHS.values())).tolist()))
CONSTS = sum(CONST_WIDTHS.values())
DECAY_AT = CONST_AT["decay"]

ROW_AT = dict(norm_mix=0, norm_mem_kv=8, norm_mem_q=16, norm_ffn=24, c=32, b_ada=40, pos_k=88, pos_v=104)
NROWS = 120


def constants():
    f = np.float32
    i, j = np.arange(P)[:, None], np.arange(P)[None, :]
    out = np.zeros((P, CONSTS), f)

    def put(name, a):
        out[:, CONST_AT[name]:CONST_AT[name] + CONST_WIDTHS[name]] = np.asarray(a, f).reshape(P, -1)

    put("ident", i == j)
    put("suffix", i >= j)
    put("prefix", i <= j)
    put("ones", np.ones((P, P)))
    put("causal", np.concatenate([np.zeros((P, P)), np.where(j <= i, 0, NEG)], 1))
    below = np.where(i < j, 0, NEG)
    put("strict", np.concatenate([below, np.zeros((P, P)), below], 1))
    for n, hd in (("1", HD), ("2", RD)):
        inv = f(10000.0) ** (-np.arange(0, hd, 2, dtype=f) / f(hd))
        ang = np.arange(T, dtype=f)[:, None] * inv[None, :]
        for name, a in (("cos", np.cos(ang)), ("sin", np.sin(ang)), ("nsin", -np.sin(ang))):
            put(name + n, a.reshape(NT, P, hd // 2).transpose(1, 0, 2))
    log_g = np.log(1.0 - 2.0 ** (-5.0 - np.arange(RH)))
    decay = [np.concatenate([np.where(j >= i, np.exp(np.maximum(j - i, 0) * g), 0), np.exp((j + P - i) * g)], 1)
             for g in log_g]
    put("decay", np.concatenate(decay, 1) * RD ** -0.5)
    seen = np.concatenate([(np.arange(NC)[None, :] * CMP_STRIDE + CMP_LEN - 1 <= i + t * P) for t in range(NT)], 1)
    put("cmpneg", np.where(seen, 0, NEG))
    put("cmp01", seen)
    return out



def plan():
    blocks = [("proj", j) for j in range(9)] + [("mem_k",), ("mem_v",)] + [("gate", j) for j in range(12)]
    blocks += [("up", j) for j in range(3)] + [("out", j) for j in range(4)] + [("mem_q",), ("mem_o",)]
    blocks += [("ffn_in", 0), ("ffn_in", 1)]
    for i in range(1, 11):
        blocks += [("ffn_in", 2 * i), ("ffn_in", 2 * i + 1), ("ffn_out", i - 1)]
    blocks += [("ffn_out", 10)]
    blocks += [("proj2", j) for j in range(17)] + [("out2", j) for j in range(4)]
    blocks += [("mlp_in", 0)]
    for i in range(1, 16):
        blocks += [("mlp_in", i), ("mlp_out", i - 1)]
    blocks += [("mlp_out", 15)]
    where = {b: s for s, b in enumerate(blocks)}
    table, raw, split_to = [], [], [0]

    def add(*step):
        table.append(step)

    def split(upto):
        while split_to[0] <= min(upto, len(blocks) - 1):
            s = split_to[0]
            add("round", s)
            add("residue", s)
            raw.append(("split", s))
            split_to[0] += 1

    def block(*b, evac=True):
        s = where[b]
        split(s)
        add("block", s)
        split(s + 2)
        if evac:
            add("evac", s)

    def norm(n):
        add("ssq", n)
        add("rstd", n)
        for t in range(NT):
            add("xhat", n, t)
        for c in range(KD // 2):
            add("turn", n, c)

    def units(pairs, fill):
        n = len(pairs)
        for i in range(n + 2):
            if i >= 2:
                for u in pairs[i - 2]:
                    add("pv", u)
                    if u in UNIT_ENDS:
                        add("o_group", UNIT_ENDS[u])
            if 1 <= i <= n:
                for u in pairs[i - 1]:
                    add("turn_p", u)
            if i < n:
                for u in pairs[i]:
                    add("scores", u)
            fill()

    add("columns")
    norm(0)
    split(1)
    for j in range(3):
        block("proj", j)
    norm(1)
    block("proj", 3)
    add("turn_qk", 0)
    block("proj", 4)
    add("turn_qk", 1)
    block("proj", 5)
    for h in (0, 1):
        add("stick", h)
    add("rope1", 1)
    block("proj", 6)
    add("suffix", 0), add("suffix", 1)
    block("proj", 7)
    add("rope1", 0)
    add("pv_stick", 0), add("pv_stick", 1)
    add("stick", 2), add("stick", 3)
    add("rope1", 2)
    block("proj", 8)
    add("rope1", 3)
    add("suffix", 2), add("suffix", 3)
    add("gates_c")
    for i in (4, 5, 6):
        add("turn_qk", i)
    block("mem_k")
    add("pv_stick", 2), add("pv_stick", 3)
    add("o_group", 0)
    add("index", 0), add("index", 1)
    add("topk", 0, 0), add("topk", 0, 1)
    add("turn_cmp", 0), add("turn_cmp", 1)
    block("mem_v")
    add("topk", 1, 0)
    raw.append(("cmp_w1", 0))
    add("cmp_hidden", 0)
    raw.append(("cmp_w1", 1))
    add("cmp_hidden", 1)
    add("topk", 1, 1)
    block("gate", 0)
    add("turn_qk", 2), add("turn_qk", 3)
    add("cmp_kv")
    add("cmp_scores")
    block("gate", 1)
    add("turn_cmp_p")
    add("cmp_pv")
    add("o_group", 1)
    fillers = iter(range(2, 12))
    units([(4, 5), (6, 7), (8, 9), (10, 11), (0, 1), (2, 3)], lambda: [block("gate", j) for j in [next(fillers)]])
    for j in fillers:
        block("gate", j)
    for c in range(3):
        add("turn_o", c)
    for j in range(3):
        block("up", j, evac=False)
        add("merge", j)
    add("merged")
    for j in range(4):
        block("out", j, evac=False)
    add("residual", 0)
    norm(2)
    block("mem_q")
    units([(12, 13), (14, 15)], lambda: None)
    add("turn_o", 3)
    block("mem_o", evac=False)
    add("residual", 1)
    norm(3)
    parts = {"first": table}
    table = parts["ffn"] = []
    ada_at = len(raw)
    block("ffn_in", 0)
    block("ffn_in", 1)
    for i in range(1, 11):
        block("ffn_in", 2 * i)
        raw.append(("ada", i - 1))
        add("ada", i - 1)
        block("ffn_in", 2 * i + 1)
        block("ffn_out", i - 1, evac=False)
        add("ada_sum", i - 1)
    block("ffn_out", 10, evac=False)
    add("mod", 0)
    table = parts["second"] = []
    add("residual", 2)
    add("ssq", 4)
    add("rstd", 4)
    add("final_norm")
    norm(5)
    ada, summed = iter(range(10, 24)), []

    def more_ada():
        if summed:
            add("ada_sum", summed.pop())
        for j in ada:
            raw.append(("ada", j))
            add("ada", j)
            summed.append(j)
            return

    for j in range(9):
        block("proj2", j)
        more_ada()
        if j == 1:
            add("fox_square", 0)
        if j == 3:
            add("fox_square", 1)
            add("fox_norm", 0)
        if j == 4:
            add("forget")
            add("fox_norm", 1)
        if j == 5:
            add("forget_sum")
        if j == 6:
            add("rope2", 0)
            for i in range(4):
                add("turn_fox", i)
        if j == 7:
            for i in range(4, 8):
                add("turn_fox", i)
        if j == 8:
            add("rope2", 1)
    add("gate_row", 0)
    rest = iter(range(9, 17))

    def more():
        for j in rest:
            block("proj2", j)
            more_ada()
            return

    more()
    for i in range(4):
        add("turn_ret", i)
    more()
    units([(16, 17), (18, 19), (20, 21), (22, 23)], more)
    for j in rest:
        block("proj2", j)
    more_ada()
    for h in range(RH):
        add("ret_scores", h)
        if h:
            add("ret_pv", h - 1)
    add("ret_pv", RH - 1)
    add("o_group", 8)
    add("mix", 0)
    add("mix", 1)
    for c in range(KD // 2):
        add("turn_mixed", c)
    for j in range(4):
        block("out2", j, evac=False)
    add("residual", 3)
    add("mod", 1)
    norm(6)
    add("gate_row", 1)
    table = parts["mlp"] = []
    block("mlp_in", 0)
    for i in range(1, 16):
        block("mlp_in", i)
        block("mlp_out", i - 1, evac=False)
    block("mlp_out", 15, evac=False)
    add("residual", 4)
    return parts, blocks, where, raw


UNITS = [("b", t, hp) for t in range(NT) for hp in range(2)] + [("c", t, h) for t in range(NT) for h in range(4)]
UNITS += [("mem", t, hp) for t in range(NT) for hp in range(2)] + [("fox", t, hp) for t in range(NT) for hp in range(4)]
GROUP = {"b": lambda t: 2, "c": lambda t: 3 + t, "mem": lambda t: 5, "fox": lambda t: 6 + t}
UNIT_ENDS = {7: 3, 11: 4, 3: 2, 15: 5, 19: 6, 23: 7}
XHAT = {n: i for i, n in enumerate([0, 1, 2, 3, 5, 6])}
GAIN = {0: "norm_mix", 1: "norm_mem_kv", 2: "norm_mem_q", 3: "norm_ffn"}
RESIDUAL = {2: "out", 3: "mem_o", 4: "ffn_out"}
ORDER = {u: 4 + n for n, u in enumerate([4, 5, 6, 7, 8, 9, 10, 11, 0, 1, 2, 3] + list(range(12, 24)))}
O_BANK = {0: 2, 1: 3, 3: 2, 4: 3, 2: 2, 5: 3, 6: 2, 7: 3, 8: 2, 9: 3}
TURNS = [("QA", 0), ("KA", 2), ("QC", 4), ("KSW", 6), ("QI", 8), ("KIB", 10), ("QB", 12)]
S_QA, S_KA, S_QC, S_KSW, S_QI, S_KI, S_KB, S_QB = 0, 2, 4, 6, 8, 10, 11, 12
PROJ2_BLOCKS = [(FQ, 256), (FQ + 256, 256), (FK, 256), (FK + 256, 256), (FF, 8), (RQ, 256), (RQ + 256, 256),
                (RK, 256), (RK + 256, 256), (FV, 256), (FV + 256, 256), (RV, 256), (RV + 256, 256),
                (FOG, 256), (FOG + 256, 256), (RG, 256), (RG + 256, 256)]
SMALL = ["x", "mem", "norm_mix", "cmp_pos_k", "cmp_w2_k", "cmp_pos_v", "cmp_w2_v", "norm_mem_q", "norm_mem_kv",
         "norm_ffn", "norm_final", "c_2", "b_ada_2", "b_forget_2", "q_norm_gain_2", "k_norm_gain_2",
         "fox_out_gain_2", "ret_out_gain_2"]


def weight_stream(w):
    _, blocks, _, raw_order = plan()

    def columns(a, c0, n=W_COLS):
        return a[:, c0:c0 + n].reshape(KD, P, -1).transpose(1, 0, 2).reshape(P, -1)

    def whole_rows(a, j):
        return a[ROWS * j:ROWS * j + ROWS].reshape(ROWS // P, P, -1).transpose(1, 0, 2).reshape(P, -1)

    def ffn_in(j):
        a = w["w_ffn_in"][0].reshape(KD, P, 2, D_FF)[:, :, :, P * j:P * j + P]
        return a.transpose(1, 0, 2, 3).reshape(P, -1)

    up = np.reshape(w["w_up"][0], (-1, D))
    of = dict(
        proj=lambda j: columns(w["w_in"][0], 256 * j, min(256, PROJ - 256 * j)),
        gate=lambda j: columns(w["w_in"][0], GM + 256 * j),
        mem_k=lambda j: columns(w["w_mem_kv"][0], 0), mem_v=lambda j: columns(w["w_mem_kv"][0], 256),
        mem_q=lambda j: columns(w["w_mem_q"][0], 0), mem_o=lambda j: whole_rows(w["w_mem_o"][0], 0),
        up=lambda j: whole_rows(up, j), out=lambda j: whole_rows(w["w_out"][0], j), ffn_in=ffn_in,
        ffn_out=lambda j: whole_rows(w["w_ffn_out"][0], j),
        proj2=lambda j: columns(w["w_in_2"][0], *PROJ2_BLOCKS[j]),
        out2=lambda j: whole_rows(w["w_out_2"][0], j), mlp_in=lambda j: columns(w["w_mlp_in_2"][0], 256 * j),
        mlp_out=lambda j: whole_rows(w["w_mlp_out_2"][0], j), ada=lambda j: columns(w["w_ada_2"][0], 256 * j),
        cmp_w1=lambda j: w["cmp_w1_v" if j else "cmp_w1_k"][0].reshape(16, P, P).transpose(1, 0, 2).reshape(P, -1))
    stream = np.zeros((len(raw_order), P, BLOCK), np.float32)
    for i, what in enumerate(raw_order):
        b = blocks[what[1]] if what[0] == "split" else what
        x = of[b[0]](b[-1] if len(b) > 1 else 0)
        stream[i, :, 0:x.shape[1]] = x
    return stream


def two_blocks_kernel(nc, d, stream, consts_dram, out_dram):
    parts, blocks, where, raw_order = plan()
    table = [step for part in parts.values() for step in part]

    with ExitStack() as ctx:
        names = {}

        def sb(stack, name, shape, dt=F32):
            return stack.enter_context(nc.sbuf_tensor("sb_" + name, shape, dt))

        def sem(name):
            if name not in names:
                names[name] = ctx.enter_context(nc.semaphore(name))
            return names[name]

        raw = sb(ctx, "raw", [P, RAW, BLOCK])
        hi = sb(ctx, "hi", [P, SPLIT, BLOCK], F32R)
        lo = sb(ctx, "lo", [P, SPLIT, BLOCK], F32R)
        h = sb(ctx, "h", [P, NT, D])
        u_hi = sb(ctx, "u_hi", [P, KD, T], F32R)
        u_lo = sb(ctx, "u_lo", [P, KD, T], F32R)
        work = sb(ctx, "work", [P, NT * 2 * FH * AUG])
        row_bc = sb(ctx, "row_bc", [P, D])
        masked = sb(ctx, "masked", [P, 2, 512])
        prob = sb(ctx, "prob", [P, 2, 512])
        prob_t = sb(ctx, "prob_t", [P, 2, 512])
        const = sb(ctx, "const", [P, DECAY_AT])
        cols = sb(ctx, "cols", [P, NROWS])
        mod = sb(ctx, "mod", [P, 48])
        scale1 = sb(ctx, "scale1", [P, 2, KD])
        c_act = sb(ctx, "c_act", [P, KD])
        c_tanh = sb(ctx, "c_tanh", [P, KD])
        ada_acc = sb(ctx, "ada_acc", [P, 2, W_COLS])
        square_sum = sb(ctx, "square_sum", [P, 7, NT])
        mean_eps = sb(ctx, "mean_eps", [P, 32])
        rstd = sb(ctx, "rstd", [P, 7, NT])
        mhalf = sb(ctx, "mhalf", [P, 32])
        neg_max = sb(ctx, "neg_max", [P, 24, 2])
        den = sb(ctx, "den", [P, 24, 2])
        rden = sb(ctx, "rden", [P, 24, 2])
        rows = row_bc[0:NROWS, 0:P]

        def scope(stack, *specs):
            return [sb(stack, *s) for s in specs]

        first = ExitStack()
        s = ExitStack()
        merged_hi, merged_lo = scope(s, ("merged_hi", [P, KD, T], F32R), ("merged_lo", [P, KD, T], F32R))
        s.close()
        proj, = scope(first, ("proj", [P, NT, PROJ]))
        s = ExitStack()
        mem_t_hi, mem_t_lo, mem_rows = scope(s, ("mem_t_hi", [P, KD, T], F32R), ("mem_t_lo", [P, KD, T], F32R),
                                             ("mem_rows", [P, NT, D]))
        s.close()
        gates, qk_t, km_t, vm, sel_neg, cmp_in, kc_t, vc, w2k, w2v, hid_x, hid_t, hid_k, hid_v, cmp_s, cmp_m, \
            cmp_d, gate_c, idx_w, best = scope(
                first, ("gates", [P, 24, T]), ("qk_t", [P, 14, T]), ("km_t", [P, 2, T]), ("vm", [P, 2, T]),
                ("sel_neg", [P, NT, T]), ("cmp_in", [P, 2, 256]), ("kc_t", [P, NC]), ("vc", [P, HD]),
                ("w2k", [P, 2, HD]), ("w2v", [P, HD]), ("hid_x", [P, 2, 16]), ("hid_t", [P, 2, 16]),
                ("hid_k", [P, NC]), ("hid_v", [P, 4, 32]), ("cmp_s", [P, NT, 4, NC]), ("cmp_m", [P, 8]),
                ("cmp_d", [P, 8]), ("gate_c", [P, NT, 4, 3]), ("idx_w", [P, NT, 4]), ("best", [P, 8]))
        qm_t = qk_t[:, 0:2, :]
        first.close()
        ff = ExitStack()
        hid_hi, hid_lo, hid, act_out = scope(ff, ("hid_hi", [P, 4, T], F32R), ("hid_lo", [P, 4, T], F32R),
                                             ("hid", [P, 512]), ("act_out", [P, 2, 512]))
        ff.close()
        second = ExitStack()
        s = ExitStack()
        mixed_hi, mixed_lo = scope(s, ("mixed_hi", [P, KD, T], F32R), ("mixed_lo", [P, KD, T], F32R))
        s.close()
        fox_t, ret_t, proj2, gains, logit, soft, fstat, decays = scope(
            second, ("fox_t", [P, 2 * FH, T]), ("ret_t", [P, 2 * RH, T]), ("proj2", [P, NT, PROJ2]),
            ("gains", [P, 2 * HD + FH + 1024]), ("logit", [P, NT, FH]), ("soft", [P, NT, FH]),
            ("fstat", [P, 4, NT * FH]), ("decays", [P, RH * 2 * P]))
        second.close()

        banks = [ctx.enter_context(nc.psum_tensor(f"bank{b}", [P, 512], F32)) for b in range(8)]
        filled = [sem(f"bank{b}_filled") for b in range(8)]
        freed = [sem(f"bank{b}_freed") for b in range(8)]
        raw_loaded = [sem(f"raw{r}_loaded") for r in range(RAW)]

        def cst(name):
            a = CONST_AT[name]
            return const[:, a:a + CONST_WIDTHS[name]]

        ident, ones = cst("ident"), cst("ones")
        norm_rows = work[:, 0:NT * D].rearrange("p (t c) -> p t c", t=NT)
        o_rows = work[:, 0:NT * 768].rearrange("p (t c) -> p t c", t=NT)
        o_mem = work[:, 0:NT * 256].rearrange("p (t c) -> p t c", t=NT)
        aug = work[:, :].rearrange("p (t s h c) -> p t s h c", t=NT, s=2, h=FH)
        spare = work[:, 1536:2048]
        gain_q, gain_k = gains[:, 0:HD], gains[:, HD:2 * HD]
        b_forget = gains[:, 2 * HD:2 * HD + FH]
        out_gain = gains[:, 2 * HD + FH:]

        def width(s):
            b = blocks[s]
            if b[0] == "proj":
                return min(256, PROJ - 256 * b[1])
            return PROJ2_BLOCKS[b[1]][1] if b[0] == "proj2" else 256

        def shaped(flat, what, s=None):
            kind = what[0]
            if kind in ("up", "out", "ffn_out", "out2", "mlp_out", "mem_o"):
                return flat.rearrange("p (k n) -> p k n", k=2)
            if kind == "cmp_w1":
                return flat.rearrange("p (k n) -> p k n", k=16)
            n = width(s) if s is not None else 256
            return flat[:, 0:KD * n].rearrange("p (k n) -> p k n", k=KD)

        raw_at = {what: i for i, what in enumerate(raw_order)}

        def raw_ready(eng, what):
            i = raw_at[what]
            eng.wait_ge(raw_loaded[i % RAW], 16 * (i // RAW + 1))
            return raw[:, i % RAW, :]

        lease, uses, fills = {}, [0] * 8, [0] * 8
        turn_of = {"stream": 0, "score": 0, "turn": 0}
        POOL = {"stream": (0, 1), "score": (4, 5), "turn": (6, 7)}

        def wait_filled(eng, key):
            b, n, _ = lease[key]
            eng.wait_ge(filled[b], n)
            return banks[b]

        def free(ins, key):
            return ins.then_inc(freed[lease[key][0]], 1)

        def wait_evacuated(eng, key):
            b, _, n = lease[key]
            eng.wait_ge(freed[b], n)

        used_at = {}

        def wait_used(eng, s):
            at = used_at[s]
            if at[0] == "block_used":
                eng.wait_ge(sem("block_used"), at[1])
            else:
                wait_filled(eng, at[0])

        def run(engine_steps):
            for step in table:
                if step[0] in engine_steps:
                    engine_steps[step[0]](*step[1:])

        block = ctx.enter_context(nc.Block())

        @block.tensor
        def _(pe):
            def claim(key, bank):
                if bank in POOL:
                    turn_of[bank] ^= 1
                    bank = POOL[bank][turn_of[bank]]
                if uses[bank]:
                    pe.wait_ge(freed[bank], uses[bank])
                uses[bank] += 1
                lease[key] = (bank, fills[bank] + 1, uses[bank])
                return banks[bank]

            def fill(ins, key):
                b = lease[key][0]
                fills[b] += 1
                ins.then_inc(filled[b], 1)

            apart = [0]

            def rows_apart(ins):
                apart[0] += 1
                ins.then_inc(sem("rows_apart"), 1)
                pe.wait_ge(sem("rows_apart"), apart[0])

            def product(out, terms):
                n = len(terms)
                for i, (a_hi, a_lo, b_hi, b_lo) in enumerate(terms):
                    nc.tensor.matmul(out, a_hi, b_hi, start=(i == 0), stop=False)
                    nc.tensor.matmul(out, a_hi, b_lo, start=False, stop=False)
                    last = nc.tensor.matmul(out, a_lo, b_hi, start=False, stop=(i == n - 1))
                return last

            def weights(s):
                pe.wait_ge(sem("lo_ready"), s + 1)
                w = blocks[s]
                return shaped(hi[:, s % SPLIT, :], w, s), shaped(lo[:, s % SPLIT, :], w, s)

            def by_token(s, key, bank, x_hi, x_lo, n):
                w_hi, w_lo = weights(s)
                ps = claim(key, bank)
                for t in range(NT):
                    tok = slice(t * P, t * P + P)
                    last = product(ps[:, t * n:t * n + n], [
                        (x_hi[:, k, tok], x_lo[:, k, tok], w_hi[:, k, :], w_lo[:, k, :]) for k in range(KD)])
                return last

            def by_feature(s, key, bank, x_hi, x_lo):
                w_hi, w_lo = weights(s)
                ps = claim(key, bank)
                for m in range(2):
                    f = slice(m * P, m * P + P)
                    last = product(ps[:, m * T:m * T + T], [
                        (w_hi[:, k, f], w_lo[:, k, f], x_hi[:, k, :], x_lo[:, k, :]) for k in range(KD)])
                return last

            def accumulate(s, group, x_hi, x_lo, k0, first, last_one):
                w_hi, w_lo = weights(s)
                for t in range(NT):
                    tok = slice(t * P, t * P + P)
                    for half in range(2):
                        key = (group, t, half)
                        ps = claim(key, 2 * t + half) if first else banks[2 * t + half]
                        n = slice(half * 512, half * 512 + 512)
                        for k in range(2):
                            x1, x2 = x_hi[:, k0 + k, tok], x_lo[:, k0 + k, tok]
                            nc.tensor.matmul(ps[:, :], x1, w_hi[:, k, n], start=first and k == 0, stop=False)
                            nc.tensor.matmul(ps[:, :], x1, w_lo[:, k, n], start=False, stop=False)
                            last = nc.tensor.matmul(ps[:, :], x2, w_hi[:, k, n], start=False,
                                                    stop=last_one and k == 1)
                        if last_one and not (t == 1 and half == 1):
                            fill(last, key)
                return last, (group, 1, 1)

            def take(s):
                kind, j = blocks[s][0], blocks[s][-1]
                key = ("block", s)
                if kind == "proj" or kind == "proj2":
                    n = 0 if kind == "proj" else 5
                    if j == 0:
                        for c in range(KD // 2):
                            wait_turned(n, c)
                    last = by_token(s, key, "stream", u_hi, u_lo, width(s))
                elif kind == "gate":
                    last = by_feature(s, key, "stream", u_hi, u_lo)
                elif kind == "mem_k":
                    for c in range(KD // 2):
                        wait_turned(1, c)
                    last = by_feature(s, key, "stream", mem_t_hi, mem_t_lo)
                elif kind == "mem_v":
                    last = by_token(s, key, "stream", mem_t_hi, mem_t_lo, 256)
                elif kind == "mem_q":
                    for c in range(KD // 2):
                        wait_turned(2, c)
                    last = by_feature(s, key, "stream", u_hi, u_lo)
                elif kind in ("ffn_in", "mlp_in"):
                    if j == 0:
                        for c in range(KD // 2):
                            wait_turned(3 if kind == "ffn_in" else 6, c)
                    last = by_feature(s, key, "score", u_hi, u_lo)
                elif kind == "up":
                    return up(s, j)
                else:
                    if kind == "out":
                        pe.wait_ge(sem("merged_split"), j + 1)
                        args = (merged_hi, merged_lo, 2 * j, j == 0, j == 3)
                    elif kind == "out2":
                        wait_evacuated(pe, ("turn_mixed", j))
                        args = (mixed_hi, mixed_lo, 2 * j, j == 0, j == 3)
                    elif kind == "mem_o":
                        wait_evacuated(pe, ("turn_o", 3))
                        args = (u_hi, u_lo, 0, True, True)
                    else:
                        n = 11 if kind == "ffn_out" else 16
                        pe.wait_ge(sem("hidden_ready"), 2 * j + 2 if kind == "ffn_out" else 22 + j + 1)
                        args = (hid_hi, hid_lo, 2 * (j % 2), j == 0, j == n - 1)
                    last, key = accumulate(s, kind, *args)
                    if not args[4]:
                        used_at[s] = ("block_used", sum(x[0] == "block_used" for x in used_at.values()) + 1)
                        last.then_inc(sem("block_used"), 1)
                        return
                fill(last, key)
                used_at[s] = (key,)

            def up(s, j):
                w_hi, w_lo = weights(s)
                if j == 0:
                    for c in range(3):
                        wait_evacuated(pe, ("turn_o", c))
                for c in range(4):
                    ps = claim(("up", j, c), c)
                    for m in range(2):
                        f = slice((2 * c + m) * P, (2 * c + m + 1) * P)
                        last = product(ps[:, m * T:m * T + T], [
                            (w_hi[:, k, f], w_lo[:, k, f], u_hi[:, 2 * j + k, :], u_lo[:, 2 * j + k, :])
                            for k in range(2)])
                    fill(last, ("up", j, c))
                used_at[s] = (("up", j, 3),)

            def wait_turned(n, c):
                wait_evacuated(pe, ("turn", n, c))
            def columns():
                pe.wait_ge(sem("const_loaded"), 16)
                pe.wait_ge(sem("rows_loaded"), 16 * len(ROW_AT))
                ps = claim(("columns",), "turn")
                fill(nc.tensor.transpose(ps[:, 0:NROWS], rows, ident[0:NROWS, 0:NROWS]), ("columns",))

            def norm_turn(n, c):
                if n == 0 and c == 0:
                    pe.wait_ge(sem("const_loaded"), 16)
                pe.wait_ge(sem("xhat_ready"), NT * XHAT[n] + NT)
                ps = claim(("turn", n, c), "turn" if c % 2 else "score")
                for k in range(2):
                    for t in range(NT):
                        f = (2 * c + k) * P
                        last = nc.tensor.transpose(ps[:, k * T + t * P:k * T + t * P + P],
                                                   norm_rows[:, t, f:f + P], ident)
                fill(last, ("turn", n, c))

            def turn_qk(i):
                ps = claim(("turn_qk", i), "turn")
                kind = TURNS[i][0]
                if kind in ("QA", "KA"):
                    wait_evacuated(pe, ("block", where["proj", 0 if kind == "QA" else 1]))
                else:
                    pe.wait_ge(sem("rope_done"), {"QC": 3, "KSW": 4, "QI": 1, "KIB": 2, "QB": 2}[kind])
                at = {"QA": QA, "KA": KA, "QC": QC, "QI": QI, "QB": QB}
                pair = {"KSW": (KSEL, KWIN), "KIB": (KI, KB)}
                for m in range(2):
                    for t in range(NT):
                        out = ps[:, m * T + t * P:m * T + t * P + P]
                        if kind in at:
                            last = nc.tensor.transpose(out, proj[:, t, at[kind] + m * P:at[kind] + m * P + P], ident)
                        else:
                            c = pair[kind][m]
                            last = nc.tensor.transpose(out[0:HD, :], proj[:, t, c:c + HD], ident)
                fill(last, ("turn_qk", i))

            def stick(hd):
                ps = claim(("stick", hd), "score")
                if hd == 0:
                    wait_evacuated(pe, ("turn_qk", 0))
                    wait_evacuated(pe, ("turn_qk", 1))
                r = slice(HD * (hd % 2), HD * (hd % 2) + HD)
                q, k = qk_t[r, S_QA + hd // 2, :], qk_t[r, S_KA + hd // 2, :]
                nc.tensor.matmul(ps[:, 0:T], k[:, 0:P], q, start=True, stop=True)
                fill(nc.tensor.matmul(ps[:, T:T + P], k[:, P:T], q[:, P:T], start=True, stop=True), ("stick", hd))

            def suffix(hd):
                pe.wait_ge(sem("softplus_ready"), hd + 1)
                ps = claim(("suffix", hd), "turn")
                l = prob_t[:, hd % 2, :]
                nc.tensor.matmul(ps[:, T:T + P], cst("suffix"), l[:, T:T + P], start=True, stop=True)
                nc.tensor.matmul(ps[:, 0:P], cst("suffix"), l[:, 0:P], start=True, stop=True)
                nc.tensor.matmul(ps[:, P:T], cst("suffix"), l[:, P:T], start=True, stop=False)
                fill(nc.tensor.matmul(ps[:, P:T], ones, l[:, T:T + P], start=False, stop=True), ("suffix", hd))

            def pv_stick(hd):
                pe.wait_ge(sem("exp_done"), hd + 1)
                if hd == 0:
                    claim(("o", 0), O_BANK[0])
                    wait_evacuated(pe, ("block", where["proj", 2]))
                w, c = prob[:, hd % 2, :], VA + HD * hd
                o0 = banks[O_BANK[0]][:, HD * hd:HD * hd + HD]
                o1 = banks[O_BANK[0]][:, HD * (4 + hd):HD * (4 + hd) + HD]
                nc.tensor.matmul(o0, w[:, 0:P], proj[:, 0, c:c + HD], start=True, stop=True)
                nc.tensor.matmul(o1, w[:, P:T], proj[:, 0, c:c + HD], start=True, stop=False)
                nc.tensor.matmul(o1, w[:, T:T + P], proj[:, 1, c:c + HD], start=False, stop=True) \
                    .then_inc(sem("pv_done"), 1)

            def index(t):
                n = P * (t + 1)
                for i in range(2):
                    ps = claim(("index", t, i), "score")
                    if t == 0 and i == 0:
                        wait_evacuated(pe, ("turn_qk", 4))
                        wait_evacuated(pe, ("turn_qk", 5))
                    r = slice(HD * i, HD * i + HD)
                    for m in range(2):
                        last = nc.tensor.matmul(ps[:, m * n:m * n + n], qk_t[r, S_QI + m, t * P:t * P + P],
                                                qk_t[r, S_KI, 0:n], start=True, stop=True)
                    fill(last, ("index", t, i))

            def turn_cmp(i):
                ps = claim(("turn_cmp", i), "turn")
                if i == 0:
                    pe.wait_ge(sem("rope_done"), 3)
                else:
                    wait_evacuated(pe, ("block", where["proj", 7]))
                c = (KCMP, VCMP)[i]
                for t in range(NT):
                    last = nc.tensor.transpose(ps[0:HD, t * P:t * P + P], proj[:, t, c:c + HD], ident)
                fill(last, ("turn_cmp", i))

            def cmp_hidden(i):
                w = shaped(raw_ready(pe, ("cmp_w1", i)), ("cmp_w1", i))
                ps = claim(("cmp_hidden", i), "turn")
                pe.wait_ge(sem("cmp_in_ready"), i + 1)
                x = cmp_in[:, i, :].rearrange("p (k n) -> p k n", k=16)
                for k in range(16):
                    last = nc.tensor.matmul(ps[:, 0:16], w[:, k, :], x[:, k, :], start=(k == 0), stop=(k == 15))
                fill(last, ("cmp_hidden", i))

            def cmp_kv():
                pe.wait_ge(sem("cmp_hid_ready"), 1)
                pe.wait_ge(sem("w2_loaded"), 16 * 3)
                ps = claim(("cmp_kv",), "turn")
                nc.tensor.matmul(ps[:, 0:NC], w2k[:, :, :].rearrange("p a b -> p (a b)"), hid_k[:, :],
                                 start=True, stop=True)
                fill(nc.tensor.matmul(ps[:, HD:2 * HD], hid_v[:, :, :].rearrange("p a b -> p (a b)"), w2v[:, :],
                                      start=True, stop=True), ("cmp_kv",))

            def cmp_scores():
                wait_evacuated(pe, ("cmp_kv",))
                wait_evacuated(pe, ("turn_qk", 2))
                ps = claim(("cmp_scores",), "score")
                for odd in range(2):
                    r = slice(HD * odd, HD * odd + HD)
                    for t in range(NT):
                        for m in range(2):
                            at = 16 * (4 * t + 2 * m + odd)
                            last = nc.tensor.matmul(ps[:, at:at + NC], qk_t[r, S_QC + m, t * P:t * P + P],
                                                    kc_t[r, :], start=True, stop=True)
                    if not odd:
                        rows_apart(last)
                fill(last, ("cmp_scores",))

            def turn_cmp_p():
                pe.wait_ge(sem("cmp_p_ready"), 1)
                ps = claim(("turn_cmp_p",), "turn")
                for t in range(NT):
                    last = nc.tensor.transpose(ps[:, t * P:t * P + P], cmp_in[:, 0, t * P:t * P + P], ident)
                fill(last, ("turn_cmp_p",))

            def cmp_pv():
                wait_evacuated(pe, ("turn_cmp_p",))
                ps = claim(("o", 1), O_BANK[1])
                for hd in range(4):
                    for t in range(NT):
                        r = slice(32 * hd, 32 * hd + NC)
                        at = HD * (4 * t + hd)
                        last = nc.tensor.matmul(ps[:, at:at + HD], cmp_in[r, 1, t * P:t * P + P], vc[r, :],
                                                start=True, stop=True, tile_position=(32 * hd, 0))
                    if hd < 3:
                        rows_apart(last)
                fill(last, ("o", 1))

            def scores(u):
                kind, t, i = UNITS[u]
                n = T if kind == "mem" else P * (t + 1)
                tok = slice(t * P, t * P + P)
                if u == 4:
                    wait_evacuated(pe, ("turn_qk", 3))
                if u == 0:
                    wait_evacuated(pe, ("turn_qk", 6))
                if u == 12:
                    wait_evacuated(pe, ("block", where["mem_q",]))
                    wait_evacuated(pe, ("block", where["mem_k",]))
                if u == 16:
                    for c in range(8):
                        wait_evacuated(pe, ("turn_fox", c))
                ps = claim(("scores", u), "score")
                if kind == "c":
                    r = slice(HD * (i % 2), HD * (i % 2) + HD)
                    last = nc.tensor.matmul(ps[:, 0:2 * n].rearrange("p (s n) -> p s n", s=2),
                                            qk_t[r, S_QC + i // 2, tok], qk_t[r, S_KSW:S_KSW + 2, 0:n],
                                            start=True, stop=True)
                else:
                    for m in range(2):
                        r = slice(HD * i, HD * i + HD)
                        if kind == "b":
                            q, k = qk_t[r, S_QB + m, tok], qk_t[r, S_KB, 0:n]
                        elif kind == "mem":
                            q, k = qm_t[r, m, tok], km_t[r, m, :]
                        else:
                            q, k = fox_t[0:AUG, 2 * i + m, tok], fox_t[0:AUG, FH + 2 * i + m, 0:n]
                        last = nc.tensor.matmul(ps[:, m * n:m * n + n], q, k, start=True, stop=True)
                fill(last, ("scores", u))

            def turn_p(u):
                kind, t, _ = UNITS[u]
                keys = NT if kind == "mem" else t + 1
                pe.wait_ge(sem("exp_done"), ORDER[u] + 1)
                ps = claim(("turn_p", u), "turn")
                for i in range(2 * keys):
                    last = nc.tensor.transpose(ps[:, i * P:i * P + P], prob[:, ORDER[u] % 2, i * P:i * P + P], ident)
                fill(last, ("turn_p", u))

            def pv(u):
                kind, t, i = UNITS[u]
                keys = NT if kind == "mem" else t + 1
                g = GROUP[kind](t)
                if ("o", g) not in lease:
                    claim(("o", g), O_BANK[g])
                if u == 12:
                    wait_evacuated(pe, ("block", where["mem_v",]))
                if u == 16:
                    wait_evacuated(pe, ("block", where["proj2", 9]))
                    wait_evacuated(pe, ("block", where["proj2", 10]))
                wait_evacuated(pe, ("turn_p", u))
                for m in range(2):
                    at = HD * {"b": 4 * t + 2 * i + m, "c": 2 * i + m, "mem": 4 * t + 2 * i + m, "fox": 2 * i + m}[kind]
                    for kt in range(keys):
                        c = HD * (2 * i + m)
                        v = {"b": lambda: proj[:, kt, VB:VB + HD],
                             "c": lambda: proj[:, kt, (VSEL, VWIN)[m]:(VSEL, VWIN)[m] + HD],
                             "mem": lambda: vm[:, kt, HD * (i + 2 * m):HD * (i + 2 * m) + HD],
                             "fox": lambda: proj2[:, kt, FV + c:FV + c + HD]}[kind]()
                        p = prob_t[:, ORDER[u] % 2, (m * keys + kt) * P:(m * keys + kt + 1) * P]
                        last = nc.tensor.matmul(banks[O_BANK[g]][:, at:at + HD], p, v,
                                                start=(kt == 0), stop=(kt == keys - 1))
                last.then_inc(sem("pv_done"), 1)

            def turn_o(c):
                if c in (0, 3):
                    wait_evacuated(pe, ("o", 0 if c == 0 else 5))
                elif c == 1:
                    wait_evacuated(pe, ("o", 2))
                else:
                    pe.wait_ge(sem("branch_c_done"), NT)
                ps = claim(("turn_o", c), "turn")
                for m in range(2):
                    for t in range(NT):
                        x = o_mem[:, t, m * P:m * P + P] if c == 3 else o_rows[:, t, 256 * c + m * P:256 * c + m * P + P]
                        last = nc.tensor.transpose(ps[:, m * T + t * P:m * T + t * P + P], x, ident)
                fill(last, ("turn_o", c))

            def ada_sum(j):
                pe.wait_ge(sem("ada_ready"), j + 1)
                ps = claim(("ada_sum", j), "turn")
                for m in range(2):
                    last = nc.tensor.matmul(ps[:, m:m + 1], ada_acc[:, j % 2, m * P:m * P + P], ones[:, 0:1],
                                            start=True, stop=True)
                fill(last, ("ada_sum", j))

            def gate_row(i):
                pe.wait_ge(sem("diag_ready"), i + 1)
                for half in range(2):
                    ps = claim(("gate_row", i, half), "score")
                    for m in range(4):
                        k = 4 * half + m
                        last = nc.tensor.matmul(ps[:, m * P:m * P + P], ones, work[:, k * P:k * P + P],
                                                start=True, stop=True)
                    fill(last, ("gate_row", i, half))

            def forget_sum():
                pe.wait_ge(sem("log_f_ready"), 1)
                ps = claim(("forget_sum",), "turn")
                nc.tensor.matmul(ps[:, 0:FH], cst("prefix"), soft[:, 0, :], start=True, stop=True)
                nc.tensor.matmul(ps[:, FH:2 * FH], cst("prefix"), soft[:, 1, :], start=True, stop=False)
                fill(nc.tensor.matmul(ps[:, FH:2 * FH], ones, soft[:, 0, :], start=False, stop=True),
                     ("forget_sum",))

            def turn_fox(i):
                pe.wait_ge(sem("aug_ready"), 3)
                ps = claim(("turn_fox", i), "turn")
                for m in range(2):
                    hd = (2 * i + m) % FH
                    for t in range(NT):
                        last = nc.tensor.transpose(ps[0:AUG, m * T + t * P:m * T + t * P + P],
                                                   aug[:, t, i // 4, hd, :], ident)
                fill(last, ("turn_fox", i))

            def turn_ret(i):
                pe.wait_ge(sem("rope2_done"), 1 + i // 2)
                ps = claim(("turn_ret", i), "turn")
                for m in range(2):
                    c = (RQ, RK)[i // 2] + RD * (2 * (i % 2) + m)
                    for t in range(NT):
                        last = nc.tensor.transpose(ps[:, m * T + t * P:m * T + t * P + P],
                                                   proj2[:, t, c:c + RD], ident)
                fill(last, ("turn_ret", i))

            def ret_scores(hd):
                if hd == 0:
                    for i in range(4):
                        wait_evacuated(pe, ("turn_ret", i))
                ps = claim(("ret_scores", hd), "score")
                q, k = ret_t[:, hd, :], ret_t[:, RH + hd, :]
                nc.tensor.matmul(ps[:, 0:T], k[:, 0:P], q, start=True, stop=True)
                fill(nc.tensor.matmul(ps[:, T:T + P], k[:, P:T], q[:, P:T], start=True, stop=True),
                     ("ret_scores", hd))

            def ret_pv(hd):
                wait_evacuated(pe, ("ret_scores", hd))
                if hd == 0:
                    claim(("o", 8), O_BANK[8])
                    claim(("o", 9), O_BANK[9])
                    wait_evacuated(pe, ("block", where["proj2", 11]))
                    wait_evacuated(pe, ("block", where["proj2", 12]))
                w, c = prob[:, hd % 2, :], RV + RD * hd
                o0, o1 = (banks[O_BANK[8 + t]][:, RD * hd:RD * hd + RD] for t in range(NT))
                nc.tensor.matmul(o0, w[:, 0:P], proj2[:, 0, c:c + RD], start=True, stop=True)
                nc.tensor.matmul(o1, w[:, P:T], proj2[:, 0, c:c + RD], start=True, stop=False)
                nc.tensor.matmul(o1, w[:, T:T + P], proj2[:, 1, c:c + RD], start=False, stop=True) \
                    .then_inc(sem("pv_done"), 1)

            def turn_mixed(c):
                pe.wait_ge(sem("mix_done"), 2)
                ps = claim(("turn_mixed", c), "turn")
                for k in range(2):
                    for t in range(NT):
                        f = (2 * c + k) * P
                        last = nc.tensor.transpose(ps[:, k * T + t * P:k * T + t * P + P],
                                                   norm_rows[:, t, f:f + P], ident)
                fill(last, ("turn_mixed", c))

            run(dict(block=take, columns=columns, turn=norm_turn, turn_qk=turn_qk, stick=stick, suffix=suffix,
                     pv_stick=pv_stick, index=index, turn_cmp=turn_cmp, cmp_hidden=cmp_hidden, cmp_kv=cmp_kv,
                     cmp_scores=cmp_scores, turn_cmp_p=turn_cmp_p, cmp_pv=cmp_pv, scores=scores, turn_p=turn_p,
                     pv=pv, turn_o=turn_o, ada_sum=ada_sum, gate_row=gate_row, forget_sum=forget_sum,
                     turn_fox=turn_fox, turn_ret=turn_ret, ret_scores=ret_scores, ret_pv=ret_pv,
                     turn_mixed=turn_mixed))

        @block.scalar
        def _(act):
            chain = [0]

            def link(ins):
                chain[0] += 1
                ins.then_inc(sem("act_chain"), 1)
                act.wait_ge(sem("act_chain"), chain[0])

            def round_block(s):
                x = raw_ready(act, ("split", s))
                n = KD * width(s) if width(s) != 256 else BLOCK
                if s >= SPLIT:
                    wait_used(act, s - SPLIT)
                nc.scalar.copy(hi[:, s % SPLIT, 0:n], x[:, 0:n]).then_inc(sem("hi_ready"), 1)

            def evac(s):
                kind, j = blocks[s][0], blocks[s][-1]
                key = ("block", s)
                ps = wait_filled(act, key)
                n = width(s)
                both = ps[:, 0:2 * n].rearrange("p (t n) -> p t n", t=2)
                if kind == "proj":
                    free(nc.scalar.copy(proj[:, :, 256 * j:256 * j + n], both), key)
                elif kind == "gate":
                    free(nc.scalar.activation(gates[:, 2 * j:2 * j + 2, :], both, ACT.Tanh, scale=0.5), key)
                elif kind in ("mem_k", "mem_v", "mem_q"):
                    dst = {"mem_k": km_t, "mem_v": vm, "mem_q": qm_t}[kind]
                    free(nc.scalar.copy(dst[:, :, :] if kind != "mem_q" else dst, both), key)
                elif kind == "proj2":
                    c = PROJ2_BLOCKS[j][0]
                    free(nc.scalar.copy(proj2[:, :, c:c + n], both), key)
                elif kind == "ffn_in":
                    if j >= 2:
                        act.wait_ge(sem("hidden_ready"), j - 1)
                    nc.scalar.activation(act_out[:, j % 2, 0:T], ps[:, 0:T], ACT.Silu) \
                        .then_inc(sem("silu_ready"), 1)
                else:
                    if j >= 2:
                        act.wait_ge(sem("hidden_ready"), 22 + j - 1)
                    free(nc.scalar.activation(act_out[:, j % 2, :], ps[:, :], ACT.Relu), key)

            def ssq(n):
                if n == 0:
                    act.wait_ge(sem("x_loaded"), 16)
                elif n == 1:
                    act.wait_ge(sem("mem_loaded"), 16)
                    wait_evacuated(act, ("turn", 0, KD // 2 - 1))
                elif n == 5:
                    act.wait_ge(sem("final_done"), NT)
                elif n == 6:
                    act.wait_ge(sem("gated"), 4)
                src = mem_rows if n == 1 else h
                for t in range(NT):
                    if n in RESIDUAL:
                        for half in range(2):
                            wait_evacuated(act, (RESIDUAL[n], t, half))
                    nc.scalar.activation(norm_rows[:, t, :], src[:, t, :], ACT.Square,
                                         accum_out=square_sum[:, n, t:t + 1]).then_inc(sem("squares_summed"), 1)

            def turn(n, c):
                ps = wait_filled(act, ("turn", n, c))
                dst = mem_t_hi if n == 1 else u_hi
                if n == 0 and c == 0:
                    wait_evacuated(act, ("columns",))
                if n >= 5 and c == 0:
                    act.wait_ge(sem("mod_ready"), n - 4)
                for m in range(2):
                    k, x = 2 * c + m, ps[:, m * T:m * T + T]
                    if n >= 5:
                        shift = mod[:, 24 * (n - 5) + k:24 * (n - 5) + k + 1]
                        last = nc.scalar.activation(dst[:, k, :], x, ACT.Identity, bias=shift,
                                                    scale=scale1[:, n - 5, k:k + 1])
                    else:
                        g = ROW_AT[GAIN[n]] + k
                        last = nc.scalar.activation(dst[:, k, :], x, ACT.Copy, scale=cols[:, g:g + 1])
                last.then_inc(sem("turn_hi"), 1)

            def columns():
                ps = wait_filled(act, ("columns",))
                free(nc.scalar.copy(cols[:, :], ps[:, 0:NROWS]), ("columns",))
                wait_evacuated(act, ("columns",))
                c = ROW_AT["c"]
                nc.scalar.activation(c_tanh[:, :], cols[:, c:c + KD], ACT.Tanh, scale=0.5) \
                    .then_inc(sem("c_tanh_ready"), 1)

            def turn_qk(i):
                ps = wait_filled(act, ("turn_qk", i))
                if TURNS[i][0] in ("KSW", "KIB"):
                    for r in (0, HD):
                        last = nc.scalar.copy(qk_t[r:r + HD, 2 * i:2 * i + 2, :],
                                              ps[0:HD, :].rearrange("p (m n) -> p m n", m=2))
                    free(last, ("turn_qk", i))
                    return
                free(nc.scalar.copy(qk_t[:, 2 * i:2 * i + 2, :], ps[:, :].rearrange("p (m n) -> p m n", m=2)),
                     ("turn_qk", i))

            def stick(hd):
                act.wait_ge(sem("stick_masked"), hd + 1)
                if hd >= 2:
                    act.wait_ge(sem("pv_done"), hd - 1)
                z, p = masked[:, hd % 2, 0:3 * P], prob[:, hd % 2, 0:3 * P]
                link(nc.scalar.activation(p, z, ACT.Abs))
                link(nc.scalar.activation(p, p, ACT.Exp, scale=-1.0))
                nc.scalar.activation(p, p, ACT.Ln, bias=1.0).then_inc(sem("log_ready"), 1)

            def suffix(hd):
                act.wait_ge(sem("stick_summed"), hd + 1)
                nc.scalar.activation(prob[:, hd % 2, 0:3 * P], masked[:, hd % 2, 0:3 * P], ACT.Exp) \
                    .then_inc(sem("exp_done"), 1)

            def gates_c():
                wait_evacuated(act, ("block", where["proj", 8]))
                nc.scalar.activation(gate_c[:, :, :, :].rearrange("p t h g -> p t (h g)"), proj[:, :, GC:GC + 12],
                                     ACT.Tanh, scale=0.5).then_inc(sem("gate_c_tanh"), 1)

            def cmp_hidden(i):
                act.wait_ge(sem("cmp_poly_ready"), i + 1)
                nc.scalar.activation(hid_t[:, i, 0:NC], hid_t[:, i, 0:NC], ACT.Tanh,
                                     scale=float(np.sqrt(2 / np.pi))).then_inc(sem("cmp_tanh_ready"), 1)

            def cmp_kv():
                ps = wait_filled(act, ("cmp_kv",))
                nc.scalar.copy(kc_t[:, :], ps[:, 0:NC])
                free(nc.scalar.copy(vc[:, :], ps[:, HD:2 * HD]), ("cmp_kv",))

            def cmp_scores():
                act.wait_ge(sem("cmp_shifted"), 1)
                s = cmp_s[:, :, :, :].rearrange("p t h n -> p (t h n)")
                nc.scalar.activation(s, s, ACT.Exp).then_inc(sem("cmp_exp_done"), 1)

            def turn_cmp_p():
                ps = wait_filled(act, ("turn_cmp_p",))
                free(nc.scalar.copy(cmp_in[:, 1, :], ps[:, 0:T]), ("turn_cmp_p",))

            def scores(u):
                kind, t, _ = UNITS[u]
                n, q = T if kind == "mem" else P * (t + 1), ORDER[u]
                act.wait_ge(sem("max_ready"), q - 3)
                if q < 6:
                    act.wait_ge(sem("pv_done"), q - 1)
                for m in range(2):
                    last = nc.scalar.activation(prob[:, q % 2, m * n:m * n + n], masked[:, q % 2, m * n:m * n + n],
                                                ACT.Exp, bias=neg_max[:, u, m:m + 1],
                                                accum_out=den[:, u, m:m + 1])
                last.then_inc(sem("exp_done"), 1)

            def turn_p(u):
                kind, t, _ = UNITS[u]
                n, q = 2 * P * (NT if kind == "mem" else t + 1), ORDER[u]
                ps = wait_filled(act, ("turn_p", u))
                act.wait_ge(sem("pv_done"), q - 1)
                free(nc.scalar.copy(prob_t[:, q % 2, 0:n], ps[:, 0:n]), ("turn_p", u))

            def turn_to(dst, key):
                ps = wait_filled(act, key)
                nc.scalar.copy(dst, ps[:, :].rearrange("p (m n) -> p m n", m=2)).then_inc(sem("turn_hi"), 1)

            def turn_o(c):
                turn_to(u_hi[:, 2 * (c % 3):2 * (c % 3) + 2, :], ("turn_o", c))

            def turn_mixed(c):
                turn_to(mixed_hi[:, 2 * c:2 * c + 2, :], ("turn_mixed", c))

            def merged():
                for c in range(4):
                    act.wait_ge(sem("merge_done"), c + 1)
                    nc.scalar.copy(merged_hi[:, 2 * c:2 * c + 2, :].rearrange("p m n -> p (m n)"),
                                   work[:, 512 * c:512 * c + 512]).then_inc(sem("merged_hi_ready"), 1)

            def gate_row(i):
                for half in range(2):
                    ps = wait_filled(act, ("gate_row", i, half))
                    free(nc.scalar.copy(row_bc[:, 512 * half:512 * half + 512], ps[:, :]), ("gate_row", i, half))

            def forget():
                act.wait_ge(sem("logit_ready"), 1)
                link(nc.scalar.activation(soft[:, :, :], logit[:, :, :], ACT.Abs))
                link(nc.scalar.activation(soft[:, :, :], soft[:, :, :], ACT.Exp, scale=-1.0))
                nc.scalar.activation(soft[:, :, :], soft[:, :, :], ACT.Ln, bias=1.0).then_inc(sem("soft_ready"), 1)

            def turn_fox(i):
                ps = wait_filled(act, ("turn_fox", i))
                free(nc.scalar.copy(fox_t[0:AUG, 2 * i:2 * i + 2, :],
                                    ps[0:AUG, :].rearrange("p (m n) -> p m n", m=2)), ("turn_fox", i))

            def turn_ret(i):
                ps = wait_filled(act, ("turn_ret", i))
                free(nc.scalar.copy(ret_t[:, 2 * i:2 * i + 2, :], ps[:, :].rearrange("p (m n) -> p m n", m=2)),
                     ("turn_ret", i))

            def mix(part):
                if part == 0:
                    wait_evacuated(act, ("block", where["proj2", 13]))
                    wait_evacuated(act, ("block", where["proj2", 14]))
                    src, dst = FOG, FOG
                else:
                    wait_evacuated(act, ("block", where["proj2", 15]))
                    wait_evacuated(act, ("block", where["proj2", 16]))
                    act.wait_ge(sem("pv_done"), 28)
                    src, dst = RG, FV
                nc.scalar.activation(proj2[:, :, dst:dst + 512], proj2[:, :, src:src + 512], ACT.Tanh, scale=0.5) \
                    .then_inc(sem("mix_tanh"), 1)

            run({"round": round_block, "evac": evac, "ssq": ssq, "turn": turn, "columns": columns,
                 "turn_qk": turn_qk, "stick": stick, "suffix": suffix, "gates_c": gates_c, "cmp_hidden": cmp_hidden,
                 "cmp_kv": cmp_kv, "cmp_scores": cmp_scores, "turn_cmp_p": turn_cmp_p, "scores": scores,
                 "turn_p": turn_p, "turn_o": turn_o, "turn_mixed": turn_mixed, "merged": merged,
                 "gate_row": gate_row, "forget": forget, "turn_fox": turn_fox, "turn_ret": turn_ret, "mix": mix})

        @block.gpsimd
        def _(pool):
            chain = [0]

            def link(ins):
                chain[0] += 1
                ins.then_inc(sem("pool_chain"), 1)
                pool.wait_ge(sem("pool_chain"), chain[0])

            def inverse_root(dst, src, mean_of, n, signal, count):
                link(nc.gpsimd.tensor_scalar(mean_eps[:, 0:n], src, 1.0 / mean_of, EPS, ALU.mult, ALU.add))
                nc.gpsimd.tensor_tensor(dst, mean_eps[:, 0:n], mhalf[:, 0:n], ALU.pow).then_inc(sem(signal), 1)
                pool.wait_ge(sem(signal), count)

            link(nc.gpsimd.memset(mhalf[:, :], -0.5))

            def rstd_of(n):
                pool.wait_ge(sem("squares_summed"), NT * (n + 1))
                inverse_root(rstd[:, n, :], square_sum[:, n, :], D, NT, "rstd_ready", n + 1)

            def head_stat(i):
                n = NT * (FH if i < 3 else RH)
                pool.wait_ge(sem("head_squares"), i + 1)
                inverse_root(fstat[:, i, 0:n], fstat[:, i, 0:n], HD if i < 3 else RD, n, "head_rstd", i + 1)

            run(dict(rstd=rstd_of, fox_square=head_stat, mix=lambda part: head_stat(2 + part)))

        @block.vector
        def _(dve):
            chain = [0]

            def link(ins):
                chain[0] += 1
                ins.then_inc(sem("dve_chain"), 1)
                dve.wait_ge(sem("dve_chain"), chain[0])

            tt, ts, stt = nc.vector.tensor_tensor, nc.vector.tensor_scalar, nc.vector.scalar_tensor_tensor

            def f32(ap):
                return ap.bitcast(F32)

            def over(ap, n):
                shape = list(ap.shape) + [n]
                return ap.unsqueeze(len(shape) - 1).broadcast_to(shape)

            def residue(s):
                x = raw[:, raw_at["split", s] % RAW, :]
                n = KD * width(s) if width(s) != 256 else BLOCK
                dve.wait_ge(sem("hi_ready"), s + 1)
                tt(lo[:, s % SPLIT, 0:n], x[:, 0:n], f32(hi[:, s % SPLIT, 0:n]), ALU.subtract) \
                    .then_inc(sem("lo_ready"), 1)

            def evac(s):
                kind, j = blocks[s][0], blocks[s][-1]
                if kind in ("ffn_in", "mlp_in"):
                    dve.wait_ge(sem("hidden_ready"), j if kind == "ffn_in" else 22 + j)
                if kind == "ffn_in":
                    dve.wait_ge(sem("silu_ready"), j + 1)
                    ps = banks[lease["block", s][0]]
                    x = hid[:, 0:T]
                    free(tt(x, act_out[:, j % 2, 0:T], ps[:, T:2 * T], ALU.mult), ("block", s))
                    wait_evacuated(dve, ("block", s))
                    dst_hi, dst_lo = hid_hi[:, j % 4, :], hid_lo[:, j % 4, :]
                    if j >= 4:
                        wait_used(dve, where["ffn_out", (j - 4) // 2])
                elif kind == "mlp_in":
                    wait_evacuated(dve, ("block", s))
                    x = hid[:, :]
                    link(tt(x, act_out[:, j % 2, :], act_out[:, j % 2, :], ALU.mult))
                    two = slice(2 * (j % 2), 2 * (j % 2) + 2)
                    dst_hi = hid_hi[:, two, :].rearrange("p m n -> p (m n)")
                    dst_lo = hid_lo[:, two, :].rearrange("p m n -> p (m n)")
                    if j >= 2:
                        wait_used(dve, where["mlp_out", j - 2])
                else:
                    return
                link(nc.vector.tensor_copy(dst_hi, x))
                tt(dst_lo, x, f32(dst_hi), ALU.subtract).then_inc(sem("hidden_ready"), 1)

            def xhat(n, t):
                dve.wait_ge(sem("rstd_ready"), n + 1)
                src = mem_rows if n == 1 else h
                ts(norm_rows[:, t, :], src[:, t, :], rstd[:, n, t:t + 1], None, ALU.mult) \
                    .then_inc(sem("xhat_ready"), 1)

            turned = [0]

            def wait_turn_hi(key):
                turned[0] += 1
                dve.wait_ge(sem("turn_hi"), turned[0])
                return banks[lease[key][0]]

            def turn(n, c):
                key = ("turn", n, c)
                ps = wait_turn_hi(key)
                up, dst = (mem_t_hi, mem_t_lo) if n == 1 else (u_hi, u_lo)
                for m in range(2):
                    k, x = 2 * c + m, ps[:, m * T:m * T + T]
                    if n >= 5:
                        shift = mod[:, 24 * (n - 5) + k:24 * (n - 5) + k + 1]
                        link(ts(masked[:, m, 0:T], x, scale1[:, n - 5, k:k + 1], shift, ALU.mult, ALU.add))
                        last = tt(dst[:, k, :], masked[:, m, 0:T], f32(up[:, k, :]), ALU.subtract)
                    else:
                        g = ROW_AT[GAIN[n]] + k
                        last = stt(dst[:, k, :], x, cols[:, g:g + 1], f32(up[:, k, :]), ALU.mult, ALU.subtract)
                free(last, key)

            def turn_to(up, dst, key):
                ps = wait_turn_hi(key)
                free(tt(dst, ps[:, :].rearrange("p (m n) -> p m n", m=2), f32(up), ALU.subtract), key)

            def turn_o(c):
                two = slice(2 * (c % 3), 2 * (c % 3) + 2)
                turn_to(u_hi[:, two, :], u_lo[:, two, :], ("turn_o", c))

            def turn_mixed(c):
                two = slice(2 * c, 2 * c + 2)
                turn_to(mixed_hi[:, two, :], mixed_lo[:, two, :], ("turn_mixed", c))

            def columns():
                dve.wait_ge(sem("c_tanh_ready"), 1)
                c = cols[:, ROW_AT["c"]:ROW_AT["c"] + KD]
                link(stt(c_act[:, :], c_tanh[:, :], 1.0, c, ALU.add, ALU.mult))
                link(ts(c_act[:, :], c_act[:, :], 0.5, None, ALU.mult))

            def rope(x, a, b, cos, sin, nsin):
                shape = list(x.shape)
                half = [shape[0], shape[1], shape[3]]
                tt(a, x, cos.unsqueeze(1).unsqueeze(1).broadcast_to(shape), ALU.mult)
                tt(b[:, :, 0, :], x[:, :, 1, :], nsin.unsqueeze(1).broadcast_to(half), ALU.mult)
                link(tt(b[:, :, 1, :], x[:, :, 0, :], sin.unsqueeze(1).broadcast_to(half), ALU.mult))
                return tt(x, a, b, ALU.add)

            def rope1(g):
                c0, heads, last_block = ((QB, 5, 4), (QI, 5, 5), (QC, 5, 7), (KSEL, 2, 8))[g]
                wait_evacuated(dve, ("block", where["proj", last_block]))
                if g == 1:
                    wait_evacuated(dve, ("turn", 1, KD // 2 - 1))
                for t in range(NT):
                    if g == 3:
                        x = proj[:, t, KSEL:KSEL + 4 * HD].rearrange("p (h r) -> p h r", h=2)[:, :, 0:HD]
                    else:
                        x = proj[:, t, c0:c0 + heads * HD].rearrange("p (h c) -> p h c", h=heads)
                    x = x.rearrange("p h (a c) -> p h a c", a=2)
                    a, b = (work[:, at:at + heads * HD].rearrange("p (h a c) -> p h a c", h=heads, a=2)
                            for at in (0, 512))
                    cs, sn, ns = (cst(w)[:, 32 * t:32 * t + 32] for w in ("cos1", "sin1", "nsin1"))
                    last = rope(x, a, b, cs, sn, ns)
                    if t == 0:
                        link(last)
                last.then_inc(sem("rope_done"), 1)
                dve.wait_ge(sem("rope_done"), (1, 0, 2, 3)[g] + 1)

            def stick(hd):
                b = hd % 2
                ps = wait_filled(dve, ("stick", hd))
                if hd >= 2:
                    dve.wait_ge(sem("exp_done"), hd - 1)
                z = masked[:, b, 0:3 * P]
                free(stt(z, ps[:, 0:3 * P], SCALE, cst("strict"), ALU.mult, ALU.add), ("stick", hd))
                wait_evacuated(dve, ("stick", hd))
                nc.vector.engine_nop().then_inc(sem("stick_masked"), 1)
                dve.wait_ge(sem("log_ready"), hd + 1)
                stt(prob_t[:, b, 0:3 * P], z, 0.0, prob[:, b, 0:3 * P], ALU.max, ALU.add) \
                    .then_inc(sem("softplus_ready"), 1)

            def suffix(hd):
                b = hd % 2
                ps = wait_filled(dve, ("suffix", hd))
                z = masked[:, b, 0:3 * P]
                stt(z, ps[:, 0:3 * P], -1.0, z, ALU.mult, ALU.add).then_inc(sem("stick_summed"), 1)
                dve.wait_ge(sem("stick_summed"), hd + 1)
                free(nc.vector.engine_nop(), ("suffix", hd))

            def index(t):
                n = P * (t + 1)
                if t == 0:
                    link(ts(idx_w[:, :, :], proj[:, :, WI:WI + 4], 1.0 / 16, None, ALU.mult))
                score, x = sel_neg[:, t, 0:n], spare[:, 0:n]
                mask = cst("causal")[:, 2 * P - n:2 * P] if t == 0 else cst("causal")
                for i in range(2):
                    ps = wait_filled(dve, ("index", t, i))
                    for m in range(2):
                        hd = i + 2 * m
                        ins = ts(x, ps[:, m * n:m * n + n], 0.0, idx_w[:, t, hd:hd + 1], ALU.max, ALU.mult)
                        if m:
                            free(ins, ("index", t, i))
                            wait_evacuated(dve, ("index", t, i))
                        else:
                            link(ins)
                        link(tt(score, x, mask if hd == 0 else score, ALU.add))

            def topk(t, part):
                n = P * (t + 1)
                score = sel_neg[:, t, 0:n]
                for _ in range(TOPK // 16):
                    link(nc.vector.max(best[:, :], score))
                    link(nc.vector.match_replace(score, best[:, :], score, TAKEN))
                if part:
                    mask = cst("causal")[:, 2 * P - n:2 * P] if t == 0 else cst("causal")
                    link(ts(score, score, 2 * NEG, NEG, ALU.is_gt, ALU.mult))
                    link(tt(score, score, mask, ALU.add))

            def turn_cmp(i):
                key = ("turn_cmp", i)
                ps = wait_filled(dve, key)
                x = cmp_in[:, i, :].rearrange("p (k n) -> p k n", k=16)
                src = ps[0:HD, 0:T].rearrange("p (n k e) -> p e k n", n=16, k=8)
                for e in range(2):
                    r = slice(HD * e, HD * e + HD)
                    nc.vector.tensor_copy(x[r, 0:8, 0:NC], src[:, e, :, 0:NC])
                    last = nc.vector.tensor_copy(x[r, 8:16, 0:NC], src[:, e, :, 1:NC + 1])
                free(last, key)
                c = ROW_AT["pos_v" if i else "pos_k"]
                nc.vector.tensor_copy(x[:, :, NC], cols[:, c:c + 16]).then_inc(sem("cmp_in_ready"), 1)

            def cmp_hidden(i):
                key = ("cmp_hidden", i)
                ps = wait_filled(dve, key)
                x, y = hid_x[:, i, :], hid_t[:, i, 0:NC]
                free(nc.vector.tensor_copy(x, ps[:, 0:16]), key)
                wait_evacuated(dve, key)
                link(ts(x[:, 0:NC], x[:, 0:NC], x[:, NC:NC + 1], None, ALU.add))
                link(tt(y, x[:, 0:NC], x[:, 0:NC], ALU.mult))
                link(ts(y, y, 0.044715, 1.0, ALU.mult, ALU.add))
                tt(y, y, x[:, 0:NC], ALU.mult).then_inc(sem("cmp_poly_ready"), 1)

            def cmp_kv():
                link(nc.vector.memset(hid_v[:, :, :], 0.0))
                dve.wait_ge(sem("cmp_tanh_ready"), 2)
                link(stt(hid_t[:, :, 0:NC], hid_t[:, :, 0:NC], 1.0, hid_x[:, :, 0:NC], ALU.add, ALU.mult))
                ts(hid_k[:, :], hid_t[:, 0, 0:NC], 0.5, None, ALU.mult)
                ts(hid_v[:, :, 0:NC], hid_t[:, 1, 0:NC].unsqueeze(1).broadcast_to([P, 4, NC]), 0.5, None,
                   ALU.mult).then_inc(sem("cmp_hid_ready"), 1)

            def cmp_scores():
                key = ("cmp_scores",)
                ps = wait_filled(dve, key)
                src = ps[:, 0:8 * 16].rearrange("p (t h n) -> p t h n", t=NT, h=4)
                for t in range(NT):
                    mask = cst("cmpneg")[:, t * NC:t * NC + NC].unsqueeze(1).broadcast_to([P, 4, NC])
                    last = stt(cmp_s[:, t, :, :], src[:, t, :, 0:NC], SCALE, mask, ALU.mult, ALU.add)
                free(last, key)
                wait_evacuated(dve, key)
                s = cmp_s[:, :, :, :].rearrange("p t h n -> p (t h) n")
                link(nc.vector.tensor_reduce(cmp_m[:, :], s, X, ALU.max))
                tt(s, s, over(cmp_m[:, :], NC), ALU.subtract).then_inc(sem("cmp_shifted"), 1)

            def gates_c_():
                dve.wait_ge(sem("gate_c_tanh"), 1)
                g = gate_c[:, :, :, :].rearrange("p t h g -> p (t h g)")
                link(ts(g, g, 0.25, 0.25, ALU.mult, ALU.add))

            def turn_cmp_p():
                p = cmp_in[:, 0, :]
                link(nc.vector.memset(p, 0.0))
                dve.wait_ge(sem("cmp_exp_done"), 1)
                for t in range(NT):
                    mask = cst("cmp01")[:, t * NC:t * NC + NC].unsqueeze(1).broadcast_to([P, 4, NC])
                    dst = p[:, t * P:t * P + P].rearrange("p (h n) -> p h n", h=4)[:, :, 0:NC]
                    last = tt(dst, cmp_s[:, t, :, :], mask, ALU.mult)
                last.then_inc(sem("cmp_p_ready"), 1)
                dve.wait_ge(sem("cmp_p_ready"), 1)
                link(nc.vector.tensor_reduce(cmp_d[:, :], p.rearrange("p (h n) -> p h n", n=32), X, ALU.add))
                link(ts(cmp_d[:, :], cmp_d[:, :], 1e-30, None, ALU.max))
                link(nc.vector.reciprocal(cmp_d[:, :], cmp_d[:, :]))
                link(tt(cmp_d[:, :], cmp_d[:, :], gate_c[:, :, :, 0].rearrange("p t h -> p (t h)"), ALU.mult))

            def scores(u):
                kind, t, _ = UNITS[u]
                n, q = T if kind == "mem" else P * (t + 1), ORDER[u]
                key = ("scores", u)
                ps = wait_filled(dve, key)
                dve.wait_ge(sem("exp_done"), q - 1)
                dst = masked[:, q % 2, 0:2 * n].rearrange("p (s n) -> p s n", s=2)
                src = ps[:, 0:2 * n].rearrange("p (s n) -> p s n", s=2)
                if kind == "mem":
                    free(ts(dst, src, SCALE, None, ALU.mult), key)
                else:
                    mask = sel_neg[:, t, 0:n] if kind == "b" else cst("causal")[:, 2 * P - n:2 * P]
                    free(stt(dst, src, 1.0 if kind == "fox" else SCALE, mask.unsqueeze(1).broadcast_to([P, 2, n]),
                             ALU.mult, ALU.add), key)
                wait_evacuated(dve, key)
                nc.vector.tensor_reduce(neg_max[:, u, :], dst, X, ALU.max, negate=True) \
                    .then_inc(sem("max_ready"), 1)

            def inverse_den(u0, n):
                d = den[:, u0:u0 + n, :].rearrange("p u s -> p (u s)")
                r = rden[:, u0:u0 + n, :].rearrange("p u s -> p (u s)")
                link(nc.vector.reciprocal(r, d))
                return r

            def o_group(g):
                key = ("o", g)
                if g == 1:
                    ps = wait_filled(dve, key)
                    for t in range(NT):
                        last = tt(o_rows[:, t, 512:768].rearrange("p (h c) -> p h c", h=4),
                                  ps[:, t * 256:t * 256 + 256].rearrange("p (h c) -> p h c", h=4),
                                  over(cmp_d[:, 4 * t:4 * t + 4], HD), ALU.mult)
                    free(last, key)
                    return
                done = {0: 4, 3: 8, 4: 12, 2: 16, 5: 20, 6: 24, 7: 28, 8: 32}[g]
                dve.wait_ge(sem("pv_done"), done)
                if g in (0, 2, 5, 8):
                    ps = banks[O_BANK[g]]
                if g == 0:
                    free(ts(o_rows[:, :, 0:256], ps[:, :].rearrange("p (t c) -> p t c", t=NT), 0.5, None, ALU.mult),
                         key)
                elif g in (3, 4):
                    t = g - 3
                    r = inverse_den(4 + 4 * t, 4)
                    link(tt(rden[:, 4 + 4 * t:8 + 4 * t, :], rden[:, 4 + 4 * t:8 + 4 * t, :],
                            gate_c[:, t, :, 1:3], ALU.mult))
                    x = spare.rearrange("p (m c) -> p m c", c=HD)
                    free(tt(x, banks[O_BANK[g]][:, :].rearrange("p (m c) -> p m c", c=HD), over(r, HD), ALU.mult),
                         key)
                    wait_evacuated(dve, key)
                    x = spare.rearrange("p (h s c) -> p h s c", h=4, s=2)
                    dst = o_rows[:, t, 512:768].rearrange("p (h c) -> p h c", h=4)
                    link(tt(dst, dst, x[:, :, 0, :], ALU.add))
                    tt(dst, dst, x[:, :, 1, :], ALU.add).then_inc(sem("branch_c_done"), 1)
                    dve.wait_ge(sem("branch_c_done"), t + 1)
                elif g in (2, 5):
                    r = inverse_den(0 if g == 2 else 12, 4)
                    if g == 2:
                        link(ts(r, r, 0.5, None, ALU.mult))
                    for t in range(NT):
                        dst = o_rows[:, t, 256:512] if g == 2 else o_mem[:, t, :]
                        last = tt(dst.rearrange("p (m i c) -> p i m c", m=2, i=2),
                                  ps[:, t * 256:t * 256 + 256].rearrange("p (i m c) -> p i m c", i=2, m=2),
                                  over(r[:, 4 * t:4 * t + 4].rearrange("p (i m) -> p i m", i=2), HD), ALU.mult)
                    free(last, key)
                elif g in (6, 7):
                    t = g - 6
                    if t == 0:
                        wait_evacuated(dve, ("gate_row", 0, 1))
                    r = inverse_den(16 + 4 * t, 4)
                    free(tt(norm_rows[:, t, 0:512].rearrange("p (m c) -> p m c", c=HD),
                            banks[O_BANK[g]][:, :].rearrange("p (m c) -> p m c", c=HD), over(r, HD), ALU.mult), key)
                else:
                    for t in range(NT):
                        free(nc.vector.tensor_copy(norm_rows[:, t, 512:1024], banks[O_BANK[8 + t]][:, :]),
                             ("o", 8 + t))

            def merge(j):
                for c in range(4):
                    key = ("up", j, c)
                    ps = wait_filled(dve, key)
                    g = gates[:, 8 * j + 2 * c:8 * j + 2 * c + 2, :].rearrange("p m n -> p (m n)")
                    dst = work[:, 512 * c:512 * c + 512]
                    x = dst if j == 0 else masked[:, c % 2, :]
                    if j == 0 and c == 0:
                        for i in range(3):
                            wait_evacuated(dve, ("turn_o", i))
                    free(stt(x, g, 1.0, ps[:, :], ALU.add, ALU.mult), key)
                    if j:
                        wait_evacuated(dve, key)
                        ins = tt(dst, dst, x, ALU.add)
                        if j == 2:
                            ins.then_inc(sem("merge_done"), 1)
                        else:
                            link(ins)
                    elif c == 3:
                        wait_evacuated(dve, key)

            def merged():
                for c in range(4):
                    dve.wait_ge(sem("merged_hi_ready"), c + 1)
                    two = slice(2 * c, 2 * c + 2)
                    tt(merged_lo[:, two, :].rearrange("p m n -> p (m n)"), work[:, 512 * c:512 * c + 512],
                       f32(merged_hi[:, two, :].rearrange("p m n -> p (m n)")), ALU.subtract) \
                        .then_inc(sem("merged_split"), 1)

            def residual(i):
                group = ("out", "mem_o", "ffn_out", "out2", "mlp_out")[i]
                for t in range(NT):
                    for half in range(2):
                        key = (group, t, half)
                        ps = wait_filled(dve, key)
                        n = slice(512 * half, 512 * half + 512)
                        if i < 3:
                            free(tt(h[:, t, n], h[:, t, n], ps[:, :], ALU.add), key)
                            continue
                        wait_evacuated(dve, ("gate_row", i - 3, half))
                        x = masked[:, half, :]
                        free(tt(x, row_bc[:, n], ps[:, :], ALU.mult), key)
                        wait_evacuated(dve, key)
                        tt(h[:, t, n], h[:, t, n], x, ALU.add).then_inc(sem("gated"), 1)

            def final_norm():
                dve.wait_ge(sem("rstd_ready"), 5)
                dve.wait_ge(sem("row_loaded"), 16)
                for t in range(NT):
                    stt(h[:, t, :], h[:, t, :], rstd[:, 4, t:t + 1], row_bc[:, :], ALU.mult, ALU.mult) \
                        .then_inc(sem("final_done"), 1)

            def ada(j):
                x = shaped(raw_ready(dve, ("ada", j)), ("ada", j))
                acc = ada_acc[:, j % 2, :]
                if j >= 2:
                    wait_filled(dve, ("ada_sum", j - 2))
                link(ts(acc, x[:, 0, :], c_act[:, 0:1], None, ALU.mult))
                for k in range(1, KD):
                    ins = stt(acc, x[:, k, :], c_act[:, k:k + 1], acc, ALU.mult, ALU.add)
                    if k < KD - 1:
                        link(ins)
                ins.then_inc(sem("ada_ready"), 1)

            def ada_sum(j):
                key = ("ada_sum", j)
                ps = wait_filled(dve, key)
                c = ROW_AT["b_ada"] + 2 * j
                free(tt(mod[:, 2 * j:2 * j + 2], ps[:, 0:2], cols[:, c:c + 2], ALU.add), key)

            def modulation(i):
                wait_evacuated(dve, ("ada_sum", 7 if i == 0 else 23))
                ts(scale1[:, i, :], mod[:, 24 * i + 8:24 * i + 16], 1.0, None, ALU.add).then_inc(sem("mod_ready"), 1)
                dve.wait_ge(sem("mod_ready"), i + 1)

            def gate_row(i):
                if i == 0:
                    wait_evacuated(dve, ("ada_sum", 9 + 2))
                    for c in range(8):
                        wait_evacuated(dve, ("turn_fox", c))
                for k in range(KD):
                    g = 16 + 24 * i + k
                    last = ts(work[:, k * P:k * P + P], ident, mod[:, g:g + 1], None, ALU.mult)
                last.then_inc(sem("diag_ready"), 1)

            def squares(x, dst, n, i, last=True):
                b = squares.turn = squares.turn ^ 1
                link(tt(masked[:, b, :], x, x, ALU.mult))
                ins = nc.vector.tensor_reduce(dst, masked[:, b, :].rearrange("p (h c) -> p h c", c=n), X, ALU.add)
                if last:
                    ins.then_inc(sem("head_squares"), 1)

            squares.turn = 0

            def fox_square(s):
                wait_evacuated(dve, ("block", where["proj2", 2 * s]))
                wait_evacuated(dve, ("block", where["proj2", 2 * s + 1]))
                for t in range(NT):
                    squares(proj2[:, t, (FQ, FK)[s]:(FQ, FK)[s] + 512], fstat[:, s, FH * t:FH * t + FH], HD, s, t == 1)

            def fox_norm(s):
                dve.wait_ge(sem("head_rstd"), s + 1)
                dve.wait_ge(sem("gains_loaded"), 16 * 5)
                if s == 0:
                    link(ts(gain_q, gain_q, SCALE, None, ALU.mult))
                gain = (gain_q, gain_k)[s].unsqueeze(1).broadcast_to([P, FH, HD])
                for t in range(NT):
                    x = proj2[:, t, (FQ, FK)[s]:(FQ, FK)[s] + 512].rearrange("p (h c) -> p h c", c=HD)
                    dst = aug[:, t, s, :, 0:HD]
                    link(tt(dst, x, over(fstat[:, s, FH * t:FH * t + FH], HD), ALU.mult))
                    last = tt(dst, dst, gain, ALU.mult)
                last.then_inc(sem("aug_ready"), 1)

            def forget():
                wait_evacuated(dve, ("block", where["proj2", 4]))
                dve.wait_ge(sem("gains_loaded"), 16 * 5)
                tt(logit[:, :, :], proj2[:, :, FF:FF + FH], b_forget.unsqueeze(1).broadcast_to([P, NT, FH]),
                   ALU.add).then_inc(sem("logit_ready"), 1)
                dve.wait_ge(sem("logit_ready"), 1)

            def forget_sum():
                dve.wait_ge(sem("soft_ready"), 1)
                stt(soft[:, :, :], logit[:, :, :], 0.0, soft[:, :, :], ALU.min, ALU.subtract) \
                    .then_inc(sem("log_f_ready"), 1)
                nc.vector.memset(aug[:, :, 0, :, HD], 1.0)
                nc.vector.memset(aug[:, :, 1, :, HD + 1], 1.0)
                key = ("forget_sum",)
                ps = wait_filled(dve, key)
                x = ps[:, 0:NT * FH].rearrange("p (t h) -> p t h", t=NT)
                nc.vector.tensor_copy(aug[:, :, 0, :, HD + 1], x)
                free(ts(aug[:, :, 1, :, HD], x, -1.0, None, ALU.mult), key)
                wait_evacuated(dve, key)
                nc.vector.engine_nop().then_inc(sem("aug_ready"), 1)

            def rope2(s):
                wait_evacuated(dve, ("block", where["proj2", 5 + 2 * s]))
                wait_evacuated(dve, ("block", where["proj2", 6 + 2 * s]))
                for t in range(NT):
                    x = proj2[:, t, (RQ, RK)[s]:(RQ, RK)[s] + 512].rearrange("p (h a c) -> p h a c", h=RH, a=2)
                    a, b = (masked[:, i, :].rearrange("p (h a c) -> p h a c", h=RH, a=2) for i in range(2))
                    cs, sn, ns = (cst(w)[:, 64 * t:64 * t + 64] for w in ("cos2", "sin2", "nsin2"))
                    last = rope(x, a, b, cs, sn, ns)
                    if t == 0:
                        link(last)
                last.then_inc(sem("rope2_done"), 1)
                dve.wait_ge(sem("rope2_done"), s + 1)

            def ret_scores(hd):
                key = ("ret_scores", hd)
                ps = wait_filled(dve, key)
                dve.wait_ge(sem("pv_done"), 28 + hd - 1)
                dve.wait_ge(sem("decays_loaded"), 16)
                decay = decays[:, hd * 2 * P:(hd + 1) * 2 * P]
                p = prob[:, hd % 2, :]
                tt(p[:, 0:T], ps[:, 0:T], decay, ALU.mult)
                free(tt(p[:, T:T + P], ps[:, T:T + P], decay[:, 0:P], ALU.mult), key)

            def mix(part):
                n, heads = (HD, FH) if part == 0 else (RD, RH)
                if part == 0:
                    wait_evacuated(dve, ("o", 9))
                rows_ = [norm_rows[:, t, 512 * part:512 * part + 512] for t in range(NT)]
                for t in range(NT):
                    squares(rows_[t], fstat[:, 2 + part, heads * t:heads * t + heads], n, 2 + part, t == 1)
                dve.wait_ge(sem("head_rstd"), 3 + part)
                for t in range(NT):
                    x = rows_[t]
                    heads_x = x.rearrange("p (h c) -> p h c", c=n)
                    link(tt(heads_x, heads_x, over(fstat[:, 2 + part, heads * t:heads * t + heads], n), ALU.mult))
                    link(stt(x, x, 0.5, out_gain[:, 512 * part:512 * part + 512], ALU.mult, ALU.mult))
                dve.wait_ge(sem("mix_tanh"), 1 + part)
                for t in range(NT):
                    th = proj2[:, t, (FOG, FV)[part]:(FOG, FV)[part] + 512]
                    if part:
                        link(stt(th, th, 1.0, proj2[:, t, RG:RG + 512], ALU.add, ALU.mult))
                        last = tt(rows_[t], rows_[t], th, ALU.mult)
                    else:
                        last = stt(rows_[t], th, 1.0, rows_[t], ALU.add, ALU.mult)
                last.then_inc(sem("mix_done"), 1)

            run({"residue": residue, "evac": evac, "xhat": xhat, "turn": turn, "turn_o": turn_o,
                 "turn_mixed": turn_mixed, "columns": columns, "rope1": rope1, "stick": stick, "suffix": suffix,
                 "index": index, "topk": topk, "turn_cmp": turn_cmp, "cmp_hidden": cmp_hidden, "cmp_kv": cmp_kv,
                 "cmp_scores": cmp_scores, "gates_c": gates_c_, "turn_cmp_p": turn_cmp_p, "scores": scores,
                 "o_group": o_group, "merge": merge, "merged": merged, "residual": residual,
                 "final_norm": final_norm, "ada": ada, "ada_sum": ada_sum, "mod": modulation, "gate_row": gate_row,
                 "fox_square": fox_square, "fox_norm": fox_norm, "forget": forget, "forget_sum": forget_sum,
                 "rope2": rope2, "ret_scores": ret_scores, "mix": mix})

        @block.sync
        def _(sp):
            def load(dst, src, signal):
                sp.dma_start(dst, src).then_inc(sem(signal) if isinstance(signal, str) else signal, 16)

            load(h[:, :, :], d["x"][0].rearrange("(t p) c -> p t c", p=P), "x_loaded")
            load(const[:, :], consts_dram[:, 0:DECAY_AT], "const_loaded")
            row_source = dict(
                norm_mix=d["norm_mix"], norm_mem_kv=d["norm_mem_kv"], norm_mem_q=d["norm_mem_q"],
                norm_ffn=d["norm_ffn"], c=d["c_2"], b_ada=d["b_ada_2"])
            for name, at in ROW_AT.items():
                if name in row_source:
                    src = row_source[name].rearrange("l (k p) -> (l k) p", p=P)
                else:
                    src = d["cmp_" + name][0].rearrange("(k e) c -> k (e c)", e=2)
                load(rows[at:at + src.shape[0], :], src, "rows_loaded")
            for i, what in enumerate(raw_order):
                if i >= RAW:
                    before = raw_order[i - RAW]
                    if before[0] == "split":
                        sp.wait_ge(sem("lo_ready"), before[1] + 1)
                    elif before[0] == "ada":
                        sp.wait_ge(sem("ada_ready"), before[1] + 1)
                    else:
                        wait_filled(sp, ("cmp_hidden", before[1]))
                b = blocks[what[1]] if what[0] == "split" else what
                n = KD * width(what[1]) if what[0] == "split" else BLOCK
                load(raw[:, i % RAW, 0:n], stream[i, :, 0:n], raw_loaded[i % RAW])
                if i == 1:
                    load(mem_rows[:, :, :], d["mem"][0].rearrange("(t p) c -> p t c", p=P), "mem_loaded")
                if i == 5:
                    for m in range(2):
                        load(w2k[:, m, :], d["cmp_w2_k"][0], "w2_loaded")
                    load(w2v[:, :], d["cmp_w2_v"][0], "w2_loaded")
                    wait_evacuated(sp, ("columns",))
                    load(row_bc[:, :], d["norm_final"].rearrange("(a c) -> a c", a=1)[0].partition_broadcast(P),
                         "row_loaded")
                if b == ("ffn_in", 3):
                    sp.wait_ge(sem("hidden_ready"), 1)
                    for dst, src in ((gain_q, d["q_norm_gain_2"][0]), (gain_k, d["k_norm_gain_2"][0]),
                                     (b_forget, d["b_forget_2"][0]),
                                     (out_gain[:, 0:512], d["fox_out_gain_2"][0].rearrange("h c -> (h c)")),
                                     (out_gain[:, 512:1024], d["ret_out_gain_2"][0].rearrange("h c -> (h c)"))):
                        load(dst, src.partition_broadcast(P), "gains_loaded")
                    load(decays[:, :], consts_dram[:, DECAY_AT:CONSTS], "decays_loaded")
            sp.wait_ge(sem("gated"), 8)
            load(out_dram[0].rearrange("(t p) c -> p t c", p=P), h[:, :, :], "stored")
            sp.wait_ge(sem("stored"), 16)


def kernel(**inputs):
    import concourse.bacc as bacc
    from concourse.bass_utils import run_bass_kernel_spmd

    nc = bacc.Bacc("TRN2", target_bir_lowering=False, num_devices=1)
    arrays, d = {}, {}
    for name in SMALL:
        a = np.ascontiguousarray(inputs[name])
        arrays[f"in_{name}"] = a
        d[name] = nc.dram_tensor(f"in_{name}", a.shape, mybir.dt.from_np(a.dtype), kind="ExternalInput").ap()
    arrays["in_stream"] = weight_stream(inputs)
    stream = nc.dram_tensor("in_stream", arrays["in_stream"].shape, F32, kind="ExternalInput").ap()
    arrays["in_constants"] = constants()
    consts_dram = nc.dram_tensor("in_constants", (P, CONSTS), F32, kind="ExternalInput").ap()
    out = nc.dram_tensor("out", (1, T, D), F32, kind="ExternalOutput").ap()
    two_blocks_kernel(nc, d, stream, consts_dram, out)
    r = run_bass_kernel_spmd(nc, [arrays], core_ids=[0])
    return r.results[0]["out"]
```

```python
from contextlib import ExitStack

import numpy as np

import concourse.bass as bass
from concourse import mybir

F32 = mybir.dt.float32
F32R = mybir.dt.float32r
ALU = mybir.AluOpType
ACT = mybir.ActivationFunctionType
X = mybir.AxisListType.X

P = 128
T = 256
NT = T // P
D = 1024
KD = D // P
HD = 64
SCALE = HD ** -0.5
EPS = 1e-6
ROOT_D = float(np.sqrt(D))
NEG = -1e30
TAKEN = -3e30
TOPK = min(256, T // 4)
CMP_LEN, CMP_STRIDE, CMP_HIDDEN = 32, 16, 128
NC = (T - CMP_LEN) // CMP_STRIDE + 1
W_COLS = 256
ROWS = 256
BLOCK = KD * W_COLS
RAW, SPLIT = 4, 3
D_FF = 2816
D_FF2 = 4096
FH, RH, RD = 8, 4, 128
AUG = HD + 2

QA, KA, VA, QB, KB, VB, QI, KI, WI, QC, KCMP, VCMP, KSEL, VSEL, KWIN, VWIN, GC, GM = np.cumsum(
    [0, 256, 256, 256, 256, 64, 64, 256, 64, 4, 256, 64, 64, 64, 64, 64, 64, 12]).tolist()
PROJ = GM
FQ, FK, FV, FOG, FF, RQ, RK, RV, RG = np.cumsum([0, 512, 512, 512, 512, 8, 512, 512, 512]).tolist()
PROJ2 = RG + 512

CONST_WIDTHS = dict(ident=P, suffix=P, prefix=P, ones=P, causal=2 * P, strict=3 * P, cos1=64, sin1=64, nsin1=64,
                    cos2=128, sin2=128, nsin2=128, cmpneg=2 * NC, cmp01=2 * NC, decay=RH * 2 * P)
CONST_AT = dict(zip(CONST_WIDTHS, np.cumsum([0] + list(CONST_WIDTHS.values())).tolist()))
CONSTS = sum(CONST_WIDTHS.values())
DECAY_AT = CONST_AT["decay"]

ROW_AT = dict(norm_mix=0, norm_mem_kv=8, norm_mem_q=16, norm_ffn=24, c=32, b_ada=40, pos_k=88, pos_v=104)
NROWS = 120


def constants():
    f = np.float32
    i, j = np.arange(P)[:, None], np.arange(P)[None, :]
    out = np.zeros((P, CONSTS), f)

    def put(name, a):
        out[:, CONST_AT[name]:CONST_AT[name] + CONST_WIDTHS[name]] = np.asarray(a, f).reshape(P, -1)

    put("ident", i == j)
    put("suffix", i >= j)
    put("prefix", i <= j)
    put("ones", np.ones((P, P)))
    put("causal", np.concatenate([np.zeros((P, P)), np.where(j <= i, 0, NEG)], 1))
    below = np.where(i < j, 0, NEG)
    put("strict", np.concatenate([below, np.zeros((P, P)), below], 1))
    for n, hd in (("1", HD), ("2", RD)):
        inv = f(10000.0) ** (-np.arange(0, hd, 2, dtype=f) / f(hd))
        ang = np.arange(T, dtype=f)[:, None] * inv[None, :]
        for name, a in (("cos", np.cos(ang)), ("sin", np.sin(ang)), ("nsin", -np.sin(ang))):
            put(name + n, a.reshape(NT, P, hd // 2).transpose(1, 0, 2))
    log_g = np.log(1.0 - 2.0 ** (-5.0 - np.arange(RH)))
    decay = [np.concatenate([np.where(j >= i, np.exp(np.maximum(j - i, 0) * g), 0), np.exp((j + P - i) * g)], 1)
             for g in log_g]
    put("decay", np.concatenate(decay, 1) * RD ** -0.5)
    seen = np.concatenate([(np.arange(NC)[None, :] * CMP_STRIDE + CMP_LEN - 1 <= i + t * P) for t in range(NT)], 1)
    put("cmpneg", np.where(seen, 0, NEG))
    put("cmp01", seen)
    return out



def plan():
    blocks = [("proj", j) for j in range(9)] + [("gate", j) for j in range(12)]
    blocks += [("up", j) for j in range(3)] + [("out", j) for j in range(4)]
    blocks += [("mem_k",), ("mem_q",), ("mem_v",), ("mem_o",), ("ffn_in", 0), ("ffn_in", 1)]
    for i in range(1, 11):
        blocks += [("ffn_in", 2 * i), ("ffn_in", 2 * i + 1), ("ffn_out", i - 1)]
    blocks += [("ffn_out", 10)]
    blocks += [("proj2", j) for j in range(17)] + [("out2", j) for j in (2, 3, 0, 1)]
    blocks += [("mlp_in", 0)]
    for i in range(1, 16):
        blocks += [("mlp_in", i), ("mlp_out", i - 1)]
    blocks += [("mlp_out", 15)]
    where = {b: s for s, b in enumerate(blocks)}
    table, raw, split_to = [], [], [0]

    def add(*step):
        table.append(step)

    def split(upto):
        while split_to[0] <= min(upto, len(blocks) - 1):
            s = split_to[0]
            add("round", s)
            add("residue", s)
            raw.append(("split", s))
            split_to[0] += 1

    def block(*b, evac=True, ahead=True):
        s = where[b]
        split(s)
        add("block", s)
        if ahead:
            split(s + 2)
        if evac:
            add("evac", s)

    def norm(n):
        add("ssq", n)
        add("rstd", n)
        for t in range(NT):
            add("xhat", n, t)

    def turn(n):
        for c in range(KD // 2):
            add("turn", n, c)

    def units(pairs, fill):
        n = len(pairs)
        for i in range(n + 2):
            if i >= 2:
                for u in pairs[i - 2]:
                    add("pv", u)
                    if u in UNIT_ENDS:
                        add("o_group", UNIT_ENDS[u])
            if 1 <= i <= n:
                for u in pairs[i - 1]:
                    add("turn_p", u)
            if i < n:
                for u in pairs[i]:
                    add("scores", u)
            fill()

    ada, summed = iter(range(24)), []

    def more_ada():
        if len(summed) == 2:
            add("ada_sum", summed.pop(0))
        for j in ada:
            raw.append(("ada", j))
            add("ada", j)
            summed.append(j)
            return

    norm(0)
    add("columns")
    split(0)
    turn(0)
    split(1)
    for j in range(4):
        block("proj", j)
        more_ada()
    add("turn_qk", 0)
    block("proj", 4)
    add("turn_qk", 1)
    block("proj", 5)
    add("stick", 0), add("stick", 1)
    add("rope1", 1)
    block("proj", 6)
    add("suffix", 0), add("suffix", 1)
    add("rope1", 0)
    block("proj", 7)
    add("pv_stick", 0), add("pv_stick", 1)
    add("stick", 2), add("stick", 3)
    block("proj", 8)
    add("turn_qk", 4)
    add("suffix", 2), add("suffix", 3)
    add("gates_c")
    add("rope1", 2)
    block("gate", 0)
    add("turn_qk", 5), add("turn_qk", 6)
    add("pv_stick", 2), add("pv_stick", 3)
    add("o_group", 0)
    add("index", 0), add("index", 1)
    add("turn_cmp", 0), add("turn_cmp", 1)
    add("rope1", 3)
    block("gate", 1)
    raw.append(("cmp_w1", 0))
    add("cmp_hidden", 0)
    raw.append(("cmp_w1", 1))
    add("cmp_hidden", 1)
    add("turn_qk", 2), add("turn_qk", 3)
    add("topk", 0, 0)
    block("gate", 2)
    add("cmp_kv")
    add("topk", 0, 1)
    block("gate", 3)
    add("cmp_scores")
    fillers = iter(range(4, 12))
    between = iter([[("turn_cmp_p",), ("topk", 1, 0)], [("cmp_pv",), ("o_group", 1), ("topk", 1, 1)]])

    def filler():
        for j in fillers:
            block("gate", j)
            break
        for steps in between:
            for step in steps:
                add(*step)
            break

    units([(4, 5), (6, 7), (8, 9), (10, 11), (0, 1), (2, 3)], filler)
    for c in range(3):
        add("turn_o", c)
    for j in range(3):
        block("up", j, evac=False)
        add("merge", j)
    for j in range(4):
        block("out", j, evac=False, ahead=j < 3)
        if j == 0:
            norm(1)
        if j == 2:
            turn(1)
    add("residual", 0)
    norm(2)
    split(where["mem_q",])
    block("mem_k")
    turn(2)
    block("mem_q")
    v = iter(("mem_v",))
    units([(12, 13), (14, 15)], lambda: [block(b) for b in v])
    add("turn_o", 3)
    block("mem_o", evac=False, ahead=False)
    add("residual", 1)
    norm(3)
    split(where["ffn_in", 1])
    turn(3)
    parts = {"first": table}
    table = parts["ffn"] = []
    block("ffn_in", 0)
    block("ffn_in", 1)
    for i in range(1, 11):
        block("ffn_in", 2 * i)
        more_ada()
        if i in (2, 5, 8):
            more_ada()
        block("ffn_in", 2 * i + 1)
        block("ffn_out", i - 1, evac=False)
    add("mod", 0)
    block("ffn_out", 10, evac=False, ahead=False)
    table = parts["second"] = []
    add("residual", 2)
    norm(5)
    split(where["proj2", 1])
    turn(5)
    add("final_norm")
    after = {0: [], 1: [("rope2", 0)], 3: [("rope2", 1)], 4: [("turn_ret", 0), ("turn_ret", 1)],
             5: [("turn_ret", 2), ("turn_ret", 3), ("fox_square", 0)], 7: [("fox_square", 1), ("fox_norm", 0)],
             8: [("forget",), ("fox_norm", 1)], 9: [("forget_sum",), ("ret_scores", 0), ("ret_scores", 1)],
             10: [("turn_fox", i) for i in range(8)],
             11: [("ret_pv", 0), ("ret_pv", 1), ("ret_scores", 2), ("ret_scores", 3), ("gate_row", 0)],
             12: [("ret_pv", 2), ("ret_pv", 3), ("o_group", 8), ("mix", 0, 0)]}
    for j in range(13):
        block("proj2", j)
        if j in (0, 1, 2, 3):
            more_ada()
        for step in after.get(j, ()):
            add(*step)
    rest = iter(range(13, 17))
    late = iter([[("mix2", 0, 0)], [("turn_mixed", 2), ("turn_mixed", 3)], [], [("mix", 1, 0)], [("mix2", 1, 0)]])

    def more():
        for j in rest:
            block("proj2", j)
            break
        for steps in late:
            for step in steps:
                add(*step)
            break

    units([(16, 17), (18, 19), (20, 21), (22, 23)], more)
    add("mix", 1, 1)
    block("out2", 2, evac=False)
    add("mix2", 1, 1)
    block("out2", 3, evac=False)
    add("turn_mixed", 0), add("turn_mixed", 1)
    block("out2", 0, evac=False)
    while summed:
        add("ada_sum", summed.pop(0))
    add("mod", 1)
    block("out2", 1, evac=False, ahead=False)
    add("residual", 3)
    norm(6)
    split(where["mlp_in", 1])
    turn(6)
    table = parts["mlp"] = []
    block("mlp_in", 0)
    for i in range(1, 16):
        block("mlp_in", i)
        if 2 <= i < 6:
            more_ada()
        if 6 <= i < 8 and summed:
            add("ada_sum", summed.pop(0))
        block("mlp_out", i - 1, evac=False)
        if i == 7:
            add("gate_row", 1)
    block("mlp_out", 15, evac=False)
    add("residual", 4)
    return parts, blocks, where, raw


UNITS = [("b", t, hp) for t in range(NT) for hp in range(2)] + [("c", t, h) for t in range(NT) for h in range(4)]
UNITS += [("mem", t, hp) for t in range(NT) for hp in range(2)] + [("fox", t, hp) for t in range(NT) for hp in range(4)]
GROUP = {"b": lambda t: 2, "c": lambda t: 3 + t, "mem": lambda t: 5, "fox": lambda t: 6 + t}
UNIT_ENDS = {7: 3, 11: 4, 3: 2, 15: 5, 19: 6, 23: 7}
XHAT = {n: i for i, n in enumerate([0, 1, 2, 3, 5, 6])}
GAIN = {0: "norm_mix", 1: "norm_mem_kv", 2: "norm_mem_q", 3: "norm_ffn"}
RESIDUAL = {2: "out", 3: "mem_o", 5: "ffn_out"}
EXP_ORDER = {u: 4 + n for n, u in enumerate([4, 5, 6, 7, 8, 9, 10, 11, 0, 1, 2, 3] + list(range(12, 24)))}
PV_ORDER = {u: n if u < 16 else n + RH for u, n in EXP_ORDER.items()}
PV_RET = EXP_ORDER[16]
O_BANK = {0: 2, 1: 3, 3: 2, 4: 3, 2: 2, 5: 3, 6: 2, 7: 3, 8: 2, 9: 3}
TURNS = [("QA", 0), ("KA", 2), ("QC", 4), ("KSW", 6), ("QI", 8), ("KIB", 10), ("QB", 12)]
S_QA, S_KA, S_QC, S_KSW, S_QI, S_KI, S_KB, S_QB = 0, 2, 4, 6, 8, 10, 11, 12
PROJ2_BLOCKS = [(c + i, 256) for c in (RQ, RK, FQ, FK) for i in (0, 256)] + [(FF, FH)] + \
    [(c + i, 256) for c in (RV, RG, FV, FOG) for i in (0, 256)]
PROJ2_LAST = {c: max(j for j, b in enumerate(PROJ2_BLOCKS) if c <= b[0] < c + 512)
              for c in (RQ, RK, FQ, FK, RV, RG, FV, FOG)}
SMALL = ["x", "mem", "norm_mix", "cmp_pos_k", "cmp_w2_k", "cmp_pos_v", "cmp_w2_v", "norm_mem_q", "norm_mem_kv",
         "norm_ffn", "norm_final", "c_2", "b_ada_2", "b_forget_2", "q_norm_gain_2", "k_norm_gain_2",
         "fox_out_gain_2", "ret_out_gain_2"]


def weight_stream(w):
    _, blocks, _, raw_order = plan()

    def columns(a, c0, n=W_COLS):
        return a[:, c0:c0 + n].reshape(KD, P, -1).transpose(1, 0, 2).reshape(P, -1)

    def whole_rows(a, j):
        return a[ROWS * j:ROWS * j + ROWS].reshape(ROWS // P, P, -1).transpose(1, 0, 2).reshape(P, -1)

    def ffn_in(j):
        a = w["w_ffn_in"][0].reshape(KD, P, 2, D_FF)[:, :, :, P * j:P * j + P]
        return a.transpose(1, 0, 2, 3).reshape(P, -1)

    up = np.reshape(w["w_up"][0], (-1, D))
    of = dict(
        proj=lambda j: columns(w["w_in"][0], 256 * j, min(256, PROJ - 256 * j)),
        gate=lambda j: columns(w["w_in"][0], GM + 256 * j),
        mem_k=lambda j: columns(w["w_mem_kv"][0], 0), mem_v=lambda j: columns(w["w_mem_kv"][0], 256),
        mem_q=lambda j: columns(w["w_mem_q"][0], 0), mem_o=lambda j: whole_rows(w["w_mem_o"][0], 0),
        up=lambda j: whole_rows(up, j), out=lambda j: whole_rows(w["w_out"][0], j), ffn_in=ffn_in,
        ffn_out=lambda j: whole_rows(w["w_ffn_out"][0], j),
        proj2=lambda j: columns(w["w_in_2"][0], *PROJ2_BLOCKS[j]),
        out2=lambda j: whole_rows(w["w_out_2"][0], j), mlp_in=lambda j: columns(w["w_mlp_in_2"][0], 256 * j),
        mlp_out=lambda j: whole_rows(w["w_mlp_out_2"][0], j), ada=lambda j: columns(w["w_ada_2"][0], 256 * j),
        cmp_w1=lambda j: w["cmp_w1_v" if j else "cmp_w1_k"][0].reshape(16, P, P).transpose(1, 0, 2).reshape(P, -1))
    stream = np.zeros((len(raw_order), P, BLOCK), np.float32)
    for i, what in enumerate(raw_order):
        b = blocks[what[1]] if what[0] == "split" else what
        x = of[b[0]](b[-1] if len(b) > 1 else 0)
        stream[i, :, 0:x.shape[1]] = x
    return stream


def two_blocks_kernel(nc, d, stream, consts_dram, out_dram):
    parts, blocks, where, raw_order = plan()
    table = [step for part in parts.values() for step in part]

    with ExitStack() as ctx:
        names = {}

        def sb(stack, name, shape, dt=F32):
            return stack.enter_context(nc.sbuf_tensor("sb_" + name, shape, dt))

        def sem(name):
            if name not in names:
                names[name] = ctx.enter_context(nc.semaphore(name))
            return names[name]

        raw = sb(ctx, "raw", [P, RAW, BLOCK])
        hi = sb(ctx, "hi", [P, SPLIT, BLOCK], F32R)
        lo = sb(ctx, "lo", [P, SPLIT, BLOCK], F32R)
        h = sb(ctx, "h", [P, NT, D])
        u_hi = sb(ctx, "u_hi", [P, KD, T], F32R)
        u_lo = sb(ctx, "u_lo", [P, KD, T], F32R)
        work = sb(ctx, "work", [P, NT * 2 * FH * AUG])
        row_bc = sb(ctx, "row_bc", [P, D])
        masked = sb(ctx, "masked", [P, 2, 512])
        prob = sb(ctx, "prob", [P, 2, 512])
        prob_t = sb(ctx, "prob_t", [P, 2, 512])
        const = sb(ctx, "const", [P, DECAY_AT])
        cols = sb(ctx, "cols", [P, NROWS])
        mod = sb(ctx, "mod", [P, 48])
        scale1 = sb(ctx, "scale1", [P, 2, KD])
        c_act = sb(ctx, "c_act", [P, KD])
        c_tanh = sb(ctx, "c_tanh", [P, KD])
        ada_acc = sb(ctx, "ada_acc", [P, 2, W_COLS])
        square_sum = sb(ctx, "square_sum", [P, 7, NT])
        rstd = sb(ctx, "rstd", [P, 7, NT])
        mhalf = sb(ctx, "mhalf", [P, NT * FH])
        neg_max = sb(ctx, "neg_max", [P, 24, 2])
        den = sb(ctx, "den", [P, 24, 2])
        rden = sb(ctx, "rden", [P, 24, 2])
        rows = row_bc[0:NROWS, 0:P]

        def scope(stack, *specs):
            return [sb(stack, *s) for s in specs]

        first = ExitStack()
        s = ExitStack()
        merged_hi, merged_lo = scope(s, ("merged_hi", [P, KD, T], F32R), ("merged_lo", [P, KD, T], F32R))
        s.close()
        proj, = scope(first, ("proj", [P, NT, PROJ]))
        s = ExitStack()
        mem_t_hi, mem_t_lo, mem_rows = scope(s, ("mem_t_hi", [P, KD, T], F32R), ("mem_t_lo", [P, KD, T], F32R),
                                             ("mem_rows", [P, NT, D]))
        s.close()
        gates, qk_t, km_t, vm, sel_neg, cmp_in, kc_t, vc, w2k, w2v, hid_x, hid_t, hid_k, hid_v, cmp_s, cmp_m, \
            cmp_d, gate_c, idx_w, best = scope(
                first, ("gates", [P, 24, T]), ("qk_t", [P, 14, T]), ("km_t", [P, 2, T]), ("vm", [P, 2, T]),
                ("sel_neg", [P, NT, T]), ("cmp_in", [P, 2, 256]), ("kc_t", [P, NC]), ("vc", [P, HD]),
                ("w2k", [P, 2, HD]), ("w2v", [P, HD]), ("hid_x", [P, 2, 16]), ("hid_t", [P, 2, 16]),
                ("hid_k", [P, NC]), ("hid_v", [P, 4, 32]), ("cmp_s", [P, NT, 4, NC]), ("cmp_m", [P, 8]),
                ("cmp_d", [P, 8]), ("gate_c", [P, NT, 4, 3]), ("idx_w", [P, NT, 4]), ("best", [P, 8]))
        qm_t = qk_t[:, 0:2, :]
        first.close()
        ff = ExitStack()
        hid_hi, hid_lo, hid, act_out = scope(ff, ("hid_hi", [P, 4, T], F32R), ("hid_lo", [P, 4, T], F32R),
                                             ("hid", [P, 512]), ("act_out", [P, 2, 512]))
        ff.close()
        second = ExitStack()
        s = ExitStack()
        mixed, = scope(s, ("mixed", [P, 2, 2, KD // 2, T], F32R))
        s.close()
        ret_t, fox_t, proj2, gains, logit, soft, fstat, decays = scope(
            second, ("ret_t", [P, 2 * RH, T]), ("fox_t", [P, 2 * FH, T]), ("proj2", [P, NT, PROJ2]),
            ("gains", [P, 2 * HD + FH + 1024]), ("logit", [P, NT, FH]), ("soft", [P, NT, FH]),
            ("fstat", [P, 5, NT * FH]), ("decays", [P, RH * 2 * P]))
        second.close()

        banks = [ctx.enter_context(nc.psum_tensor(f"bank{b}", [P, 512], F32)) for b in range(8)]
        filled = [sem(f"bank{b}_filled") for b in range(8)]
        freed = [sem(f"bank{b}_freed") for b in range(8)]
        raw_loaded = [sem(f"raw{r}_loaded") for r in range(RAW)]

        def cst(name):
            a = CONST_AT[name]
            return const[:, a:a + CONST_WIDTHS[name]]

        ident, ones = cst("ident"), cst("ones")
        norm_rows = work[:, 0:NT * D].rearrange("p (t c) -> p t c", t=NT)
        o_rows = work[:, 0:NT * 768].rearrange("p (t c) -> p t c", t=NT)
        o_mem = work[:, 0:NT * 256].rearrange("p (t c) -> p t c", t=NT)
        aug = work[:, :].rearrange("p (t s h c) -> p t s h c", t=NT, s=2, h=FH)
        spare = work[:, 1536:2048]
        second_rows = proj2[:, :, RV:RV + D]
        fox_rows = [norm_rows[:, t, 0:512] for t in range(NT)]
        ret_rows = [proj2[:, t, RK:RK + 512] for t in range(NT)]
        gain_q, gain_k = gains[:, 0:HD], gains[:, HD:2 * HD]
        b_forget = gains[:, 2 * HD:2 * HD + FH]
        out_gain = gains[:, 2 * HD + FH:]

        def width(s):
            b = blocks[s]
            if b[0] == "proj":
                return min(256, PROJ - 256 * b[1])
            return PROJ2_BLOCKS[b[1]][1] if b[0] == "proj2" else 256

        def shaped(flat, what, s=None):
            kind = what[0]
            if kind in ("up", "out", "ffn_out", "out2", "mlp_out", "mem_o"):
                return flat.rearrange("p (k n) -> p k n", k=2)
            if kind == "cmp_w1":
                return flat.rearrange("p (k n) -> p k n", k=16)
            n = width(s) if s is not None else 256
            return flat[:, 0:KD * n].rearrange("p (k n) -> p k n", k=KD)

        raw_at = {what: i for i, what in enumerate(raw_order)}

        def raw_ready(eng, what):
            i = raw_at[what]
            eng.wait_ge(raw_loaded[i % RAW], 16 * (i // RAW + 1))
            return raw[:, i % RAW, :]

        lease, uses, fills = {}, [0] * 8, [0] * 8
        turn_of = {"stream": 0, "score": 0, "turn": 0}
        POOL = {"stream": (0, 1), "score": (4, 5), "turn": (6, 7)}

        def wait_filled(eng, key):
            b, n, _ = lease[key]
            eng.wait_ge(filled[b], n)
            return banks[b]

        def free(ins, key):
            return ins.then_inc(freed[lease[key][0]], 1)

        def wait_evacuated(eng, key):
            b, _, n = lease[key]
            eng.wait_ge(freed[b], n)

        used_at = {}

        def wait_used(eng, s):
            at = used_at[s]
            if at[0] == "block_used":
                eng.wait_ge(sem("block_used"), at[1])
            else:
                wait_filled(eng, at[0])

        def run(engine_steps):
            for step in table:
                if step[0] in engine_steps:
                    engine_steps[step[0]](*step[1:])

        block = ctx.enter_context(nc.Block())

        @block.tensor
        def _(pe):
            def claim(key, bank):
                if bank in POOL:
                    turn_of[bank] ^= 1
                    bank = POOL[bank][turn_of[bank]]
                if uses[bank]:
                    pe.wait_ge(freed[bank], uses[bank])
                uses[bank] += 1
                lease[key] = (bank, fills[bank] + 1, uses[bank])
                return banks[bank]

            def fill(ins, key):
                b = lease[key][0]
                fills[b] += 1
                ins.then_inc(filled[b], 1)

            apart = [0]

            def rows_apart(ins):
                apart[0] += 1
                ins.then_inc(sem("rows_apart"), 1)
                pe.wait_ge(sem("rows_apart"), apart[0])

            def product(out, terms, ready=None):
                n = len(terms)
                for i, (a_hi, a_lo, b_hi, b_lo) in enumerate(terms):
                    if ready is not None and i % 2 == 0:
                        ready(i // 2)
                    nc.tensor.matmul(out, a_hi, b_hi, start=(i == 0), stop=False)
                    nc.tensor.matmul(out, a_hi, b_lo, start=False, stop=False)
                    last = nc.tensor.matmul(out, a_lo, b_hi, start=False, stop=(i == n - 1))
                return last

            def weights(s):
                pe.wait_ge(sem("lo_ready"), s + 1)
                w = blocks[s]
                return shaped(hi[:, s % SPLIT, :], w, s), shaped(lo[:, s % SPLIT, :], w, s)

            def by_token(s, key, bank, x_hi, x_lo, n, ready=None):
                w_hi, w_lo = weights(s)
                ps = claim(key, bank)
                for t in range(NT):
                    tok = slice(t * P, t * P + P)
                    last = product(ps[:, t * n:t * n + n], [
                        (x_hi[:, k, tok], x_lo[:, k, tok], w_hi[:, k, :], w_lo[:, k, :]) for k in range(KD)],
                        None if t else ready)
                return last

            def by_feature(s, key, bank, x_hi, x_lo, ready=None):
                w_hi, w_lo = weights(s)
                ps = claim(key, bank)
                for m in range(2):
                    f = slice(m * P, m * P + P)
                    last = product(ps[:, m * T:m * T + T], [
                        (w_hi[:, k, f], w_lo[:, k, f], x_hi[:, k, :], x_lo[:, k, :]) for k in range(KD)],
                        None if m else ready)
                return last

            def accumulate(s, group, x_hi, x_lo, k0, first, last_one):
                w_hi, w_lo = weights(s)
                for t in range(NT):
                    tok = slice(t * P, t * P + P)
                    for half in range(2):
                        key = (group, t, half)
                        ps = claim(key, 2 * t + half) if first else banks[2 * t + half]
                        n = slice(half * 512, half * 512 + 512)
                        for k in range(2):
                            x1, x2 = x_hi[:, k0 + k, tok], x_lo[:, k0 + k, tok]
                            nc.tensor.matmul(ps[:, :], x1, w_hi[:, k, n], start=first and k == 0, stop=False)
                            nc.tensor.matmul(ps[:, :], x1, w_lo[:, k, n], start=False, stop=False)
                            last = nc.tensor.matmul(ps[:, :], x2, w_hi[:, k, n], start=False,
                                                    stop=last_one and k == 1)
                        if last_one and not (t == 1 and half == 1):
                            fill(last, key)
                return last, (group, 1, 1)

            def take(s):
                kind, j = blocks[s][0], blocks[s][-1]
                key = ("block", s)
                if kind in ("proj", "proj2"):
                    n = 0 if kind == "proj" else 5
                    last = by_token(s, key, "stream", u_hi, u_lo, width(s), turned(n) if j == 0 else None)
                elif kind == "gate":
                    last = by_feature(s, key, "stream", u_hi, u_lo)
                elif kind == "mem_k":
                    last = by_feature(s, key, "stream", mem_t_hi, mem_t_lo, turned(1))
                elif kind == "mem_v":
                    last = by_token(s, key, "stream", mem_t_hi, mem_t_lo, 256)
                elif kind == "mem_q":
                    last = by_feature(s, key, "stream", u_hi, u_lo, turned(2))
                elif kind in ("ffn_in", "mlp_in"):
                    n = 3 if kind == "ffn_in" else 6
                    last = by_feature(s, key, "score", u_hi, u_lo, turned(n) if j == 0 else None)
                elif kind == "up":
                    return up(s, j)
                else:
                    if kind == "out":
                        pe.wait_ge(sem("merged_split"), j + 1)
                        args = (merged_hi, merged_lo, 2 * j, j == 0, j == 3)
                    elif kind == "out2":
                        wait_evacuated(pe, ("turn_mixed", j))
                        part = mixed[:, int(j < 2)]
                        args = (part[:, 0], part[:, 1], 2 * (j % 2), j == 2, j == 1)
                    elif kind == "mem_o":
                        wait_evacuated(pe, ("turn_o", 3))
                        args = (u_hi, u_lo, 0, True, True)
                    else:
                        n = 11 if kind == "ffn_out" else 16
                        pe.wait_ge(sem("hidden_ready"), 2 * j + 2 if kind == "ffn_out" else 22 + j + 1)
                        args = (hid_hi, hid_lo, 2 * (j % 2), j == 0, j == n - 1)
                    last, key = accumulate(s, kind, *args)
                    if not args[4]:
                        used_at[s] = ("block_used", sum(x[0] == "block_used" for x in used_at.values()) + 1)
                        last.then_inc(sem("block_used"), 1)
                        return
                fill(last, key)
                used_at[s] = (key,)

            def up(s, j):
                w_hi, w_lo = weights(s)
                if j == 0:
                    for c in range(3):
                        wait_evacuated(pe, ("turn_o", c))
                for c in range(4):
                    ps = claim(("up", j, c), c)
                    for m in range(2):
                        f = slice((2 * c + m) * P, (2 * c + m + 1) * P)
                        last = product(ps[:, m * T:m * T + T], [
                            (w_hi[:, k, f], w_lo[:, k, f], u_hi[:, 2 * j + k, :], u_lo[:, 2 * j + k, :])
                            for k in range(2)])
                    fill(last, ("up", j, c))
                used_at[s] = (("up", j, 3),)

            def turned(n):
                return lambda c: wait_evacuated(pe, ("turn", n, c))
            def columns():
                pe.wait_ge(sem("ident_loaded"), 16)
                pe.wait_ge(sem("rows_loaded"), 16 * len(ROW_AT))
                ps = claim(("columns",), "turn")
                fill(nc.tensor.transpose(ps[:, 0:NROWS], rows, ident[0:NROWS, 0:NROWS]), ("columns",))

            def norm_turn(n, c):
                if c:
                    return
                if n == 0:
                    pe.wait_ge(sem("ident_loaded"), 16)
                ps = [claim(("turn", n, i), "turn" if i % 2 else "score") for i in range(KD // 2)]
                rows_of = second_rows if n == 5 else norm_rows
                for t in range(NT):
                    pe.wait_ge(sem("xhat_ready"), NT * XHAT[n] + t + 1)
                    for k in range(KD):
                        at = (k % 2) * T + t * P
                        last = nc.tensor.transpose(ps[k // 2][:, at:at + P], rows_of[:, t, k * P:k * P + P], ident)
                        if t and k % 2:
                            fill(last, ("turn", n, k // 2))

            def turn_qk(i):
                ps = claim(("turn_qk", i), "turn")
                kind = TURNS[i][0]
                if kind in ("QA", "KA"):
                    wait_evacuated(pe, ("block", where["proj", 0 if kind == "QA" else 1]))
                else:
                    pe.wait_ge(sem("rope_done"), {"QC": 3, "KSW": 4, "QI": 1, "KIB": 2, "QB": 2}[kind])
                at = {"QA": QA, "KA": KA, "QC": QC, "QI": QI, "QB": QB}
                pair = {"KSW": (KSEL, KWIN), "KIB": (KI, KB)}
                for m in range(2):
                    for t in range(NT):
                        out = ps[:, m * T + t * P:m * T + t * P + P]
                        if kind in at:
                            last = nc.tensor.transpose(out, proj[:, t, at[kind] + m * P:at[kind] + m * P + P], ident)
                        else:
                            c = pair[kind][m]
                            last = nc.tensor.transpose(out[0:HD, :], proj[:, t, c:c + HD], ident)
                fill(last, ("turn_qk", i))

            def stick(hd):
                ps = claim(("stick", hd), "score")
                if hd == 0:
                    wait_evacuated(pe, ("turn_qk", 0))
                    wait_evacuated(pe, ("turn_qk", 1))
                r = slice(HD * (hd % 2), HD * (hd % 2) + HD)
                q, k = qk_t[r, S_QA + hd // 2, :], qk_t[r, S_KA + hd // 2, :]
                nc.tensor.matmul(ps[:, 0:T], k[:, 0:P], q, start=True, stop=True)
                fill(nc.tensor.matmul(ps[:, T:T + P], k[:, P:T], q[:, P:T], start=True, stop=True), ("stick", hd))

            def suffix(hd):
                pe.wait_ge(sem("softplus_ready"), hd + 1)
                ps = claim(("suffix", hd), "turn")
                l = prob_t[:, hd % 2, :]
                nc.tensor.matmul(ps[:, T:T + P], cst("suffix"), l[:, T:T + P], start=True, stop=True)
                nc.tensor.matmul(ps[:, 0:P], cst("suffix"), l[:, 0:P], start=True, stop=True)
                nc.tensor.matmul(ps[:, P:T], cst("suffix"), l[:, P:T], start=True, stop=False)
                fill(nc.tensor.matmul(ps[:, P:T], ones, l[:, T:T + P], start=False, stop=True), ("suffix", hd))

            def pv_stick(hd):
                pe.wait_ge(sem("exp_done"), hd + 1)
                if hd == 0:
                    claim(("o", 0), O_BANK[0])
                    wait_evacuated(pe, ("block", where["proj", 2]))
                w, c = prob[:, hd % 2, :], VA + HD * hd
                o0 = banks[O_BANK[0]][:, HD * hd:HD * hd + HD]
                o1 = banks[O_BANK[0]][:, HD * (4 + hd):HD * (4 + hd) + HD]
                nc.tensor.matmul(o0, w[:, 0:P], proj[:, 0, c:c + HD], start=True, stop=True)
                nc.tensor.matmul(o1, w[:, P:T], proj[:, 0, c:c + HD], start=True, stop=False)
                nc.tensor.matmul(o1, w[:, T:T + P], proj[:, 1, c:c + HD], start=False, stop=True) \
                    .then_inc(sem("pv_done"), 1)

            def index(t):
                n = P * (t + 1)
                for i in range(2):
                    ps = claim(("index", t, i), "score")
                    if t == 0 and i == 0:
                        wait_evacuated(pe, ("turn_qk", 4))
                        wait_evacuated(pe, ("turn_qk", 5))
                    r = slice(HD * i, HD * i + HD)
                    for m in range(2):
                        last = nc.tensor.matmul(ps[:, m * n:m * n + n], qk_t[r, S_QI + m, t * P:t * P + P],
                                                qk_t[r, S_KI, 0:n], start=True, stop=True)
                    fill(last, ("index", t, i))

            def turn_cmp(i):
                ps = claim(("turn_cmp", i), "turn")
                if i == 0:
                    pe.wait_ge(sem("rope_done"), 3)
                else:
                    wait_evacuated(pe, ("block", where["proj", 7]))
                c = (KCMP, VCMP)[i]
                for t in range(NT):
                    last = nc.tensor.transpose(ps[0:HD, t * P:t * P + P], proj[:, t, c:c + HD], ident)
                fill(last, ("turn_cmp", i))

            def cmp_hidden(i):
                w = shaped(raw_ready(pe, ("cmp_w1", i)), ("cmp_w1", i))
                ps = claim(("cmp_hidden", i), "turn")
                pe.wait_ge(sem("cmp_in_ready"), i + 1)
                x = cmp_in[:, i, :].rearrange("p (k n) -> p k n", k=16)
                for k in range(16):
                    last = nc.tensor.matmul(ps[:, 0:16], w[:, k, :], x[:, k, :], start=(k == 0), stop=(k == 15))
                fill(last, ("cmp_hidden", i))

            def cmp_kv():
                pe.wait_ge(sem("cmp_hid_ready"), 1)
                pe.wait_ge(sem("w2_loaded"), 16 * 3)
                ps = claim(("cmp_kv",), "turn")
                nc.tensor.matmul(ps[:, 0:NC], w2k[:, :, :].rearrange("p a b -> p (a b)"), hid_k[:, :],
                                 start=True, stop=True)
                fill(nc.tensor.matmul(ps[:, HD:2 * HD], hid_v[:, :, :].rearrange("p a b -> p (a b)"), w2v[:, :],
                                      start=True, stop=True), ("cmp_kv",))

            def cmp_scores():
                wait_evacuated(pe, ("cmp_kv",))
                wait_evacuated(pe, ("turn_qk", 2))
                ps = claim(("cmp_scores",), "score")
                for odd in range(2):
                    r = slice(HD * odd, HD * odd + HD)
                    for t in range(NT):
                        for m in range(2):
                            at = 16 * (4 * t + 2 * m + odd)
                            last = nc.tensor.matmul(ps[:, at:at + NC], qk_t[r, S_QC + m, t * P:t * P + P],
                                                    kc_t[r, :], start=True, stop=True)
                    if not odd:
                        rows_apart(last)
                fill(last, ("cmp_scores",))

            def turn_cmp_p():
                pe.wait_ge(sem("cmp_p_ready"), 1)
                ps = claim(("turn_cmp_p",), "turn")
                for t in range(NT):
                    last = nc.tensor.transpose(ps[:, t * P:t * P + P], cmp_in[:, 0, t * P:t * P + P], ident)
                fill(last, ("turn_cmp_p",))

            def cmp_pv():
                wait_evacuated(pe, ("turn_cmp_p",))
                ps = claim(("o", 1), O_BANK[1])
                for hd in range(4):
                    for t in range(NT):
                        r = slice(32 * hd, 32 * hd + NC)
                        at = HD * (4 * t + hd)
                        last = nc.tensor.matmul(ps[:, at:at + HD], cmp_in[r, 1, t * P:t * P + P], vc[r, :],
                                                start=True, stop=True, tile_position=(32 * hd, 0))
                    if hd < 3:
                        rows_apart(last)
                fill(last, ("o", 1))

            def scores(u):
                kind, t, i = UNITS[u]
                n = T if kind == "mem" else P * (t + 1)
                tok = slice(t * P, t * P + P)
                if u == 4:
                    wait_evacuated(pe, ("turn_qk", 3))
                if u == 0:
                    wait_evacuated(pe, ("turn_qk", 6))
                if u == 12:
                    wait_evacuated(pe, ("block", where["mem_q",]))
                    wait_evacuated(pe, ("block", where["mem_k",]))
                if u == 16:
                    for c in range(8):
                        wait_evacuated(pe, ("turn_fox", c))
                ps = claim(("scores", u), "score")
                if kind == "c":
                    r = slice(HD * (i % 2), HD * (i % 2) + HD)
                    last = nc.tensor.matmul(ps[:, 0:2 * n].rearrange("p (s n) -> p s n", s=2),
                                            qk_t[r, S_QC + i // 2, tok], qk_t[r, S_KSW:S_KSW + 2, 0:n],
                                            start=True, stop=True)
                else:
                    for m in range(2):
                        r = slice(HD * i, HD * i + HD)
                        if kind == "b":
                            q, k = qk_t[r, S_QB + m, tok], qk_t[r, S_KB, 0:n]
                        elif kind == "mem":
                            q, k = qm_t[r, m, tok], km_t[r, m, :]
                        else:
                            q, k = fox_t[0:AUG, 2 * i + m, tok], fox_t[0:AUG, FH + 2 * i + m, 0:n]
                        last = nc.tensor.matmul(ps[:, m * n:m * n + n], q, k, start=True, stop=True)
                fill(last, ("scores", u))

            def turn_p(u):
                kind, t, _ = UNITS[u]
                keys = NT if kind == "mem" else t + 1
                pe.wait_ge(sem("exp_done"), EXP_ORDER[u] + 1)
                ps = claim(("turn_p", u), "turn")
                for i in range(2 * keys):
                    last = nc.tensor.transpose(ps[:, i * P:i * P + P], prob[:, EXP_ORDER[u] % 2, i * P:i * P + P], ident)
                fill(last, ("turn_p", u))

            def pv(u):
                kind, t, i = UNITS[u]
                keys = NT if kind == "mem" else t + 1
                g = GROUP[kind](t)
                if ("o", g) not in lease:
                    claim(("o", g), O_BANK[g])
                if u == 12:
                    wait_evacuated(pe, ("block", where["mem_v",]))
                if u == 16:
                    wait_evacuated(pe, ("block", where["proj2", PROJ2_LAST[FV]]))
                wait_evacuated(pe, ("turn_p", u))
                for m in range(2):
                    at = HD * {"b": 4 * t + 2 * i + m, "c": 2 * i + m, "mem": 4 * t + 2 * i + m, "fox": 2 * i + m}[kind]
                    for kt in range(keys):
                        c = HD * (2 * i + m)
                        v = {"b": lambda: proj[:, kt, VB:VB + HD],
                             "c": lambda: proj[:, kt, (VSEL, VWIN)[m]:(VSEL, VWIN)[m] + HD],
                             "mem": lambda: vm[:, kt, HD * (i + 2 * m):HD * (i + 2 * m) + HD],
                             "fox": lambda: proj2[:, kt, FV + c:FV + c + HD]}[kind]()
                        p = prob_t[:, EXP_ORDER[u] % 2, (m * keys + kt) * P:(m * keys + kt + 1) * P]
                        last = nc.tensor.matmul(banks[O_BANK[g]][:, at:at + HD], p, v,
                                                start=(kt == 0), stop=(kt == keys - 1))
                last.then_inc(sem("pv_done"), 1)

            def turn_o(c):
                if c in (0, 3):
                    wait_evacuated(pe, ("o", 0 if c == 0 else 5))
                elif c == 1:
                    wait_evacuated(pe, ("o", 2))
                else:
                    pe.wait_ge(sem("branch_c_done"), NT)
                ps = claim(("turn_o", c), "turn")
                for m in range(2):
                    for t in range(NT):
                        x = o_mem[:, t, m * P:m * P + P] if c == 3 else o_rows[:, t, 256 * c + m * P:256 * c + m * P + P]
                        last = nc.tensor.transpose(ps[:, m * T + t * P:m * T + t * P + P], x, ident)
                fill(last, ("turn_o", c))

            def ada_sum(j):
                pe.wait_ge(sem("ada_ready"), j + 1)
                ps = claim(("ada_sum", j), "turn")
                for m in range(2):
                    last = nc.tensor.matmul(ps[:, m:m + 1], ada_acc[:, j % 2, m * P:m * P + P], ones[:, 0:1],
                                            start=True, stop=True)
                fill(last, ("ada_sum", j))

            def gate_row(i):
                pe.wait_ge(sem("diag_ready"), i + 1)
                for half in range(2):
                    ps = claim(("gate_row", i, half), "score")
                    for m in range(4):
                        k = 4 * half + m
                        last = nc.tensor.matmul(ps[:, m * P:m * P + P], ones, work[:, k * P:k * P + P],
                                                start=True, stop=True)
                    fill(last, ("gate_row", i, half))

            def forget_sum():
                pe.wait_ge(sem("log_f_ready"), 1)
                ps = claim(("forget_sum",), "turn")
                nc.tensor.matmul(ps[:, 0:FH], cst("prefix"), soft[:, 0, :], start=True, stop=True)
                nc.tensor.matmul(ps[:, FH:2 * FH], cst("prefix"), soft[:, 1, :], start=True, stop=False)
                fill(nc.tensor.matmul(ps[:, FH:2 * FH], ones, soft[:, 0, :], start=False, stop=True),
                     ("forget_sum",))

            def turn_fox(i):
                pe.wait_ge(sem("aug_ready"), 3)
                ps = claim(("turn_fox", i), "turn")
                for m in range(2):
                    hd = (2 * i + m) % FH
                    for t in range(NT):
                        last = nc.tensor.transpose(ps[0:AUG, m * T + t * P:m * T + t * P + P],
                                                   aug[:, t, i // 4, hd, :], ident)
                fill(last, ("turn_fox", i))

            def turn_ret(i):
                pe.wait_ge(sem("rope2_done"), 1 + i // 2)
                ps = claim(("turn_ret", i), "turn")
                for m in range(2):
                    c = (RQ, RK)[i // 2] + RD * (2 * (i % 2) + m)
                    for t in range(NT):
                        last = nc.tensor.transpose(ps[:, m * T + t * P:m * T + t * P + P],
                                                   proj2[:, t, c:c + RD], ident)
                fill(last, ("turn_ret", i))

            def ret_scores(hd):
                if hd == 0:
                    for i in range(4):
                        wait_evacuated(pe, ("turn_ret", i))
                ps = claim(("ret_scores", hd), "score")
                q, k = ret_t[:, hd, :], ret_t[:, RH + hd, :]
                nc.tensor.matmul(ps[:, 0:T], k[:, 0:P], q, start=True, stop=True)
                fill(nc.tensor.matmul(ps[:, T:T + P], k[:, P:T], q[:, P:T], start=True, stop=True),
                     ("ret_scores", hd))

            def ret_pv(hd):
                wait_evacuated(pe, ("ret_scores", hd))
                if hd == 0:
                    claim(("o", 8), O_BANK[8])
                    claim(("o", 9), O_BANK[9])
                    wait_evacuated(pe, ("block", where["proj2", PROJ2_LAST[RV]]))
                w, c = prob[:, hd % 2, :], RV + RD * hd
                o0, o1 = (banks[O_BANK[8 + t]][:, RD * hd:RD * hd + RD] for t in range(NT))
                nc.tensor.matmul(o0, w[:, 0:P], proj2[:, 0, c:c + RD], start=True, stop=True)
                nc.tensor.matmul(o1, w[:, P:T], proj2[:, 0, c:c + RD], start=True, stop=False)
                nc.tensor.matmul(o1, w[:, T:T + P], proj2[:, 1, c:c + RD], start=False, stop=True) \
                    .then_inc(sem("pv_done"), 1)

            def turn_mixed(c):
                pe.wait_ge(sem("mix_done"), 1 if c >= 2 else 3)
                ps = claim(("turn_mixed", c), "turn")
                for k in range(2):
                    for t in range(NT):
                        f = (2 * (c % 2) + k) * P
                        x = ret_rows[t] if c >= 2 else fox_rows[t]
                        last = nc.tensor.transpose(ps[:, k * T + t * P:k * T + t * P + P], x[:, f:f + P], ident)
                fill(last, ("turn_mixed", c))

            run(dict(block=take, columns=columns, turn=norm_turn, turn_qk=turn_qk, stick=stick, suffix=suffix,
                     pv_stick=pv_stick, index=index, turn_cmp=turn_cmp, cmp_hidden=cmp_hidden, cmp_kv=cmp_kv,
                     cmp_scores=cmp_scores, turn_cmp_p=turn_cmp_p, cmp_pv=cmp_pv, scores=scores, turn_p=turn_p,
                     pv=pv, turn_o=turn_o, ada_sum=ada_sum, gate_row=gate_row, forget_sum=forget_sum,
                     turn_fox=turn_fox, turn_ret=turn_ret, ret_scores=ret_scores, ret_pv=ret_pv,
                     turn_mixed=turn_mixed))

        @block.scalar
        def _(act):
            chain = [0]

            def link(ins):
                chain[0] += 1
                ins.then_inc(sem("act_chain"), 1)
                act.wait_ge(sem("act_chain"), chain[0])

            def round_block(s):
                x = raw_ready(act, ("split", s))
                n = KD * width(s) if width(s) != 256 else BLOCK
                if s >= SPLIT:
                    wait_used(act, s - SPLIT)
                nc.scalar.copy(hi[:, s % SPLIT, 0:n], x[:, 0:n]).then_inc(sem("hi_ready"), 1)

            def evac(s):
                kind, j = blocks[s][0], blocks[s][-1]
                key = ("block", s)
                ps = wait_filled(act, key)
                n = width(s)
                both = ps[:, 0:2 * n].rearrange("p (t n) -> p t n", t=2)
                if kind == "proj":
                    free(nc.scalar.copy(proj[:, :, 256 * j:256 * j + n], both), key)
                elif kind == "gate":
                    free(nc.scalar.activation(gates[:, 2 * j:2 * j + 2, :], both, ACT.Tanh, scale=0.5), key)
                elif kind in ("mem_k", "mem_v", "mem_q"):
                    dst = {"mem_k": km_t, "mem_v": vm, "mem_q": qm_t}[kind]
                    free(nc.scalar.copy(dst[:, :, :] if kind != "mem_q" else dst, both), key)
                elif kind == "proj2":
                    c = PROJ2_BLOCKS[j][0]
                    free(nc.scalar.copy(proj2[:, :, c:c + n], both), key)
                elif kind == "ffn_in":
                    if j >= 2:
                        act.wait_ge(sem("hidden_ready"), j - 1)
                    nc.scalar.activation(act_out[:, j % 2, 0:T], ps[:, 0:T], ACT.Silu) \
                        .then_inc(sem("silu_ready"), 1)
                else:
                    if j >= 2:
                        act.wait_ge(sem("hidden_ready"), 22 + j - 1)
                    free(nc.scalar.activation(act_out[:, j % 2, :], ps[:, :], ACT.Relu), key)

            def ssq(n):
                if n == 1:
                    act.wait_ge(sem("mem_loaded"), 16)
                    act.wait_ge(sem("merged_split"), 4)
                src = mem_rows if n == 1 else h
                for t in range(NT):
                    if n == 0:
                        act.wait_ge(sem(f"x{t}_loaded"), 16)
                    if n in RESIDUAL:
                        for half in range(2):
                            wait_evacuated(act, (RESIDUAL[n], t, half))
                    if n == 6:
                        act.wait_ge(sem(("tile0_gated", "tile1_gated")[t]), 2)
                    if n == 5:
                        nc.scalar.activation((masked, prob)[t][:, :, :].rearrange("p a b -> p (a b)"), h[:, t, :],
                                             ACT.Square, accum_out=square_sum[:, 4, t:t + 1]) \
                            .then_inc(sem("squares_summed"), 1)
                        act.wait_ge(sem("gain_applied"), t + 1)
                        nc.scalar.activation((prob_t, act_out)[t][:, :, :].rearrange("p a b -> p (a b)"),
                                             norm_rows[:, t, :], ACT.Square, accum_out=square_sum[:, 5, t:t + 1]) \
                            .then_inc(sem("squares_summed"), 1)
                        continue
                    nc.scalar.activation(norm_rows[:, t, :], src[:, t, :], ACT.Square,
                                         accum_out=square_sum[:, n, t:t + 1]).then_inc(sem("squares_summed"), 1)

            def turn(n, c):
                ps = wait_filled(act, ("turn", n, c))
                dst = mem_t_hi if n == 1 else u_hi
                if n == 0 and c == 0:
                    wait_evacuated(act, ("columns",))
                if n >= 5 and c == 0:
                    act.wait_ge(sem("mod_ready"), n - 4)
                for m in range(2):
                    k, x = 2 * c + m, ps[:, m * T:m * T + T]
                    if n >= 5:
                        shift = mod[:, 24 * (n - 5) + k:24 * (n - 5) + k + 1]
                        if c >= 2:
                            wait_evacuated(act, ("turn", n, c - 2))
                        last = nc.scalar.activation(masked[:, c % 2, m * T:m * T + T], x, ACT.Identity, bias=shift,
                                                    scale=scale1[:, n - 5, k:k + 1])
                    else:
                        g = ROW_AT[GAIN[n]] + k
                        last = nc.scalar.activation(dst[:, k, :], x, ACT.Copy, scale=cols[:, g:g + 1])
                last.then_inc(sem("turn_hi"), 1)

            def columns():
                ps = wait_filled(act, ("columns",))
                free(nc.scalar.copy(cols[:, :], ps[:, 0:NROWS]), ("columns",))
                wait_evacuated(act, ("columns",))
                c = ROW_AT["c"]
                nc.scalar.activation(c_tanh[:, :], cols[:, c:c + KD], ACT.Tanh, scale=0.5) \
                    .then_inc(sem("c_tanh_ready"), 1)

            def turn_qk(i):
                ps = wait_filled(act, ("turn_qk", i))
                if TURNS[i][0] in ("KSW", "KIB"):
                    for r in (0, HD):
                        last = nc.scalar.copy(qk_t[r:r + HD, 2 * i:2 * i + 2, :],
                                              ps[0:HD, :].rearrange("p (m n) -> p m n", m=2))
                    free(last, ("turn_qk", i))
                    return
                free(nc.scalar.copy(qk_t[:, 2 * i:2 * i + 2, :], ps[:, :].rearrange("p (m n) -> p m n", m=2)),
                     ("turn_qk", i))

            def stick(hd):
                if hd % 2 == 0:
                    return
                z, p = masked[:, :, 0:3 * P], prob[:, :, 0:3 * P]
                for i in range(2):
                    act.wait_ge(sem("stick_masked"), hd + i)
                    if hd >= 2:
                        act.wait_ge(sem("pv_done"), hd + i - 2)
                    link(nc.scalar.activation(p[:, i, :], z[:, i, :], ACT.Abs))
                    link(nc.scalar.activation(p[:, i, :], p[:, i, :], ACT.Exp, scale=-1.0))
                for i in range(2):
                    nc.scalar.activation(p[:, i, :], p[:, i, :], ACT.Ln, bias=1.0).then_inc(sem("log_ready"), 1)

            def suffix(hd):
                act.wait_ge(sem("stick_summed"), hd + 1)
                nc.scalar.activation(prob[:, hd % 2, 0:3 * P], masked[:, hd % 2, 0:3 * P], ACT.Exp) \
                    .then_inc(sem("exp_done"), 1)

            def gates_c():
                wait_evacuated(act, ("block", where["proj", 8]))
                nc.scalar.activation(gate_c[:, :, :, :].rearrange("p t h g -> p t (h g)"), proj[:, :, GC:GC + 12],
                                     ACT.Tanh, scale=0.5).then_inc(sem("gate_c_tanh"), 1)

            def cmp_hidden(i):
                act.wait_ge(sem("cmp_poly_ready"), i + 1)
                nc.scalar.activation(hid_t[:, i, 0:NC], hid_t[:, i, 0:NC], ACT.Tanh,
                                     scale=float(np.sqrt(2 / np.pi))).then_inc(sem("cmp_tanh_ready"), 1)

            def cmp_kv():
                ps = wait_filled(act, ("cmp_kv",))
                nc.scalar.copy(kc_t[:, :], ps[:, 0:NC])
                free(nc.scalar.copy(vc[:, :], ps[:, HD:2 * HD]), ("cmp_kv",))

            def cmp_scores():
                act.wait_ge(sem("cmp_shifted"), 1)
                s = cmp_s[:, :, :, :].rearrange("p t h n -> p (t h n)")
                nc.scalar.activation(s, s, ACT.Exp).then_inc(sem("cmp_exp_done"), 1)

            def turn_cmp_p():
                ps = wait_filled(act, ("turn_cmp_p",))
                free(nc.scalar.copy(cmp_in[:, 1, :], ps[:, 0:T]), ("turn_cmp_p",))

            def scores(u):
                kind, t, _ = UNITS[u]
                n, q = T if kind == "mem" else P * (t + 1), EXP_ORDER[u]
                act.wait_ge(sem("max_ready"), q - 3)
                if q < 6 or u in (16, 17):
                    act.wait_ge(sem("pv_done"), PV_ORDER[u] - 1)
                for m in range(2):
                    last = nc.scalar.activation(prob[:, q % 2, m * n:m * n + n], masked[:, q % 2, m * n:m * n + n],
                                                ACT.Exp, bias=neg_max[:, u, m:m + 1],
                                                accum_out=den[:, u, m:m + 1])
                last.then_inc(sem("exp_done"), 1)

            def turn_p(u):
                kind, t, _ = UNITS[u]
                n, q = 2 * P * (NT if kind == "mem" else t + 1), EXP_ORDER[u]
                ps = wait_filled(act, ("turn_p", u))
                act.wait_ge(sem("pv_done"), PV_ORDER[u] - 1)
                free(nc.scalar.copy(prob_t[:, q % 2, 0:n], ps[:, 0:n]), ("turn_p", u))

            def turn_to(dst, key):
                ps = wait_filled(act, key)
                nc.scalar.copy(dst, ps[:, :].rearrange("p (m n) -> p m n", m=2)).then_inc(sem("turn_hi"), 1)

            def turn_o(c):
                turn_to(u_hi[:, 2 * (c % 3):2 * (c % 3) + 2, :], ("turn_o", c))

            def turn_mixed(c):
                two = slice(2 * (c % 2), 2 * (c % 2) + 2)
                turn_to(mixed[:, int(c < 2), 0, two, :], ("turn_mixed", c))

            def merge(j):
                for c in range(4 if j == 2 else 0):
                    act.wait_ge(sem("merge_done"), c + 1)
                    nc.scalar.copy(merged_hi[:, 2 * c:2 * c + 2, :].rearrange("p m n -> p (m n)"),
                                   work[:, 512 * c:512 * c + 512]).then_inc(sem("merged_hi_ready"), 1)

            def gate_row(i):
                for half in range(2):
                    ps = wait_filled(act, ("gate_row", i, half))
                    free(nc.scalar.copy(row_bc[:, 512 * half:512 * half + 512], ps[:, :]), ("gate_row", i, half))

            def forget():
                act.wait_ge(sem("logit_ready"), 1)
                link(nc.scalar.activation(soft[:, :, :], logit[:, :, :], ACT.Abs))
                link(nc.scalar.activation(soft[:, :, :], soft[:, :, :], ACT.Exp, scale=-1.0))
                nc.scalar.activation(soft[:, :, :], soft[:, :, :], ACT.Ln, bias=1.0).then_inc(sem("soft_ready"), 1)

            def turn_fox(i):
                ps = wait_filled(act, ("turn_fox", i))
                free(nc.scalar.copy(fox_t[0:AUG, 2 * i:2 * i + 2, :],
                                    ps[0:AUG, :].rearrange("p (m n) -> p m n", m=2)), ("turn_fox", i))

            def turn_ret(i):
                ps = wait_filled(act, ("turn_ret", i))
                free(nc.scalar.copy(ret_t[:, 2 * i:2 * i + 2, :], ps[:, :].rearrange("p (m n) -> p m n", m=2)),
                     ("turn_ret", i))

            def mix(part, t):
                if t:
                    return
                src, dst = ((RG, RQ), (FOG, FOG))[part]
                wait_evacuated(act, ("block", where["proj2", PROJ2_LAST[src]]))
                nc.scalar.activation(proj2[:, :, dst:dst + 512], proj2[:, :, src:src + 512], ACT.Tanh, scale=0.5) \
                    .then_inc(sem("mix_tanh"), 1)

            run({"round": round_block, "evac": evac, "ssq": ssq, "turn": turn, "columns": columns,
                 "turn_qk": turn_qk, "stick": stick, "suffix": suffix, "gates_c": gates_c, "cmp_hidden": cmp_hidden,
                 "cmp_kv": cmp_kv, "cmp_scores": cmp_scores, "turn_cmp_p": turn_cmp_p, "scores": scores,
                 "turn_p": turn_p, "turn_o": turn_o, "turn_mixed": turn_mixed, "merge": merge,
                 "gate_row": gate_row, "forget": forget, "turn_fox": turn_fox, "turn_ret": turn_ret, "mix": mix})

        @block.gpsimd
        def _(pool):
            chain = [0]

            def link(ins):
                chain[0] += 1
                ins.then_inc(sem("pool_chain"), 1)
                pool.wait_ge(sem("pool_chain"), chain[0])

            def inverse_root(dst, src, n):
                link(nc.gpsimd.tensor_scalar(src, src, n * EPS, None, ALU.add))
                return nc.gpsimd.tensor_tensor(dst, src, mhalf[:, 0:src.shape[-1]], ALU.pow)

            link(nc.gpsimd.memset(mhalf[:, :], -0.5))

            def rstd_of(n):
                for t in range(NT):
                    s, r = square_sum[:, n, t:t + 1], rstd[:, n, t:t + 1]
                    if n != 5:
                        pool.wait_ge(sem("squares_summed"), NT * n + t + 1)
                        inverse_root(r, s, D).then_inc(sem("rstd_ready"), 1)
                        continue
                    r4 = rstd[:, 4, t:t + 1]
                    pool.wait_ge(sem("squares_summed"), NT * 4 + 2 * t + 1)
                    link(inverse_root(r4, square_sum[:, 4, t:t + 1], D))
                    pool.wait_ge(sem("squares_summed"), NT * 4 + 2 * t + 2)
                    link(nc.gpsimd.tensor_scalar(s, s, r4, r4, ALU.mult, ALU.mult))
                    link(nc.gpsimd.tensor_scalar(r4, r4, ROOT_D, None, ALU.mult))
                    inverse_root(r, s, 1).then_inc(sem("rstd_ready"), 1)

            def residual(i):
                for half in range(2 if i >= 3 else 0):
                    pool.wait_ge(sem("product_gated"), 2 * (i - 3) + half + 1)
                    n = slice(512 * half, 512 * half + 512)
                    nc.gpsimd.tensor_tensor(h[:, 0, n], h[:, 0, n], prob[:, half, :], ALU.add) \
                        .then_inc(sem("tile0_gated"), 1)

            def head_stat(i):
                n = NT * FH if i < 2 else FH
                pool.wait_ge(sem("head_squares"), i + 1)
                inverse_root(fstat[:, i, 0:n], fstat[:, i, 0:n], RD if i == 2 else HD).then_inc(sem("head_rstd"), 1)

            run(dict(rstd=rstd_of, residual=residual, fox_square=head_stat, mix=lambda part, t: head_stat(2 + part + t)))

        @block.vector
        def _(dve):
            chain = [0]

            def link(ins):
                chain[0] += 1
                ins.then_inc(sem("dve_chain"), 1)
                dve.wait_ge(sem("dve_chain"), chain[0])

            tt, ts, stt = nc.vector.tensor_tensor, nc.vector.tensor_scalar, nc.vector.scalar_tensor_tensor

            def f32(ap):
                return ap.bitcast(F32)

            def over(ap, n):
                shape = list(ap.shape) + [n]
                return ap.unsqueeze(len(shape) - 1).broadcast_to(shape)

            def residue(s):
                x = raw[:, raw_at["split", s] % RAW, :]
                n = KD * width(s) if width(s) != 256 else BLOCK
                dve.wait_ge(sem("hi_ready"), s + 1)
                tt(lo[:, s % SPLIT, 0:n], x[:, 0:n], f32(hi[:, s % SPLIT, 0:n]), ALU.subtract) \
                    .then_inc(sem("lo_ready"), 1)

            def evac(s):
                kind, j = blocks[s][0], blocks[s][-1]
                if kind in ("ffn_in", "mlp_in"):
                    dve.wait_ge(sem("hidden_ready"), j if kind == "ffn_in" else 22 + j)
                if kind == "ffn_in":
                    dve.wait_ge(sem("silu_ready"), j + 1)
                    ps = banks[lease["block", s][0]]
                    x = hid[:, 0:T]
                    free(tt(x, act_out[:, j % 2, 0:T], ps[:, T:2 * T], ALU.mult), ("block", s))
                    wait_evacuated(dve, ("block", s))
                    dst_hi, dst_lo = hid_hi[:, j % 4, :], hid_lo[:, j % 4, :]
                    if j >= 4:
                        wait_used(dve, where["ffn_out", (j - 4) // 2])
                elif kind == "mlp_in":
                    wait_evacuated(dve, ("block", s))
                    x = hid[:, :]
                    link(tt(x, act_out[:, j % 2, :], act_out[:, j % 2, :], ALU.mult))
                    two = slice(2 * (j % 2), 2 * (j % 2) + 2)
                    dst_hi = hid_hi[:, two, :].rearrange("p m n -> p (m n)")
                    dst_lo = hid_lo[:, two, :].rearrange("p m n -> p (m n)")
                    if j >= 2:
                        wait_used(dve, where["mlp_out", j - 2])
                else:
                    return
                link(nc.vector.tensor_copy(dst_hi, x))
                tt(dst_lo, x, f32(dst_hi), ALU.subtract).then_inc(sem("hidden_ready"), 1)

            def xhat(n, t):
                dve.wait_ge(sem("rstd_ready"), NT * XHAT[n] + t + 1)
                r = rstd[:, n, t:t + 1]
                if n == 5:
                    ins = ts(second_rows[:, t, :], norm_rows[:, t, :], rstd[:, 4, t:t + 1], r, ALU.mult, ALU.mult)
                else:
                    src = mem_rows if n == 1 else h
                    ins = ts(norm_rows[:, t, :], src[:, t, :], r, ROOT_D, ALU.mult, ALU.mult)
                ins.then_inc(sem("xhat_ready"), 1)

            turned = [0]

            def wait_turn_hi(key):
                turned[0] += 1
                dve.wait_ge(sem("turn_hi"), turned[0])
                return banks[lease[key][0]]

            def turn(n, c):
                key = ("turn", n, c)
                ps = wait_turn_hi(key)
                up, dst = (mem_t_hi, mem_t_lo) if n == 1 else (u_hi, u_lo)
                if n >= 5:
                    two = slice(2 * c, 2 * c + 2)
                    x = masked[:, c % 2, :].rearrange("p (m n) -> p m n", m=2)
                    link(nc.vector.tensor_copy(up[:, two, :], x))
                    free(tt(dst[:, two, :], x, f32(up[:, two, :]), ALU.subtract), key)
                    return
                for m in range(2):
                    k, x = 2 * c + m, ps[:, m * T:m * T + T]
                    g = ROW_AT[GAIN[n]] + k
                    last = stt(dst[:, k, :], x, cols[:, g:g + 1], f32(up[:, k, :]), ALU.mult, ALU.subtract)
                free(last, key)

            def turn_to(up, dst, key):
                ps = wait_turn_hi(key)
                free(tt(dst, ps[:, :].rearrange("p (m n) -> p m n", m=2), f32(up), ALU.subtract), key)

            def turn_o(c):
                two = slice(2 * (c % 3), 2 * (c % 3) + 2)
                turn_to(u_hi[:, two, :], u_lo[:, two, :], ("turn_o", c))

            def turn_mixed(c):
                part, two = mixed[:, int(c < 2)], slice(2 * (c % 2), 2 * (c % 2) + 2)
                turn_to(part[:, 0, two, :], part[:, 1, two, :], ("turn_mixed", c))

            def columns():
                dve.wait_ge(sem("c_tanh_ready"), 1)
                c = cols[:, ROW_AT["c"]:ROW_AT["c"] + KD]
                link(stt(c_act[:, :], c_tanh[:, :], 1.0, c, ALU.add, ALU.mult))
                link(ts(c_act[:, :], c_act[:, :], 0.5, None, ALU.mult))

            def rope(x, a, b, cos, sin, nsin):
                shape = list(x.shape)
                half = [shape[0], shape[1], shape[3]]
                tt(a, x, cos.unsqueeze(1).unsqueeze(1).broadcast_to(shape), ALU.mult)
                tt(b[:, :, 0, :], x[:, :, 1, :], nsin.unsqueeze(1).broadcast_to(half), ALU.mult)
                link(tt(b[:, :, 1, :], x[:, :, 0, :], sin.unsqueeze(1).broadcast_to(half), ALU.mult))
                return tt(x, a, b, ALU.add)

            def rope1(g):
                c0, heads, last_block = ((QB, 5, 4), (QI, 5, 5), (QC, 5, 7), (KSEL, 2, 8))[g]
                wait_evacuated(dve, ("block", where["proj", last_block]))
                if g == 1:
                    wait_evacuated(dve, ("turn", 0, KD // 2 - 1))
                for t in range(NT):
                    if g == 3:
                        x = proj[:, t, KSEL:KSEL + 4 * HD].rearrange("p (h r) -> p h r", h=2)[:, :, 0:HD]
                    else:
                        x = proj[:, t, c0:c0 + heads * HD].rearrange("p (h c) -> p h c", h=heads)
                    x = x.rearrange("p h (a c) -> p h a c", a=2)
                    a, b = (work[:, at:at + heads * HD].rearrange("p (h a c) -> p h a c", h=heads, a=2)
                            for at in ((1536, 1792) if g == 3 else (0, 512)))
                    cs, sn, ns = (cst(w)[:, 32 * t:32 * t + 32] for w in ("cos1", "sin1", "nsin1"))
                    last = rope(x, a, b, cs, sn, ns)
                    if t == 0:
                        link(last)
                last.then_inc(sem("rope_done"), 1)
                dve.wait_ge(sem("rope_done"), (1, 0, 2, 3)[g] + 1)

            def stick(hd):
                b = hd % 2
                ps = wait_filled(dve, ("stick", hd))
                if hd >= 2:
                    dve.wait_ge(sem("exp_done"), hd - 1)
                z = masked[:, b, 0:3 * P]
                free(stt(z, ps[:, 0:3 * P], SCALE, cst("strict"), ALU.mult, ALU.add), ("stick", hd))
                wait_evacuated(dve, ("stick", hd))
                nc.vector.engine_nop().then_inc(sem("stick_masked"), 1)
                for i in range(2 if b else 0):
                    dve.wait_ge(sem("log_ready"), hd + i)
                    stt(prob_t[:, i, 0:3 * P], masked[:, i, 0:3 * P], 0.0, prob[:, i, 0:3 * P], ALU.max, ALU.add) \
                        .then_inc(sem("softplus_ready"), 1)

            def suffix(hd):
                b = hd % 2
                ps = wait_filled(dve, ("suffix", hd))
                z = masked[:, b, 0:3 * P]
                stt(z, ps[:, 0:3 * P], -1.0, z, ALU.mult, ALU.add).then_inc(sem("stick_summed"), 1)
                dve.wait_ge(sem("stick_summed"), hd + 1)
                free(nc.vector.engine_nop(), ("suffix", hd))

            def index(t):
                n = P * (t + 1)
                if t == 0:
                    link(ts(idx_w[:, :, :], proj[:, :, WI:WI + 4], 1.0 / 16, None, ALU.mult))
                score, x = sel_neg[:, t, 0:n], spare[:, 0:n]
                mask = cst("causal")[:, 2 * P - n:2 * P] if t == 0 else cst("causal")
                for i in range(2):
                    ps = wait_filled(dve, ("index", t, i))
                    for m in range(2):
                        hd = i + 2 * m
                        ins = ts(x, ps[:, m * n:m * n + n], 0.0, idx_w[:, t, hd:hd + 1], ALU.max, ALU.mult)
                        if m:
                            free(ins, ("index", t, i))
                            wait_evacuated(dve, ("index", t, i))
                        else:
                            link(ins)
                        link(tt(score, x, mask if hd == 0 else score, ALU.add))

            def topk(t, part):
                n = P * (t + 1)
                score = sel_neg[:, t, 0:n]
                for _ in range(TOPK // 16):
                    link(nc.vector.max(best[:, :], score))
                    link(nc.vector.match_replace(score, best[:, :], score, TAKEN))
                if part:
                    mask = cst("causal")[:, 2 * P - n:2 * P] if t == 0 else cst("causal")
                    link(ts(score, score, 2 * NEG, NEG, ALU.is_gt, ALU.mult))
                    link(tt(score, score, mask, ALU.add))

            def turn_cmp(i):
                key = ("turn_cmp", i)
                ps = wait_filled(dve, key)
                x = cmp_in[:, i, :].rearrange("p (k n) -> p k n", k=16)
                src = ps[0:HD, 0:T].rearrange("p (n k e) -> p e k n", n=16, k=8)
                for e in range(2):
                    r = slice(HD * e, HD * e + HD)
                    nc.vector.tensor_copy(x[r, 0:8, 0:NC], src[:, e, :, 0:NC])
                    last = nc.vector.tensor_copy(x[r, 8:16, 0:NC], src[:, e, :, 1:NC + 1])
                free(last, key)
                c = ROW_AT["pos_v" if i else "pos_k"]
                nc.vector.tensor_copy(x[:, :, NC], cols[:, c:c + 16]).then_inc(sem("cmp_in_ready"), 1)

            def cmp_hidden(i):
                key = ("cmp_hidden", i)
                ps = wait_filled(dve, key)
                x, y = hid_x[:, i, :], hid_t[:, i, 0:NC]
                free(nc.vector.tensor_copy(x, ps[:, 0:16]), key)
                wait_evacuated(dve, key)
                link(ts(x[:, 0:NC], x[:, 0:NC], x[:, NC:NC + 1], None, ALU.add))
                link(tt(y, x[:, 0:NC], x[:, 0:NC], ALU.mult))
                link(ts(y, y, 0.044715, 1.0, ALU.mult, ALU.add))
                tt(y, y, x[:, 0:NC], ALU.mult).then_inc(sem("cmp_poly_ready"), 1)

            def cmp_kv():
                link(nc.vector.memset(hid_v[:, :, :], 0.0))
                dve.wait_ge(sem("cmp_tanh_ready"), 2)
                link(stt(hid_t[:, :, 0:NC], hid_t[:, :, 0:NC], 1.0, hid_x[:, :, 0:NC], ALU.add, ALU.mult))
                ts(hid_k[:, :], hid_t[:, 0, 0:NC], 0.5, None, ALU.mult)
                ts(hid_v[:, :, 0:NC], hid_t[:, 1, 0:NC].unsqueeze(1).broadcast_to([P, 4, NC]), 0.5, None,
                   ALU.mult).then_inc(sem("cmp_hid_ready"), 1)

            def cmp_scores():
                key = ("cmp_scores",)
                ps = wait_filled(dve, key)
                src = ps[:, 0:8 * 16].rearrange("p (t h n) -> p t h n", t=NT, h=4)
                for t in range(NT):
                    mask = cst("cmpneg")[:, t * NC:t * NC + NC].unsqueeze(1).broadcast_to([P, 4, NC])
                    last = stt(cmp_s[:, t, :, :], src[:, t, :, 0:NC], SCALE, mask, ALU.mult, ALU.add)
                free(last, key)
                wait_evacuated(dve, key)
                s = cmp_s[:, :, :, :].rearrange("p t h n -> p (t h) n")
                link(nc.vector.tensor_reduce(cmp_m[:, :], s, X, ALU.max))
                tt(s, s, over(cmp_m[:, :], NC), ALU.subtract).then_inc(sem("cmp_shifted"), 1)

            def gates_c_():
                dve.wait_ge(sem("gate_c_tanh"), 1)
                g = gate_c[:, :, :, :].rearrange("p t h g -> p (t h g)")
                link(ts(g, g, 0.25, 0.25, ALU.mult, ALU.add))

            def turn_cmp_p():
                p = cmp_in[:, 0, :]
                link(nc.vector.memset(p, 0.0))
                dve.wait_ge(sem("cmp_exp_done"), 1)
                for t in range(NT):
                    mask = cst("cmp01")[:, t * NC:t * NC + NC].unsqueeze(1).broadcast_to([P, 4, NC])
                    dst = p[:, t * P:t * P + P].rearrange("p (h n) -> p h n", h=4)[:, :, 0:NC]
                    last = tt(dst, cmp_s[:, t, :, :], mask, ALU.mult)
                last.then_inc(sem("cmp_p_ready"), 1)
                dve.wait_ge(sem("cmp_p_ready"), 1)
                link(nc.vector.tensor_reduce(cmp_d[:, :], p.rearrange("p (h n) -> p h n", n=32), X, ALU.add))
                link(ts(cmp_d[:, :], cmp_d[:, :], 1e-30, None, ALU.max))
                link(nc.vector.reciprocal(cmp_d[:, :], cmp_d[:, :]))
                link(tt(cmp_d[:, :], cmp_d[:, :], gate_c[:, :, :, 0].rearrange("p t h -> p (t h)"), ALU.mult))

            def scores(u):
                kind, t, _ = UNITS[u]
                n, q = T if kind == "mem" else P * (t + 1), EXP_ORDER[u]
                key = ("scores", u)
                ps = wait_filled(dve, key)
                dve.wait_ge(sem("exp_done"), q - 1)
                dst = masked[:, q % 2, 0:2 * n].rearrange("p (s n) -> p s n", s=2)
                src = ps[:, 0:2 * n].rearrange("p (s n) -> p s n", s=2)
                if kind == "mem":
                    free(ts(dst, src, SCALE, None, ALU.mult), key)
                else:
                    mask = sel_neg[:, t, 0:n] if kind == "b" else cst("causal")[:, 2 * P - n:2 * P]
                    free(stt(dst, src, 1.0 if kind == "fox" else SCALE, mask.unsqueeze(1).broadcast_to([P, 2, n]),
                             ALU.mult, ALU.add), key)
                wait_evacuated(dve, key)
                nc.vector.tensor_reduce(neg_max[:, u, :], dst, X, ALU.max, negate=True) \
                    .then_inc(sem("max_ready"), 1)

            def inverse_den(u0, n):
                d = den[:, u0:u0 + n, :].rearrange("p u s -> p (u s)")
                r = rden[:, u0:u0 + n, :].rearrange("p u s -> p (u s)")
                link(nc.vector.reciprocal(r, d))
                return r

            def o_group(g):
                key = ("o", g)
                if g == 1:
                    ps = wait_filled(dve, key)
                    for t in range(NT):
                        last = tt(o_rows[:, t, 512:768].rearrange("p (h c) -> p h c", h=4),
                                  ps[:, t * 256:t * 256 + 256].rearrange("p (h c) -> p h c", h=4),
                                  over(cmp_d[:, 4 * t:4 * t + 4], HD), ALU.mult)
                    free(last, key)
                    return
                done = {0: 4, 3: 8, 4: 12, 2: 16, 5: 20, 8: 24, 6: 28, 7: 32}[g]
                dve.wait_ge(sem("pv_done"), done)
                if g in (0, 2, 5, 8):
                    ps = banks[O_BANK[g]]
                if g == 0:
                    free(ts(o_rows[:, :, 0:256], ps[:, :].rearrange("p (t c) -> p t c", t=NT), 0.5, None, ALU.mult),
                         key)
                elif g in (3, 4):
                    t = g - 3
                    r = inverse_den(4 + 4 * t, 4)
                    link(tt(rden[:, 4 + 4 * t:8 + 4 * t, :], rden[:, 4 + 4 * t:8 + 4 * t, :],
                            gate_c[:, t, :, 1:3], ALU.mult))
                    x = spare.rearrange("p (m c) -> p m c", c=HD)
                    free(tt(x, banks[O_BANK[g]][:, :].rearrange("p (m c) -> p m c", c=HD), over(r, HD), ALU.mult),
                         key)
                    wait_evacuated(dve, key)
                    x = spare.rearrange("p (h s c) -> p h s c", h=4, s=2)
                    dst = o_rows[:, t, 512:768].rearrange("p (h c) -> p h c", h=4)
                    link(tt(dst, dst, x[:, :, 0, :], ALU.add))
                    tt(dst, dst, x[:, :, 1, :], ALU.add).then_inc(sem("branch_c_done"), 1)
                    dve.wait_ge(sem("branch_c_done"), t + 1)
                elif g in (2, 5):
                    r = inverse_den(0 if g == 2 else 12, 4)
                    if g == 2:
                        link(ts(r, r, 0.5, None, ALU.mult))
                    for t in range(NT):
                        dst = o_rows[:, t, 256:512] if g == 2 else o_mem[:, t, :]
                        last = tt(dst.rearrange("p (m i c) -> p i m c", m=2, i=2),
                                  ps[:, t * 256:t * 256 + 256].rearrange("p (i m c) -> p i m c", i=2, m=2),
                                  over(r[:, 4 * t:4 * t + 4].rearrange("p (i m) -> p i m", i=2), HD), ALU.mult)
                    free(last, key)
                elif g in (6, 7):
                    t = g - 6
                    if t == 0:
                        wait_evacuated(dve, ("gate_row", 0, 1))
                    r = inverse_den(16 + 4 * t, 4)
                    free(tt(norm_rows[:, t, 0:512].rearrange("p (m c) -> p m c", c=HD),
                            banks[O_BANK[g]][:, :].rearrange("p (m c) -> p m c", c=HD), over(r, HD), ALU.mult), key)
                else:
                    for t in range(NT):
                        free(nc.vector.tensor_copy(ret_rows[t], banks[O_BANK[8 + t]][:, :]), ("o", 8 + t))

            def merge(j):
                for c in range(4):
                    key = ("up", j, c)
                    ps = wait_filled(dve, key)
                    g = gates[:, 8 * j + 2 * c:8 * j + 2 * c + 2, :].rearrange("p m n -> p (m n)")
                    dst = work[:, 512 * c:512 * c + 512]
                    x = dst if j == 0 else masked[:, c % 2, :]
                    if j == 0 and c == 0:
                        for i in range(3):
                            wait_evacuated(dve, ("turn_o", i))
                    free(stt(x, g, 1.0, ps[:, :], ALU.add, ALU.mult), key)
                    if j:
                        wait_evacuated(dve, key)
                        ins = tt(dst, dst, x, ALU.add)
                        if j == 2:
                            ins.then_inc(sem("merge_done"), 1)
                            if c:
                                merged_residue(c - 1)
                        else:
                            link(ins)
                    elif c == 3:
                        wait_evacuated(dve, key)
                if j == 2:
                    merged_residue(3)

            def merged_residue(c):
                dve.wait_ge(sem("merged_hi_ready"), c + 1)
                two = slice(2 * c, 2 * c + 2)
                tt(merged_lo[:, two, :].rearrange("p m n -> p (m n)"), work[:, 512 * c:512 * c + 512],
                   f32(merged_hi[:, two, :].rearrange("p m n -> p (m n)")), ALU.subtract) \
                    .then_inc(sem("merged_split"), 1)

            def residual(i):
                group = ("out", "mem_o", "ffn_out", "out2", "mlp_out")[i]
                for t in range(NT):
                    for half in range(2):
                        key = (group, t, half)
                        ps = wait_filled(dve, key)
                        n = slice(512 * half, 512 * half + 512)
                        if i < 3:
                            free(tt(h[:, t, n], h[:, t, n], ps[:, :], ALU.add), key)
                            continue
                        wait_evacuated(dve, ("gate_row", i - 3, half))
                        x = (prob, masked)[t][:, half, :]
                        free(tt(x, row_bc[:, n], ps[:, :], ALU.mult), key)
                        wait_evacuated(dve, key)
                        if t == 0:
                            nc.vector.engine_nop().then_inc(sem("product_gated"), 1)
                        else:
                            tt(h[:, t, n], h[:, t, n], x, ALU.add).then_inc(sem("tile1_gated"), 1)
                    if i == 2:
                        dve.wait_ge(sem("row_loaded"), 16)
                        wait_evacuated(dve, key)
                        tt(norm_rows[:, t, :], h[:, t, :], row_bc[:, :], ALU.mult).then_inc(sem("gain_applied"), 1)

            def final_norm():
                for t in range(NT):
                    last = ts(h[:, t, :], norm_rows[:, t, :], rstd[:, 4, t:t + 1], None, ALU.mult)
                link(last)

            def ada(j):
                x = shaped(raw_ready(dve, ("ada", j)), ("ada", j))
                acc = ada_acc[:, j % 2, :]
                if j >= 2:
                    wait_filled(dve, ("ada_sum", j - 2))
                link(ts(acc, x[:, 0, :], c_act[:, 0:1], None, ALU.mult))
                for k in range(1, KD):
                    ins = stt(acc, x[:, k, :], c_act[:, k:k + 1], acc, ALU.mult, ALU.add)
                    if k < KD - 1:
                        link(ins)
                ins.then_inc(sem("ada_ready"), 1)

            def ada_sum(j):
                key = ("ada_sum", j)
                ps = wait_filled(dve, key)
                c = ROW_AT["b_ada"] + 2 * j
                free(tt(mod[:, 2 * j:2 * j + 2], ps[:, 0:2], cols[:, c:c + 2], ALU.add), key)

            def modulation(i):
                wait_evacuated(dve, ("ada_sum", 7 if i == 0 else 19))
                ts(scale1[:, i, :], mod[:, 24 * i + 8:24 * i + 16], 1.0, None, ALU.add).then_inc(sem("mod_ready"), 1)
                dve.wait_ge(sem("mod_ready"), i + 1)

            def gate_row(i):
                wait_evacuated(dve, ("ada_sum", 12 * i + 11))
                if i == 0:
                    for c in range(8):
                        wait_evacuated(dve, ("turn_fox", c))
                for k in range(KD):
                    g = 16 + 24 * i + k
                    last = ts(work[:, k * P:k * P + P], ident, mod[:, g:g + 1], None, ALU.mult)
                last.then_inc(sem("diag_ready"), 1)

            def squares(x, scratch, dst, n, last=True):
                link(tt(scratch, x, x, ALU.mult))
                ins = nc.vector.tensor_reduce(dst, scratch.rearrange("p (h c) -> p h c", c=n), X, ALU.add)
                if last:
                    ins.then_inc(sem("head_squares"), 1)

            def fox_square(s):
                c = (FQ, FK)[s]
                wait_evacuated(dve, ("block", where["proj2", PROJ2_LAST[c]]))
                for t in range(NT):
                    squares(proj2[:, t, c:c + 512], masked[:, t, :], fstat[:, s, FH * t:FH * t + FH], HD, t == 1)
                dve.wait_ge(sem("head_squares"), s + 1)

            def fox_norm(s):
                dve.wait_ge(sem("head_rstd"), s + 1)
                dve.wait_ge(sem("gains_loaded"), 16 * 5)
                root = HD ** 0.5
                if s == 0:
                    ts(gain_q, gain_q, SCALE * root, None, ALU.mult)
                    link(ts(gain_k, gain_k, root, None, ALU.mult))
                gain = (gain_q, gain_k)[s].unsqueeze(1).broadcast_to([P, FH, HD])
                for t in range(NT):
                    x = proj2[:, t, (FQ, FK)[s]:(FQ, FK)[s] + 512].rearrange("p (h c) -> p h c", c=HD)
                    dst = aug[:, t, s, :, 0:HD]
                    link(tt(dst, x, over(fstat[:, s, FH * t:FH * t + FH], HD), ALU.mult))
                    last = tt(dst, dst, gain, ALU.mult)
                last.then_inc(sem("aug_ready"), 1)

            def forget():
                wait_evacuated(dve, ("block", where["proj2", 8]))
                dve.wait_ge(sem("gains_loaded"), 16 * 5)
                tt(logit[:, :, :], proj2[:, :, FF:FF + FH], b_forget.unsqueeze(1).broadcast_to([P, NT, FH]),
                   ALU.add).then_inc(sem("logit_ready"), 1)
                dve.wait_ge(sem("logit_ready"), 1)

            def forget_sum():
                dve.wait_ge(sem("soft_ready"), 1)
                stt(soft[:, :, :], logit[:, :, :], 0.0, soft[:, :, :], ALU.min, ALU.subtract) \
                    .then_inc(sem("log_f_ready"), 1)
                nc.vector.memset(aug[:, :, 0, :, HD], 1.0)
                nc.vector.memset(aug[:, :, 1, :, HD + 1], 1.0)
                key = ("forget_sum",)
                ps = wait_filled(dve, key)
                x = ps[:, 0:NT * FH].rearrange("p (t h) -> p t h", t=NT)
                nc.vector.tensor_copy(aug[:, :, 0, :, HD + 1], x)
                free(ts(aug[:, :, 1, :, HD], x, -1.0, None, ALU.mult), key)
                wait_evacuated(dve, key)
                nc.vector.engine_nop().then_inc(sem("aug_ready"), 1)

            def rope2(s):
                wait_evacuated(dve, ("block", where["proj2", PROJ2_LAST[(RQ, RK)[s]]]))
                for t in range(NT):
                    x = proj2[:, t, (RQ, RK)[s]:(RQ, RK)[s] + 512].rearrange("p (h a c) -> p h a c", h=RH, a=2)
                    a, b = (masked[:, i, :].rearrange("p (h a c) -> p h a c", h=RH, a=2) for i in range(2))
                    cs, sn, ns = (cst(w)[:, 64 * t:64 * t + 64] for w in ("cos2", "sin2", "nsin2"))
                    last = rope(x, a, b, cs, sn, ns)
                    if t == 0:
                        link(last)
                last.then_inc(sem("rope2_done"), 1)
                dve.wait_ge(sem("rope2_done"), s + 1)

            def ret_scores(hd):
                key = ("ret_scores", hd)
                ps = wait_filled(dve, key)
                dve.wait_ge(sem("pv_done"), PV_RET + hd - 1)
                dve.wait_ge(sem("decays_loaded"), 16)
                decay = decays[:, hd * 2 * P:(hd + 1) * 2 * P]
                p = prob[:, hd % 2, :]
                tt(p[:, 0:T], ps[:, 0:T], decay, ALU.mult)
                free(tt(p[:, T:T + P], ps[:, T:T + P], decay[:, 0:P], ALU.mult), key)

            def mix(part, t):
                if part == 0:
                    for i in range(NT):
                        wait_evacuated(dve, ("o", 8 + i))
                        squares(ret_rows[i], proj2[:, i, FQ:FQ + 512], fstat[:, 2, RH * i:RH * i + RH], RD, i == 1)
                else:
                    wait_evacuated(dve, ("o", 6 + t))
                    squares(fox_rows[t], proj2[:, t, FK:FK + 512], fstat[:, 3 + t, 0:FH], HD)

            def mix2(part, t):
                i = 2 + part + t
                n = HD if part else RD
                dve.wait_ge(sem("head_rstd"), i + 1)
                dve.wait_ge(sem("mix_tanh"), 1 + part)
                for tile in (t,) if part else range(NT):
                    x = fox_rows[tile] if part else ret_rows[tile]
                    r = fstat[:, i, 0:FH] if part else fstat[:, i, RH * tile:RH * tile + RH]
                    heads_x = x.rearrange("p (h c) -> p h c", c=n)
                    link(tt(heads_x, heads_x, over(r, n), ALU.mult))
                    gain = out_gain[:, 0:512] if part else out_gain[:, 512:1024]
                    link(stt(x, x, 0.5 * float(np.sqrt(n)), gain, ALU.mult, ALU.mult))
                    if part:
                        last = stt(x, proj2[:, tile, FOG:FOG + 512], 1.0, x, ALU.add, ALU.mult)
                    else:
                        th = proj2[:, tile, RQ:RQ + 512]
                        link(stt(th, th, 1.0, proj2[:, tile, RG:RG + 512], ALU.add, ALU.mult))
                        last = tt(x, x, th, ALU.mult)
                last.then_inc(sem("mix_done"), 1)

            run({"residue": residue, "evac": evac, "xhat": xhat, "turn": turn, "turn_o": turn_o,
                 "turn_mixed": turn_mixed, "columns": columns, "rope1": rope1, "stick": stick, "suffix": suffix,
                 "index": index, "topk": topk, "turn_cmp": turn_cmp, "cmp_hidden": cmp_hidden, "cmp_kv": cmp_kv,
                 "cmp_scores": cmp_scores, "gates_c": gates_c_, "turn_cmp_p": turn_cmp_p, "scores": scores,
                 "o_group": o_group, "merge": merge, "residual": residual,
                 "final_norm": final_norm, "ada": ada, "ada_sum": ada_sum, "mod": modulation, "gate_row": gate_row,
                 "fox_square": fox_square, "fox_norm": fox_norm, "forget": forget, "forget_sum": forget_sum,
                 "rope2": rope2, "ret_scores": ret_scores, "mix": mix, "mix2": mix2})

        @block.sync
        def _(sp):
            def load(dst, src, signal):
                sp.dma_start(dst, src).then_inc(sem(signal) if isinstance(signal, str) else signal, 16)

            for t in range(NT):
                load(h[:, t, :], d["x"][0, t * P:t * P + P, :], f"x{t}_loaded")
            load(const[:, 0:P], consts_dram[:, 0:P], "ident_loaded")
            for i, what in enumerate(raw_order):
                if i >= RAW:
                    before = raw_order[i - RAW]
                    if before[0] == "split":
                        sp.wait_ge(sem("lo_ready"), before[1] + 1)
                    elif before[0] == "ada":
                        sp.wait_ge(sem("ada_ready"), before[1] + 1)
                    else:
                        wait_filled(sp, ("cmp_hidden", before[1]))
                b = blocks[what[1]] if what[0] == "split" else what
                n = KD * width(what[1]) if what[0] == "split" else BLOCK
                load(raw[:, i % RAW, 0:n], stream[i, :, 0:n], raw_loaded[i % RAW])
                if i == 0:
                    row_source = dict(
                        norm_mix=d["norm_mix"], norm_mem_kv=d["norm_mem_kv"], norm_mem_q=d["norm_mem_q"],
                        norm_ffn=d["norm_ffn"], c=d["c_2"], b_ada=d["b_ada_2"])
                    for name, at in ROW_AT.items():
                        if name in row_source:
                            src = row_source[name].rearrange("l (k p) -> (l k) p", p=P)
                        else:
                            src = d["cmp_" + name][0].rearrange("(k e) c -> k (e c)", e=2)
                        load(rows[at:at + src.shape[0], :], src, "rows_loaded")
                if i == 1:
                    load(const[:, P:DECAY_AT], consts_dram[:, P:DECAY_AT], "const_loaded")
                if b == ("out", 3):
                    sp.wait_ge(sem("merge_done"), 4)
                    load(mem_rows[:, :, :], d["mem"][0].rearrange("(t p) c -> p t c", p=P), "mem_loaded")
                if i == 5:
                    for m in range(2):
                        load(w2k[:, m, :], d["cmp_w2_k"][0], "w2_loaded")
                    load(w2v[:, :], d["cmp_w2_v"][0], "w2_loaded")
                    wait_evacuated(sp, ("columns",))
                    load(row_bc[:, :], d["norm_final"].rearrange("(a c) -> a c", a=1)[0].partition_broadcast(P),
                         "row_loaded")
                if b == ("ffn_in", 3):
                    sp.wait_ge(sem("hidden_ready"), 1)
                    for dst, src in ((gain_q, d["q_norm_gain_2"][0]), (gain_k, d["k_norm_gain_2"][0]),
                                     (b_forget, d["b_forget_2"][0]),
                                     (out_gain[:, 0:512], d["fox_out_gain_2"][0].rearrange("h c -> (h c)")),
                                     (out_gain[:, 512:1024], d["ret_out_gain_2"][0].rearrange("h c -> (h c)"))):
                        load(dst, src.partition_broadcast(P), "gains_loaded")
                    load(decays[:, :], consts_dram[:, DECAY_AT:CONSTS], "decays_loaded")
            for t in range(NT):
                sp.wait_ge(sem(("tile0_gated", "tile1_gated")[t]), 4)
                load(out_dram[0, t * P:t * P + P, :], h[:, t, :], "stored")
            sp.wait_ge(sem("stored"), 16 * NT)


def kernel(**inputs):
    import concourse.bacc as bacc
    from concourse.bass_utils import run_bass_kernel_spmd

    nc = bacc.Bacc("TRN2", target_bir_lowering=False, num_devices=1)
    arrays, d = {}, {}
    for name in SMALL:
        a = np.ascontiguousarray(inputs[name])
        arrays[f"in_{name}"] = a
        d[name] = nc.dram_tensor(f"in_{name}", a.shape, mybir.dt.from_np(a.dtype), kind="ExternalInput").ap()
    arrays["in_stream"] = weight_stream(inputs)
    stream = nc.dram_tensor("in_stream", arrays["in_stream"].shape, F32, kind="ExternalInput").ap()
    arrays["in_constants"] = constants()
    consts_dram = nc.dram_tensor("in_constants", (P, CONSTS), F32, kind="ExternalInput").ap()
    out = nc.dram_tensor("out", (1, T, D), F32, kind="ExternalOutput").ap()
    two_blocks_kernel(nc, d, stream, consts_dram, out)
    r = run_bass_kernel_spmd(nc, [arrays], core_ids=[0])
    return r.results[0]["out"]
```
